# Optimizing a Trainium2 kernel written in Bass

```python
import math
import jax, jax.numpy as jnp
from jax import lax
import numpy as np

D_MODEL = 1024
BATCH = 1
SEQ = 256
DEPTH = 2

HEAD_DIM = 64
Q_BLOCK = 128
NSA_HEADS = 8
NSA_KV_HEADS = 2
CMP_LEN = 32
CMP_STRIDE = 16
CMP_HIDDEN = 256
SLC_LEN = 64
SLC_TOPN = 16
NSA_WINDOW = 512
FORCE_SCORE = 1e4
SB_HEADS = 4
SWA_HEADS = 4
SWA_KV_HEADS = 2
SWA_WINDOW = 128
NUM_BUCKETS = 32
MAX_DISTANCE = 128
N_BIAS_HEADS = NSA_HEADS + SWA_HEADS
D_FF = 2816
NORM_EPS = 1e-6
NEG_INF = -1e30
N_BRANCHES = 3

SPLIT_SIZES = (
    NSA_HEADS * HEAD_DIM,
    NSA_KV_HEADS * HEAD_DIM, NSA_KV_HEADS * HEAD_DIM,
    NSA_KV_HEADS * HEAD_DIM, NSA_KV_HEADS * HEAD_DIM,
    NSA_KV_HEADS * HEAD_DIM, NSA_KV_HEADS * HEAD_DIM,
    3 * NSA_HEADS,
    SB_HEADS * HEAD_DIM, SB_HEADS * HEAD_DIM, SB_HEADS * HEAD_DIM,
    SWA_HEADS * HEAD_DIM, SWA_KV_HEADS * HEAD_DIM, SWA_KV_HEADS * HEAD_DIM,
    N_BRANCHES * D_MODEL,
)
D_IN = sum(SPLIT_SIZES)
SPLIT_POINTS = tuple(int(p) for p in np.cumsum(SPLIT_SIZES)[:-1])


def rms_norm(x, w):
    xf = x.astype(jnp.float32)
    y = xf * lax.rsqrt(jnp.mean(xf * xf, axis=-1, keepdims=True) + NORM_EPS)
    return (y * w.astype(jnp.float32)).astype(x.dtype)

def swiglu(x, w_gate, w_up, w_down):
    return (jax.nn.silu(x @ w_gate) * (x @ w_up)) @ w_down

def t5_bucket(dist):
    max_exact = NUM_BUCKETS // 2
    d = jnp.maximum(dist, 0)
    df = jnp.maximum(d, 1).astype(jnp.float32)
    large = max_exact + (jnp.log(df / max_exact) / math.log(MAX_DISTANCE / max_exact)
                         * (NUM_BUCKETS - max_exact)).astype(jnp.int32)
    large = jnp.minimum(large, NUM_BUCKETS - 1)
    return jnp.where(d < max_exact, d, large)

def masked_softmax(logits, mask):
    p = jax.nn.softmax(jnp.where(mask, logits, NEG_INF), axis=-1)
    return p * mask

def nsa_attention(q, k_cmp, v_cmp, k_slc, v_slc, k_win, v_win, gate_logits,
                  q_norm, k_norm, cmp_pos, cmp_k_w1, cmp_k_w2, cmp_v_w1, cmp_v_w2, bias_table):
    B, S = q.shape[0], q.shape[1]
    G, R, Dh = NSA_KV_HEADS, NSA_HEADS // NSA_KV_HEADS, HEAD_DIM
    scale = Dh ** -0.5
    qg = rms_norm(q, q_norm).reshape(B, S, G, R, Dh).transpose(0, 2, 3, 1, 4)
    gates = jax.nn.sigmoid(gate_logits.astype(jnp.float32)).reshape(B, S, 3, G, R)

    n_cmp = (S - CMP_LEN) // CMP_STRIDE + 1
    cmp_idx = np.arange(n_cmp)[:, None] * CMP_STRIDE + np.arange(CMP_LEN)[None, :]
    cmp_end = jnp.asarray(cmp_idx[:, -1], jnp.int32)

    def compress(t, w1, w2):
        blocks = t[:, cmp_idx] + cmp_pos[:, None, :]
        blocks = blocks.transpose(0, 3, 1, 2, 4).reshape(B, G, n_cmp, CMP_LEN * Dh)
        return jax.nn.silu(blocks @ w1) @ w2

    kc = rms_norm(compress(k_cmp, cmp_k_w1, cmp_k_w2), k_norm)
    vc = compress(v_cmp, cmp_v_w1, cmp_v_w2)

    n_slc = S // SLC_LEN
    slc_start = np.arange(n_slc) * SLC_LEN
    overlap = jnp.asarray((cmp_idx[:, :1] < slc_start[None, :] + SLC_LEN)
                          & (cmp_idx[:, -1:] >= slc_start[None, :]), jnp.float32)
    top_n = min(SLC_TOPN, n_slc)
    ks = rms_norm(k_slc, k_norm).transpose(0, 2, 1, 3).reshape(B, G, n_slc, SLC_LEN, Dh)
    vs = v_slc.transpose(0, 2, 1, 3).reshape(B, G, n_slc, SLC_LEN, Dh)

    pad = ((0, 0), (0, 0), (NSA_WINDOW, 0), (0, 0))
    kw = jnp.pad(rms_norm(k_win, k_norm).transpose(0, 2, 1, 3), pad)
    vw = jnp.pad(v_win.transpose(0, 2, 1, 3), pad)

    head_bias = bias_table[:, :NSA_HEADS].T.reshape(G, R, NUM_BUCKETS).astype(jnp.float32)
    b_idx = jnp.arange(B)[:, None, None, None]
    g_idx = jnp.arange(G)[None, :, None, None]
    g5 = jnp.arange(G)[None, :, None, None, None]
    r5 = jnp.arange(R)[None, None, :, None, None]
    slc_ids = jnp.arange(n_slc)[None, :]

    def block(i):
        q0 = i * Q_BLOCK
        t = q0 + jnp.arange(Q_BLOCK)
        qb = lax.dynamic_slice_in_dim(qg, q0, Q_BLOCK, axis=3)

        dist_c = t[:, None] - cmp_end[None, :]
        s_c = (jnp.einsum('bgrqd,bgnd->bgrqn', qb, kc).astype(jnp.float32) * scale
               + head_bias[:, :, t5_bucket(dist_c)])
        p_c = masked_softmax(s_c, dist_c >= 0)
        o_c = jnp.einsum('bgrqn,bgnd->bgrqd', p_c.astype(vc.dtype), vc)

        imp = jnp.einsum('bgrqn,nj->bgqj', p_c, overlap)
        cur = (t // SLC_LEN)[:, None]
        forced = (slc_ids == 0) | (slc_ids == cur) | (slc_ids == cur - 1)
        score = jnp.where(forced, FORCE_SCORE, jnp.where(slc_ids <= cur, imp, -1.0))
        _, sel = lax.top_k(score, top_n)
        kg = ks[b_idx, g_idx, sel].reshape(B, G, Q_BLOCK, top_n * SLC_LEN, Dh)
        vg = vs[b_idx, g_idx, sel].reshape(B, G, Q_BLOCK, top_n * SLC_LEN, Dh)
        pos = (sel[..., None] * SLC_LEN + jnp.arange(SLC_LEN)).reshape(B, G, Q_BLOCK, top_n * SLC_LEN)
        dist_s = t[None, None, :, None] - pos
        s_s = (jnp.einsum('bgrqd,bgqkd->bgrqk', qb, kg).astype(jnp.float32) * scale
               + head_bias[g5, r5, t5_bucket(dist_s)[:, :, None]])
        p_s = masked_softmax(s_s, (dist_s >= 0)[:, :, None])
        o_s = jnp.einsum('bgrqk,bgqkd->bgrqd', p_s.astype(vg.dtype), vg)

        kb = lax.dynamic_slice_in_dim(kw, q0, Q_BLOCK + NSA_WINDOW, axis=2)
        vb = lax.dynamic_slice_in_dim(vw, q0, Q_BLOCK + NSA_WINDOW, axis=2)
        key_pos = q0 - NSA_WINDOW + jnp.arange(Q_BLOCK + NSA_WINDOW)
        dist_w = t[:, None] - key_pos[None, :]
        mask_w = (dist_w >= 0) & (dist_w < NSA_WINDOW) & (key_pos[None, :] >= 0)
        s_w = (jnp.einsum('bgrqd,bgkd->bgrqk', qb, kb).astype(jnp.float32) * scale
               + head_bias[:, :, t5_bucket(dist_w)])
        p_w = masked_softmax(s_w, mask_w)
        o_w = jnp.einsum('bgrqk,bgkd->bgrqd', p_w.astype(vb.dtype), vb)

        g = lax.dynamic_slice_in_dim(gates, q0, Q_BLOCK, axis=1).transpose(2, 0, 3, 4, 1)[..., None]
        return (g[0] * o_c + g[1] * o_s + g[2] * o_w).astype(q.dtype)

    o = lax.map(block, jnp.arange(S // Q_BLOCK))
    return o.transpose(1, 0, 4, 2, 3, 5).reshape(B, S, NSA_HEADS * Dh)

def stick_breaking_attention(q, k, v):
    B, S = q.shape[0], q.shape[1]
    scale = HEAD_DIM ** -0.5
    qh = q.transpose(0, 2, 1, 3)
    kh = k.transpose(0, 2, 1, 3)
    vh = v.transpose(0, 2, 1, 3)
    key_pos = jnp.arange(S)

    def block(i):
        q0 = i * Q_BLOCK
        t = q0 + jnp.arange(Q_BLOCK)
        qb = lax.dynamic_slice_in_dim(qh, q0, Q_BLOCK, axis=2)
        z = jnp.einsum('bhqd,bhkd->bhqk', qb, kh).astype(jnp.float32) * scale
        mask = key_pos[None, :] < t[:, None]
        log_fail = jnp.where(mask, jax.nn.log_sigmoid(-z), 0.0)
        after = lax.cumsum(log_fail, axis=3, reverse=True) - log_fail
        w = jnp.where(mask, jnp.exp(jax.nn.log_sigmoid(z) + after), 0.0)
        return jnp.einsum('bhqk,bhkd->bhqd', w.astype(vh.dtype), vh)

    o = lax.map(block, jnp.arange(S // Q_BLOCK))
    return o.transpose(1, 0, 3, 2, 4).reshape(B, S, SB_HEADS * HEAD_DIM)

def swa_sink_attention(q, k, v, q_norm, k_norm, sinks, bias_table):
    B, S = q.shape[0], q.shape[1]
    G, R, Dh = SWA_KV_HEADS, SWA_HEADS // SWA_KV_HEADS, HEAD_DIM
    scale = Dh ** -0.5
    qg = rms_norm(q, q_norm).reshape(B, S, G, R, Dh).transpose(0, 2, 3, 1, 4)
    pad = ((0, 0), (0, 0), (SWA_WINDOW, 0), (0, 0))
    kp = jnp.pad(rms_norm(k, k_norm).transpose(0, 2, 1, 3), pad)
    vp = jnp.pad(v.transpose(0, 2, 1, 3), pad)
    head_bias = bias_table[:, NSA_HEADS:].T.reshape(G, R, NUM_BUCKETS).astype(jnp.float32)
    sink = sinks.astype(jnp.float32).reshape(1, G, R, 1, 1)

    def block(i):
        q0 = i * Q_BLOCK
        t = q0 + jnp.arange(Q_BLOCK)
        qb = lax.dynamic_slice_in_dim(qg, q0, Q_BLOCK, axis=3)
        kb = lax.dynamic_slice_in_dim(kp, q0, Q_BLOCK + SWA_WINDOW, axis=2)
        vb = lax.dynamic_slice_in_dim(vp, q0, Q_BLOCK + SWA_WINDOW, axis=2)
        key_pos = q0 - SWA_WINDOW + jnp.arange(Q_BLOCK + SWA_WINDOW)
        dist = t[:, None] - key_pos[None, :]
        mask = (dist >= 0) & (dist < SWA_WINDOW) & (key_pos[None, :] >= 0)
        s = (jnp.einsum('bgrqd,bgkd->bgrqk', qb, kb).astype(jnp.float32) * scale
             + head_bias[:, :, t5_bucket(dist)])
        s = jnp.where(mask, s, NEG_INF)
        m = jnp.maximum(jnp.max(s, axis=-1, keepdims=True), sink)
        e = jnp.exp(s - m)
        p = e / (jnp.sum(e, axis=-1, keepdims=True) + jnp.exp(sink - m))
        return jnp.einsum('bgrqk,bgkd->bgrqd', p.astype(vb.dtype), vb)

    o = lax.map(block, jnp.arange(S // Q_BLOCK))
    return o.transpose(1, 0, 4, 2, 3, 5).reshape(B, S, SWA_HEADS * Dh)

def first_inputs(seed: int = 0) -> dict:
    key = jax.random.key(seed)
    ks = jax.random.split(key, 32)
    L, D, F = DEPTH, D_MODEL, D_FF

    def w(k, shape, fan_in):
        return jax.random.normal(k, shape, jnp.float32) * fan_in ** -0.5

    def gain(k, shape):
        return 1.0 + 0.02 * jax.random.normal(k, shape, jnp.float32)

    return {
        "x": jax.random.normal(ks[0], (BATCH, SEQ, D), jnp.float32),
        "rel_bias": 0.5 * jax.random.normal(ks[1], (NUM_BUCKETS, N_BIAS_HEADS), jnp.float32),
        "ffn1_norm": gain(ks[2], (L, D)),
        "ffn1_w_gate": w(ks[3], (L, D, F), D),
        "ffn1_w_up": w(ks[4], (L, D, F), D),
        "ffn1_w_down": w(ks[5], (L, F, D), F),
        "mix_norm": gain(ks[6], (L, D)),
        "w_in": w(ks[7], (L, D, D_IN), D),
        "nsa_q_norm": gain(ks[8], (L, HEAD_DIM)),
        "nsa_k_norm": gain(ks[9], (L, HEAD_DIM)),
        "nsa_cmp_pos": 0.5 * jax.random.normal(ks[10], (L, CMP_LEN, HEAD_DIM), jnp.float32),
        "nsa_cmp_k_w1": w(ks[11], (L, CMP_LEN * HEAD_DIM, CMP_HIDDEN), CMP_LEN * HEAD_DIM),
        "nsa_cmp_k_w2": w(ks[12], (L, CMP_HIDDEN, HEAD_DIM), CMP_HIDDEN),
        "nsa_cmp_v_w1": w(ks[13], (L, CMP_LEN * HEAD_DIM, CMP_HIDDEN), CMP_LEN * HEAD_DIM),
        "nsa_cmp_v_w2": w(ks[14], (L, CMP_HIDDEN, HEAD_DIM), CMP_HIDDEN),
        "swa_q_norm": gain(ks[15], (L, HEAD_DIM)),
        "swa_k_norm": gain(ks[16], (L, HEAD_DIM)),
        "swa_sinks": jax.random.normal(ks[17], (L, SWA_HEADS), jnp.float32),
        "w_up_nsa": w(ks[18], (L, NSA_HEADS * HEAD_DIM, D), NSA_HEADS * HEAD_DIM),
        "w_up_sb": w(ks[19], (L, SB_HEADS * HEAD_DIM, D), SB_HEADS * HEAD_DIM),
        "w_up_swa": w(ks[20], (L, SWA_HEADS * HEAD_DIM, D), SWA_HEADS * HEAD_DIM),
        "w_out": w(ks[21], (L, D, D), D),
        "ffn2_norm": gain(ks[22], (L, D)),
        "ffn2_w_gate": w(ks[23], (L, D, F), D),
        "ffn2_w_up": w(ks[24], (L, D, F), D),
        "ffn2_w_down": w(ks[25], (L, F, D), F),
    }

def first_block(x, rel_bias, ffn1_norm, ffn1_w_gate, ffn1_w_up, ffn1_w_down, mix_norm, w_in,
              nsa_q_norm, nsa_k_norm, nsa_cmp_pos, nsa_cmp_k_w1, nsa_cmp_k_w2, nsa_cmp_v_w1,
              nsa_cmp_v_w2, swa_q_norm, swa_k_norm, swa_sinks, w_up_nsa, w_up_sb, w_up_swa, w_out,
              ffn2_norm, ffn2_w_gate, ffn2_w_up, ffn2_w_down):
    B, S = x.shape[0], x.shape[1]

    def heads(t, n):
        return t.reshape(B, S, n, HEAD_DIM)

    for l in range(DEPTH):
        h = rms_norm(x, ffn1_norm[l])
        x = x + 0.5 * swiglu(h, ffn1_w_gate[l], ffn1_w_up[l], ffn1_w_down[l])

        h = rms_norm(x, mix_norm[l])
        (nq, nkc, nvc, nks, nvs, nkw, nvw, ngate, sq, sk, sv, wq, wk, wv, bgate) = jnp.split(
            h @ w_in[l], SPLIT_POINTS, axis=-1)
        y_nsa = nsa_attention(heads(nq, NSA_HEADS), heads(nkc, NSA_KV_HEADS), heads(nvc, NSA_KV_HEADS),
                              heads(nks, NSA_KV_HEADS), heads(nvs, NSA_KV_HEADS),
                              heads(nkw, NSA_KV_HEADS), heads(nvw, NSA_KV_HEADS), ngate,
                              nsa_q_norm[l], nsa_k_norm[l], nsa_cmp_pos[l], nsa_cmp_k_w1[l],
                              nsa_cmp_k_w2[l], nsa_cmp_v_w1[l], nsa_cmp_v_w2[l], rel_bias)
        y_sb = stick_breaking_attention(heads(sq, SB_HEADS), heads(sk, SB_HEADS), heads(sv, SB_HEADS))
        y_swa = swa_sink_attention(heads(wq, SWA_HEADS), heads(wk, SWA_KV_HEADS), heads(wv, SWA_KV_HEADS),
                                   swa_q_norm[l], swa_k_norm[l], swa_sinks[l], rel_bias)

        g = jax.nn.sigmoid(bgate.astype(jnp.float32)).reshape(B, S, N_BRANCHES, D_MODEL).astype(x.dtype)
        merged = (g[:, :, 0] * (y_nsa @ w_up_nsa[l]) + g[:, :, 1] * (y_sb @ w_up_sb[l])
                  + g[:, :, 2] * (y_swa @ w_up_swa[l]))
        x = x + merged @ w_out[l]

        h = rms_norm(x, ffn2_norm[l])
        x = x + 0.5 * swiglu(h, ffn2_w_gate[l], ffn2_w_up[l], ffn2_w_down[l])
    return x


CHUNK = 64
N_MEM = 256
D_MIX = D_MODEL
D_GLA = D_MIX // 2
D_SGU = D_MIX - D_GLA
GLA_HEADS = 4
D_QK = D_GLA // 2
GLA_DK = D_QK // GLA_HEADS
GLA_DV = D_GLA // GLA_HEADS
GATE_RANK = 16
GATE_TEMP = 16.0
SGU_GROUPS = 4
SGU_BLOCK = 128
SGU_CH = D_SGU // SGU_GROUPS
XATTN_HEADS = 4
XATTN_DH = D_MODEL // XATTN_HEADS
N_EXPERTS = 16
N_EXPERT_GROUPS = 4
EXPERTS_PER_GROUP = N_EXPERTS // N_EXPERT_GROUPS
TOP_K = 2
D_EXPERT = D_MODEL // 2
DN_ALPHA = (2.0 * DEPTH) ** 0.25
DN_BETA = (8.0 * DEPTH) ** -0.25
LN_EPS = 1e-5
RMS_EPS = 1e-6
D_IN_2 = 2 * D_QK + 2 * D_GLA + GATE_RANK + 2 * D_SGU


def layer_norm(x, g, b):
    xf = x.astype(jnp.float32)
    mu = jnp.mean(xf, axis=-1, keepdims=True)
    var = jnp.mean(jnp.square(xf - mu), axis=-1, keepdims=True)
    y = (xf - mu) * lax.rsqrt(var + LN_EPS)
    return (y * g.astype(jnp.float32) + b.astype(jnp.float32)).astype(x.dtype)

def split_proj(p):
    sizes = (D_QK, D_QK, D_GLA, D_GLA, GATE_RANK, D_SGU, D_SGU)
    outs, start = [], 0
    for s in sizes:
        outs.append(p[..., start:start + s])
        start += s
    return outs

def gla_group(q, k, v, r, a_low, w_a2, b_a, gn_g):
    B, S, _ = q.shape
    nc = S // CHUNK
    log_a = jax.nn.log_sigmoid((a_low @ w_a2 + b_a).astype(jnp.float32)) / GATE_TEMP

    def to_chunks(t, d):
        return t.astype(jnp.float32).reshape(B, nc, CHUNK, GLA_HEADS, d).transpose(1, 0, 3, 2, 4)

    qc = to_chunks(q, GLA_DK) * (GLA_DK ** -0.5)
    kc = to_chunks(k, GLA_DK)
    vc = to_chunks(v, GLA_DV)
    gc = to_chunks(log_a, GLA_DK)

    def step(state, inp):
        q_c, k_c, v_c, g_c = inp
        bcum = jnp.cumsum(g_c, axis=2)
        b_last = bcum[:, :, -1:, :]
        k_dec = k_c * jnp.exp(b_last - bcum)
        state = jnp.exp(b_last[:, :, 0, :])[..., None] * state + jnp.einsum('bhck,bhcv->bhkv', k_dec, v_c)
        o = jnp.einsum('bhck,bhkv->bhcv', q_c, state)
        return state, o

    s0 = jnp.zeros((B, GLA_HEADS, GLA_DK, GLA_DV), jnp.float32)
    _, o = lax.scan(step, s0, (qc, kc, vc, gc))
    o = o.transpose(1, 0, 3, 2, 4).reshape(B, S, GLA_HEADS, GLA_DV)
    o = o * lax.rsqrt(jnp.mean(jnp.square(o), axis=-1, keepdims=True) + RMS_EPS)
    o = o.reshape(B, S, D_GLA) * gn_g.astype(jnp.float32)
    out = o * jax.nn.silu(r.astype(jnp.float32))
    return out.astype(q.dtype)

def sgu_group(u, v, w_s, b_s, ln_g, ln_b):
    B, S, _ = u.shape
    nb = S // SGU_BLOCK
    u = jax.nn.gelu(u)
    v = jax.nn.gelu(v).reshape(B, S, SGU_GROUPS, SGU_CH)
    v = layer_norm(v, ln_g.reshape(SGU_GROUPS, SGU_CH), ln_b.reshape(SGU_GROUPS, SGU_CH))
    v = v.reshape(B, nb, SGU_BLOCK, SGU_GROUPS, SGU_CH)
    pos = jnp.arange(SGU_BLOCK)
    mask = (pos[None, :] // CHUNK) <= (pos[:, None] // CHUNK)
    w_m = jnp.where(mask[None], w_s, jnp.zeros_like(w_s))
    mixed = jnp.einsum('gts,bnsgc->bntgc', w_m, v) + b_s.T[None, None, :, :, None]
    out = u.reshape(B, nb, SGU_BLOCK, SGU_GROUPS, SGU_CH) * mixed
    return out.reshape(B, S, D_SGU)

def mem_xattn(x, mem, wq, wk, wv, wo):
    B, S, _ = x.shape
    M = mem.shape[1]
    q = (x @ wq).reshape(B, S, XATTN_HEADS, XATTN_DH)
    k = (mem @ wk).reshape(B, M, XATTN_HEADS, XATTN_DH)
    v = (mem @ wv).reshape(B, M, XATTN_HEADS, XATTN_DH)
    s = jnp.einsum('bshd,bmhd->bhsm', q, k).astype(jnp.float32) * (XATTN_DH ** -0.5)
    p = jax.nn.softmax(s, axis=-1).astype(v.dtype)
    o = jnp.einsum('bhsm,bmhd->bshd', p, v).reshape(B, S, D_MODEL)
    return o @ wo

def grouped_moe(x, w_router, b_router, w_gate, w_up, w_down):
    B, S, D = x.shape
    xt = x.reshape(B * S, D)
    scores = jax.nn.softmax((xt @ w_router + b_router).astype(jnp.float32), axis=-1)
    grp = scores.reshape(-1, N_EXPERT_GROUPS, EXPERTS_PER_GROUP)
    group_score = jnp.sum(lax.top_k(grp, TOP_K)[0], axis=-1)
    g_sel = jnp.argmax(group_score, axis=-1)
    in_grp = jnp.sum(grp * jax.nn.one_hot(g_sel, N_EXPERT_GROUPS, dtype=jnp.float32)[:, :, None], axis=1)
    top_w, top_i = lax.top_k(in_grp, TOP_K)
    top_w = top_w / jnp.sum(top_w, axis=-1, keepdims=True)
    eid = g_sel[:, None] * EXPERTS_PER_GROUP + top_i
    gate = jnp.sum(jax.nn.one_hot(eid, N_EXPERTS, dtype=jnp.float32) * top_w[..., None], axis=1)
    gate = gate.astype(x.dtype)
    y = jnp.zeros_like(xt)
    for e in range(N_EXPERTS):
        h = jax.nn.silu(xt @ w_gate[e]) * (xt @ w_up[e])
        y = y + gate[:, e:e + 1] * (h @ w_down[e])
    return y.reshape(B, S, D)

def second_inputs(seed: int = 0) -> dict:
    key = jax.random.key(seed)
    ks = jax.random.split(key, 24)
    f32 = jnp.float32

    def nrm(k, shape, fan_in, scale=1.0):
        return jax.random.normal(k, shape, f32) * (scale * fan_in ** -0.5)

    def gain(k, shape):
        return 1.0 + 0.02 * jax.random.normal(k, shape, f32)

    return {
        "x": jax.random.normal(ks[0], (BATCH, SEQ, D_MODEL), f32),
        "mem": jax.random.normal(ks[1], (BATCH, N_MEM, D_MODEL), f32),
        "w_in": nrm(ks[2], (DEPTH, D_MODEL, D_IN_2), D_MODEL),
        "w_a2": nrm(ks[3], (DEPTH, GATE_RANK, D_QK), GATE_RANK),
        "b_a": 1.0 + 0.5 * jax.random.normal(ks[4], (DEPTH, D_QK), f32),
        "gla_norm_g": gain(ks[5], (DEPTH, D_GLA)),
        "w_s": nrm(ks[6], (DEPTH, SGU_GROUPS, SGU_BLOCK, SGU_BLOCK), SGU_BLOCK),
        "b_s": gain(ks[7], (DEPTH, SGU_GROUPS, SGU_BLOCK)),
        "sgu_ln_g": gain(ks[8], (DEPTH, D_SGU)),
        "sgu_ln_b": 0.02 * jax.random.normal(ks[9], (DEPTH, D_SGU), f32),
        "w_out": nrm(ks[10], (DEPTH, D_MIX, D_MODEL), D_MIX, DN_BETA),
        "wq_x": nrm(ks[11], (DEPTH, D_MODEL, D_MODEL), D_MODEL),
        "wk_x": nrm(ks[12], (DEPTH, D_MODEL, D_MODEL), D_MODEL),
        "wv_x": nrm(ks[13], (DEPTH, D_MODEL, D_MODEL), D_MODEL),
        "wo_x": nrm(ks[14], (DEPTH, D_MODEL, D_MODEL), D_MODEL, DN_BETA),
        "w_router": nrm(ks[15], (D_MODEL, N_EXPERTS), D_MODEL),
        "b_router": 0.01 * jax.random.normal(ks[16], (N_EXPERTS,), f32),
        "w_gate": nrm(ks[17], (DEPTH, N_EXPERTS, D_MODEL, D_EXPERT), D_MODEL),
        "w_up": nrm(ks[18], (DEPTH, N_EXPERTS, D_MODEL, D_EXPERT), D_MODEL),
        "w_down": nrm(ks[19], (DEPTH, N_EXPERTS, D_EXPERT, D_MODEL), D_EXPERT, DN_BETA),
        "ln_g": gain(ks[20], (DEPTH, 3, D_MODEL)),
        "ln_b": 0.02 * jax.random.normal(ks[21], (DEPTH, 3, D_MODEL), f32),
    }

def second_block(x, mem, w_in, w_a2, b_a, gla_norm_g, w_s, b_s, sgu_ln_g, sgu_ln_b, w_out,
              wq_x, wk_x, wv_x, wo_x, w_router, b_router, w_gate, w_up, w_down, ln_g, ln_b):
    for l in range(DEPTH):
        q, k, v, r, a_low, u, v_sgu = split_proj(x @ w_in[l])
        y_gla = gla_group(q, k, v, r, a_low, w_a2[l], b_a[l], gla_norm_g[l])
        y_sgu = sgu_group(u, v_sgu, w_s[l], b_s[l], sgu_ln_g[l], sgu_ln_b[l])
        h = jnp.concatenate([y_gla, y_sgu], axis=-1) @ w_out[l]
        x = layer_norm(DN_ALPHA * x + h, ln_g[l, 0], ln_b[l, 0])
        h = mem_xattn(x, mem, wq_x[l], wk_x[l], wv_x[l], wo_x[l])
        x = layer_norm(DN_ALPHA * x + h, ln_g[l, 1], ln_b[l, 1])
        h = grouped_moe(x, w_router, b_router, w_gate[l], w_up[l], w_down[l])
        x = layer_norm(DN_ALPHA * x + h, ln_g[l, 2], ln_b[l, 2])
    return x


def setup_inputs(seed=0):
    out = dict(first_inputs(seed))
    for name, value in second_inputs(seed + 1).items():
        if name != "x":
            out[name + "_2"] = value
    return out


def reference(
    x, rel_bias, ffn1_norm, ffn1_w_gate, ffn1_w_up, ffn1_w_down, mix_norm, w_in, nsa_q_norm,
    nsa_k_norm, nsa_cmp_pos, nsa_cmp_k_w1, nsa_cmp_k_w2, nsa_cmp_v_w1, nsa_cmp_v_w2, swa_q_norm,
    swa_k_norm, swa_sinks, w_up_nsa, w_up_sb, w_up_swa, w_out, ffn2_norm, ffn2_w_gate,
    ffn2_w_up, ffn2_w_down, mem_2, w_in_2, w_a2_2, b_a_2, gla_norm_g_2, w_s_2, b_s_2,
    sgu_ln_g_2, sgu_ln_b_2, w_out_2, wq_x_2, wk_x_2, wv_x_2, wo_x_2, w_router_2, b_router_2,
    w_gate_2, w_up_2, w_down_2, ln_g_2, ln_b_2,
):
    x = first_block(
        x, rel_bias, ffn1_norm, ffn1_w_gate, ffn1_w_up, ffn1_w_down, mix_norm, w_in, nsa_q_norm,
        nsa_k_norm, nsa_cmp_pos, nsa_cmp_k_w1, nsa_cmp_k_w2, nsa_cmp_v_w1, nsa_cmp_v_w2,
        swa_q_norm, swa_k_norm, swa_sinks, w_up_nsa, w_up_sb, w_up_swa, w_out, ffn2_norm,
        ffn2_w_gate, ffn2_w_up, ffn2_w_down,
    )
    return second_block(
        x, mem_2, w_in_2, w_a2_2, b_a_2, gla_norm_g_2, w_s_2, b_s_2, sgu_ln_g_2, sgu_ln_b_2,
        w_out_2, wq_x_2, wk_x_2, wv_x_2, wo_x_2, w_router_2, b_router_2, w_gate_2, w_up_2,
        w_down_2, ln_g_2, ln_b_2,
    )


_drawn_inputs = setup_inputs


def setup_inputs(seed=0):
    import zlib

    import numpy as np

    out = dict(_drawn_inputs(seed))
    spreads = {}
    factors = {'nsa_q_norm': 5.378,
     'nsa_k_norm': 4.363,
     'swa_q_norm': 8.0,
     'swa_k_norm': 3.403,
     'swa_sinks': 3.377,
     'gla_norm_g_2': 8.0,
     'b_s_2': 3.865,
     'sgu_ln_g_2': 5.336,
     'sgu_ln_b_2': 6.545,
     'b_router_2': 3.273}
    for name, (base, spread) in spreads.items():
        noise = np.random.default_rng([zlib.crc32(name.encode()), seed]).standard_normal(out[name].shape)
        drawn = base * np.exp(spread * noise) if base else spread * noise
        out[name] = __import__('jax').numpy.asarray(drawn.astype(out[name].dtype))
    for name, factor in factors.items():
        out[name] = (out[name] * factor).astype(out[name].dtype)
    return out
```

```python
import math
from contextlib import ExitStack, contextmanager

import numpy as np

import concourse.bass as bass
from concourse import mybir

F32 = mybir.dt.float32
ALU = mybir.AluOpType
ACT = mybir.ActivationFunctionType
AX = mybir.AxisListType

P = 128
S = 256
T = S // P
D = 1024
K = D // P
L = 2
F = 2816
FP = F // 256
FR = F // 256
HD = 64
D_IN = 5656
W1 = 202
N1 = D_IN // W1
D_IN2 = 2576
W2 = 184
N2 = D_IN2 // W2
SLOTS = 4
SLOT = 2048
NE = 16
DE = 512
NCMP = 15
(NQ, KC, VC, KS, VS, KW, VW, NG, SQ_, SK_, SV_, WQ, WK, WV, BG) = (
    0, 512, 640, 768, 896, 1024, 1152, 1280, 1304, 1560, 1816, 2072, 2328, 2456, 2584)
GQ, GK, GV, GR, GA, SU, SV2 = 0, 256, 512, 1024, 1536, 1552, 2064
ALPHA = (2.0 * L) ** 0.25
C1 = (FP * 2 + FR) * 2 + N1 + 4 + 2 + 4 + 4
C2 = N2 + 4 + 16 + 6 * NE + 2
V_F1, V_MIX, V_F2, V_POS, V_QN, V_KN, V_WQN, V_WKN, V_GN, V_BS = 0, 8, 16, 24, 40, 41, 42, 43, 44, 48
VL = 52
(O_ID, O_MB, O_MS, O_MC, O_MCN, O_SB, O_SBN, O_U, O_ONE, O_REV, O_CHO, O_FLIP) = (
    0, 128, 384, 640, 670, 700, 1084, 1468, 1596, 1724, 1852, 1854)
CONW = 1982
DVE1, DVE2 = 59, 50
NLOAD = 1 + L * (3 + 1 + 8 + 2) + 5
UNITS = [(2, 0, 0), (2, 0, 1)] + [(k, g, t) for k in range(2) for g in range(2) for t in range(T)]
NU = len(UNITS)


def both(u):
    return sum(t for _, _, t in UNITS[:u])



class Ring:

    def __init__(self):
        self.v, self.n = 0, 0

    def next(self):
        self.n += 1
        return (self.n - 1) % SLOTS

    def full(self):
        return self.v * (16 // SLOTS) + 16 * ((self.n - 1) // SLOTS + 1)

    def done(self):
        return self.v + SLOTS + self.n


class Steps:

    def __init__(self, eng, sem):
        self.eng, self.sem, self.v, self.n = eng, sem, 0, 0

    def link(self, ins):
        ins.then_inc(self.sem, 1)
        self.n += 1
        self.eng.wait_ge(self.sem, self.v + self.n)


def wait_apart(eng, sem, value, held, least):
    value = eng.compute_val(value)
    eng.wait_ge(held, least)
    eng.wait_ge(sem, value)


@contextmanager
def loop(eng, count, *counters):
    before = [(c.v, c.n) for c, _ in counters]
    with eng.Fori(0, count) as i:
        for (c, per), (v, n) in zip(counters, before):
            c.v = v + i * per
        yield i
        for (c, per), (v, n) in zip(counters, before):
            assert c.n - n == per, f"a turn has {c.n - n} steps, not {per}"
    for (c, per), (v, n) in zip(counters, before):
        c.v, c.n = v, n + count * per


def build(nc, a, out, con, hot_rev, hot, scratch):
    ctx = ExitStack()
    with ctx:
        def sb(name, shape):
            return ctx.enter_context(nc.sbuf_tensor(name, shape, F32))[:]

        def sem(name):
            return ctx.enter_context(nc.semaphore(name))

        CON = sb("CON", [P, CONW])
        IDENT = CON[:, O_ID:O_ID + P]
        X = sb("X", [P, T, D])
        TMP = sb("TMP", [P, T, D])
        HT = sb("HT", [P, K, S])
        RINGS = sb("RINGS", [P, SLOTS, SLOT])
        PROJ = sb("PROJ", [P, T, D_IN])
        GT = PROJ.rearrange("p t n -> p (t n)")[:, 0:22 * S].rearrange("p (j n) -> p j n", n=S)
        TT = sb("TT", [P, 20, S])
        QKN = sb("QKN", [P, T, 18, HD])
        KD = sb("KD", [P, T, 5, 2, 2, HD])
        BIAS = sb("BIAS", [P, 12, S])
        BIASC = sb("BIASC", [P, 16, NCMP])
        PR = sb("PR", [P, 2, 4, S])
        PT = sb("PT", [P, 2, 2, 512])
        Y = sb("Y", [P, T, D])
        BT = sb("BT", [P, 2, 16, 64])
        LV = sb("LV", [P, VL + 2])
        VECT = sb("VECT", [P, L * VL])
        VEC = sb("VEC", [L * VL, P])
        HS = sb("HS", [64, 2, 256])
        HST = sb("HST", [P, 2, 64])
        HSTV = sb("HSTV", [P, 2, 4, 32])
        KCN = sb("KCN", [64, 2, HD])
        KCT = sb("KCT", [P, 64])
        VCB = sb("VCB", [P, 4, HD])
        PC = sb("PC", [P, 16, 32])
        SMALL = sb("SMALL", [P, 512])
        SINK = sb("SINK", [P, L, 4])
        NEGH = sb("NEGH", [P, 64])
        WAB = sb("WAB", [17, S])
        AT = sb("AT", [32, S])
        BR = sb("BR", [P, NE])
        GATE = sb("GATE", [P, NE, T])
        GCUR = sb("GCUR", [P, 4])
        COEF = sb("COEF", [P, 2, 4])
        SINKL = sb("SINKL", [P, 4])
        YD = sb("YD", [P, 256])
        RTN = sb("RTN", [P, 8])
        RTC = sb("RTC", [P, 128])
        RB = sb("RB", [32, 12])
        RBP = sb("RBP", [32, 3, 2, 2])

        def flat(x):
            return x.rearrange("p t n -> p (t n)")

        MEMT = flat(KD.rearrange("p t a b c d -> p t (a b c d)"))[:, 0:2048].rearrange("p (k n) -> p k n", n=S)
        HOTR = flat(PROJ)[0:32, 0:512]
        HOT = flat(PROJ)[0:32, 512:1024]
        VBIAS = flat(PROJ)[0:12, 1024:1536]
        BFLIP = flat(PROJ)[:, 2048:2048 + 12 * S].rearrange("p (h n) -> p h n", h=12)
        SIL = flat(Y)[:, 0:1024].rearrange("p (a n) -> p a n", a=2)
        EX = flat(TMP)[:, 0:1536].rearrange("p (h n) -> p h n", h=4)
        GX = PR.rearrange("p u h n -> p (u h n)")[:, 0:1024].rearrange("p (h n) -> p h n", h=4)
        ZS = PR.rearrange("p u h n -> p (u h n)")[:, 0:1536].rearrange("p (h n) -> p h n", h=4)
        LNGB = flat(BIAS)[:, 0:2 * D].rearrange("p (g n) -> p g n", g=2)
        SGB = flat(BIAS)[:, 2 * D:2 * D + 1024].rearrange("p (g n) -> p g n", g=2)
        BTF = BT.rearrange("p a r n -> p (a r n)")
        STATE = BTF[:, 0:1280].rearrange("p (c h v) -> p c h v", c=5, h=2)
        WST = BTF[:, 1280:1792].rearrange("p (g t) -> p g t", g=4)
        VX = flat(PROJ)[:, 0:2048].rearrange("p (t n) -> p t n", t=2)
        PXT = flat(PROJ)[:, 2048:4096].rearrange("p (b h n) -> p b h n", b=2, h=4)
        EH = flat(PROJ)[:, 4096:5120].rearrange("p (j n) -> p j n", n=S)
        KDEC = QKN[:, :, 0:4, :].rearrange("p t h d -> p t (h d)")
        KEXP = QKN[:, :, 4:8, :].rearrange("p t h d -> p t (h d)")

        def spread(ap, at, n):
            return bass.AP(tensor=ap.tensor, offset=ap.offset, ap=[*ap.ap[:at], [0, n], *ap.ap[at:]])

        PS = ctx.enter_context(nc.psum_tensor("PS", [P, 8, 512], F32))[:]

        ring_full = [sem(f"ring_full{i}") for i in range(SLOTS)]
        chunks_done = sem("chunks_done")
        consts_loaded = sem("consts_loaded")
        x_loaded = sem("x_loaded")
        mem_loaded = sem("mem_loaded")
        bias_row = sem("bias_row")
        rb_ready = sem("rb_ready")
        bias_stored = sem("bias_stored")
        bias_loaded = sem("bias_loaded")
        hot_ready = sem("hot_ready")
        vec_ready = sem("vec_ready")
        vec_taken = sem("vec_taken")
        lv_ready = sem("lv_ready")
        zeroed = sem("zeroed")
        x_ready = sem("x_ready")
        squares_ready = sem("squares_ready")
        rstd_ready = sem("rstd_ready")
        src_ready = sem("src_ready")
        tr_ready = sem("tr_ready")
        ht_a = sem("ht_a")
        ht_d = sem("ht_d")
        silu_ready = sem("silu_ready")
        hidden_ready = sem("hidden_ready")
        proj_a = sem("proj_a")
        proj_d = sem("proj_d")
        head_sq = sem("head_sq")
        head_ms = sem("head_ms")
        head_rstd = sem("head_rstd")
        gates_ready = sem("gates_ready")
        heads_ready = sem("heads_ready")
        keys_copied = sem("keys_copied")
        htr_ready = sem("htr_ready")
        tt_a = sem("tt_a")
        tt_d = sem("tt_d")
        blocks_ready = sem("blocks_ready")
        cmp_hidden = sem("cmp_hidden")
        cmp_tr = sem("cmp_tr")
        cmp_trs = sem("cmp_trs")
        cmp_ms = sem("cmp_ms")
        cmp_rstd = sem("cmp_rstd")
        cmp_keys = sem("cmp_keys")
        cmp_kt = sem("cmp_kt")
        cmp_kts = sem("cmp_kts")
        scc_ready = sem("scc_ready")
        pc_in = sem("pc_in")
        pc_exp = sem("pc_exp")
        pc_ready = sem("pc_ready")
        pct_ready = sem("pct_ready")
        pct_taken = sem("pct_taken")
        oc_ready = sem("oc_ready")
        sc_ready = sem("sc_ready")
        sc_taken = sem("sc_taken")
        sc_max = sem("sc_max")
        exp_ready = sem("exp_ready")
        pt_ready = sem("pt_ready")
        pt_a = sem("pt_a")
        pt_d = sem("pt_d")
        o_ready = sem("o_ready")
        o_taken = sem("o_taken")
        z_ready = sem("z_ready")
        z_copied = sem("z_copied")
        z_abs = sem("z_abs")
        z_ln = sem("z_ln")
        sp_ready = sem("sp_ready")
        after_ready = sem("after_ready")
        w_arg = sem("w_arg")
        w_ready = sem("w_ready")
        osb_ready = sem("osb_ready")
        rows_taken = sem("rows_taken")
        ga_ready = sem("ga_ready")
        ga_copied = sem("ga_copied")
        gl_ready = sem("gl_ready")
        gl_abs = sem("gl_abs")
        gl_ln = sem("gl_ln")
        gl_sp = sem("gl_sp")
        gl_cum = sem("gl_cum")
        gl_exp = sem("gl_exp")
        kdec_ready = sem("kdec_ready")
        kv_ready = sem("kv_ready")
        state_ready = sem("state_ready")
        go_ready = sem("go_ready")
        go_sq = sem("go_sq")
        gs_ms = sem("gs_ms")
        gs_rstd = sem("gs_rstd")
        gelu_ready = sem("gelu_ready")
        sv_centred = sem("sv_centred")
        sv_sq = sem("sv_sq")
        vn_ready = sem("vn_ready")
        mix_ready = sem("mix_ready")
        layer_in = sem("layer_in")
        ws_copied = sem("ws_copied")
        lngb_in = sem("lngb_in")
        qk_a = sem("qk_a")
        qk_d = sem("qk_d")
        vx_a = sem("vx_a")
        vx_d = sem("vx_d")
        xs_ready = sem("xs_ready")
        xm_ready = sem("xm_ready")
        xe_ready = sem("xe_ready")
        xp_ready = sem("xp_ready")
        xt_ready = sem("xt_ready")
        xt_a = sem("xt_a")
        xt_d = sem("xt_d")
        xo_ready = sem("xo_ready")
        xo_a = sem("xo_a")
        xo_d = sem("xo_d")
        rt_in = sem("rt_in")
        rt_exp = sem("rt_exp")
        moe_taken = sem("moe_taken")
        out_ready = sem("out_ready")
        out_stored = sem("out_stored")
        act_step = sem("act_step")
        dve_step = sem("dve_step")
        pool_step = sem("pool_step")

        def tr1(l, k):
            return l * 5 + k

        def tr2(l, k):
            return 1 + 5 * L + l * 4 + k

        def st1(l, k):
            return l * 3 + k

        def st2(l, k):
            return 3 * L + l * 3 + k

        x_view = a["x"][0].rearrange("(t p) n -> p t n", p=P)
        out_view = out[0].rearrange("(t p) n -> p t n", p=P)

        block = ctx.enter_context(nc.Block())

        @block.sync
        def _(sp):
            ring = Ring()

            def load(src, shape_fn):
                slot = ring.next()
                sp.wait_ge(chunks_done, ring.v + ring.n)
                sp.dma_start(shape_fn(RINGS[:, slot, :]), src).then_inc(ring_full[slot], 16)

            def cols(w, l, c0, n):
                src = w[l].rearrange("(k p) n -> p k n", p=P)[:, :, bass.ds(c0, n)]
                load(src, lambda r: r[:, 0:src.shape[1] * n].rearrange("p (k n) -> p k n", n=n))

            def rows(w, l, r0, n=D):
                src = w[l, bass.ds(r0, 2 * P), :].rearrange("(k p) n -> p k n", p=P)
                load(src, lambda r: r[:, 0:2 * n].rearrange("p (k n) -> p k n", n=n))

            def many(count, fn, per=1):
                unit = SLOTS // math.gcd(SLOTS, per)
                whole = count // unit
                if whole > 1:
                    with loop(sp, whole, (ring, unit * per)) as i:
                        for j in range(unit):
                            fn(i * unit + j)
                    left = whole * unit
                else:
                    left = 0
                for j in range(left, count):
                    fn(j)

            def swiglu(l, n):
                def pair(j):
                    cols(a[n + "_w_gate"], l, j * 256, 256)
                    cols(a[n + "_w_up"], l, j * 256, 256)
                many(FP, pair, 2)
                many(FR, lambda j: rows(a[n + "_w_down"], l, j * 256))

            with loop(sp, L, (ring, C1)) as l:
                swiglu(l, "ffn1")
                many(N1, lambda j: cols(a["w_in"], l, j * W1, W1))
                for kv in ("k", "v"):
                    for i in range(2):
                        src = a[f"nsa_cmp_{kv}_w1"][l, i * 1024:(i + 1) * 1024, :].rearrange("(k p) n -> p k n", p=P)
                        load(src, lambda r: r.rearrange("p (k n) -> p k n", n=256))
                for kv in ("k", "v"):
                    src = a[f"nsa_cmp_{kv}_w2"][l].rearrange("(k p) n -> p k n", p=P)
                    load(src, lambda r: r[:, 0:2 * HD].rearrange("p (k n) -> p k n", n=HD))
                rows(a["w_up_nsa"], l, 0)
                rows(a["w_up_nsa"], l, 256)
                rows(a["w_up_sb"], l, 0)
                rows(a["w_up_swa"], l, 0)
                many(4, lambda j: rows(a["w_out"], l, j * 256))
                swiglu(l, "ffn2")

            with loop(sp, L, (ring, C2)) as l:
                many(N2, lambda j: cols(a["w_in_2"], l, j * W2, W2))
                load(a["w_s_2"][l].rearrange("g t s -> t g s"),
                     lambda r: r[:, 0:512].rearrange("p (g s) -> p g s", s=P))
                many(4, lambda j: rows(a["w_out_2"], l, j * 256))
                for n in ("wq_x_2", "wk_x_2", "wv_x_2"):
                    many(4, lambda j: cols(a[n], l, j * 256, 256))
                many(4, lambda j: rows(a["wo_x_2"], l, j * 256))
                src_r = a["w_router_2"].rearrange("(k p) n -> p k n", p=P)
                load(src_r, lambda r: r[:, 0:K * NE].rearrange("p (k n) -> p k n", n=NE))

                def expert(e):
                    for i in range(2):
                        for w in (a["w_gate_2"], a["w_up_2"]):
                            src = w[l].rearrange("e (k p) n -> p e k n", p=P)[:, bass.ds(e, 1), :, i * 256:(i + 1) * 256]
                            load(src.rearrange("p e k n -> p (e k) n"), lambda r: r.rearrange("p (k n) -> p k n", n=256))
                    for i in range(2):
                        src = a["w_down_2"][l].rearrange("e (k p) n -> p e k n", p=P)[:, bass.ds(e, 1), 2 * i:2 * i + 2, :]
                        load(src.rearrange("p e k n -> p (e k) n"), lambda r: r.rearrange("p (k n) -> p k n", n=D))
                many(NE, expert, 6)

        @block.gpsimd
        def _(pool):
            steps = Steps(pool, pool_step)
            nload = 0
            nc.gpsimd.dma_start(CON, con).then_inc(consts_loaded, 16)
            nload += 1
            for l in range(L):
                b = l * VL
                for name, at, n in (("ffn1_norm", V_F1, 8), ("mix_norm", V_MIX, 8), ("ffn2_norm", V_F2, 8)):
                    nc.gpsimd.dma_start(VEC[b + at:b + at + n, :], a[name][l].rearrange("(k p) -> k p", p=P)).then_inc(consts_loaded, 16)
                    nload += 1
                nc.gpsimd.dma_start(VEC[b + V_POS:b + V_POS + 16, :],
                                    a["nsa_cmp_pos"][l].rearrange("(r q) d -> r (q d)", q=2)).then_inc(consts_loaded, 16)
                nload += 1
                for name, at in (("nsa_q_norm", V_QN), ("nsa_k_norm", V_KN), ("swa_q_norm", V_WQN), ("swa_k_norm", V_WKN)):
                    for h in range(2):
                        nc.gpsimd.dma_start(VEC[b + at:b + at + 1, h * HD:(h + 1) * HD], a[name][l:l + 1, :]).then_inc(consts_loaded, 16)
                        nload += 1
                nc.gpsimd.dma_start(VEC[b + V_GN:b + V_GN + 4, :], a["gla_norm_g_2"][l].rearrange("(k p) -> k p", p=P)).then_inc(consts_loaded, 16)
                nc.gpsimd.dma_start(VEC[b + V_BS:b + V_BS + 4, :], a["b_s_2"][l]).then_inc(consts_loaded, 16)
                nload += 2
            nc.gpsimd.dma_start(RB, a["rel_bias"]).then_inc(consts_loaded, 16)
            nc.gpsimd.dma_start(HOTR, hot_rev).then_inc(consts_loaded, 16)
            nc.gpsimd.dma_start(HOT, hot).then_inc(consts_loaded, 16)
            nc.gpsimd.dma_start(SINK.rearrange("p l h -> p (l h)"),
                                a["swa_sinks"].rearrange("l h -> (l h)").rearrange("(o n) -> o n", o=1).to_broadcast([P, L * 4])).then_inc(consts_loaded, 16)
            nc.gpsimd.dma_start(BR, a["b_router_2"].rearrange("(o n) -> o n", o=1).to_broadcast([P, NE])).then_inc(consts_loaded, 16)
            nload += 5
            assert nload == NLOAD
            nc.gpsimd.memset(NEGH, -0.5).then_inc(zeroed, 1)
            nc.gpsimd.memset(BT, 0.0).then_inc(zeroed, 1)
            nc.gpsimd.memset(PC, 0.0).then_inc(zeroed, 1)
            nc.gpsimd.memset(AT, 1.0).then_inc(zeroed, 1)
            nc.gpsimd.memset(VCB, 0.0).then_inc(zeroed, 1)
            pool.wait_ge(bias_row, 1)
            nc.gpsimd.dma_start(scratch, VBIAS).then_inc(bias_stored, 16)
            pool.wait_ge(bias_stored, 16)
            nc.gpsimd.dma_start(BFLIP, bass.AP(tensor=scratch.tensor, offset=P, ap=[[1, P], [512, 12], [1, S]])).then_inc(bias_loaded, 16)
            pool.wait_ge(zeroed, 1)

            def row_rstd(n, eps):
                wait_apart(pool, squares_ready, n + 1, zeroed, 1)
                steps.link(nc.gpsimd.tensor_scalar(SMALL[:, 2:4], SMALL[:, 0:2], 1.0 / D, eps, ALU.mult, ALU.add))
                nc.gpsimd.tensor_tensor(SMALL[:, 4:6], SMALL[:, 2:4], NEGH[:, 0:2], ALU.pow).then_inc(rstd_ready, 1)

            with loop(pool, L, (steps, 3)) as l:
                row_rstd(st1(l, 0), 1e-6)
                row_rstd(st1(l, 1), 1e-6)
                pool.wait_ge(head_ms, l + 1)
                nc.gpsimd.tensor_tensor(SMALL[:, 96:132], SMALL[:, 48:84], NEGH[:, 0:36], ALU.pow).then_inc(head_rstd, 1)
                pool.wait_ge(cmp_ms, l + 1)
                nc.gpsimd.tensor_tensor(SMALL[0:64, 141:142], SMALL[0:64, 140:141], NEGH[0:64, 0:1], ALU.pow).then_inc(cmp_rstd, 1)
                row_rstd(st1(l, 2), 1e-6)

            with loop(pool, L, (steps, 3)) as l:
                for k in range(3):
                    pool.wait_ge(src_ready, tr2(l, 0 if k == 0 else k + 1) + 1)
                    for i, n in enumerate(("ln_g_2", "ln_b_2")):
                        nc.gpsimd.dma_start(LNGB[:, i, :], a[n][bass.ds(l, 1), k, :].to_broadcast([P, D])).then_inc(lngb_in, 16)
                    if k == 0:
                        nc.gpsimd.dma_start(SGB[:, 0, :], a["sgu_ln_g_2"][bass.ds(l, 1), :].to_broadcast([P, 512])).then_inc(layer_in, 16)
                        nc.gpsimd.dma_start(SGB[:, 1, :], a["sgu_ln_b_2"][bass.ds(l, 1), :].to_broadcast([P, 512])).then_inc(layer_in, 16)
                        nc.gpsimd.dma_start(WAB[0:16, :], a["w_a2_2"][l]).then_inc(layer_in, 16)
                        nc.gpsimd.dma_start(WAB[16:17, :], a["b_a_2"][bass.ds(l, 1), :]).then_inc(layer_in, 16)
                        pool.wait_ge(gs_ms, l + 1)
                        nc.gpsimd.tensor_tensor(SMALL[:, 176:192], SMALL[:, 160:176], NEGH[:, 0:16], ALU.pow).then_inc(gs_rstd, 1)
                    row_rstd(st2(l, k), 1e-5)

        @block.tensor
        def _(pe):
            ring = Ring()
            mm = nc.tensor.matmul

            def take():
                slot = ring.next()
                pe.wait_ge(ring_full[slot], ring.full())
                return RINGS[:, slot, :]

            def transpose_rows(src, n):
                pe.wait_ge(ht_a, n * 2 + 2)
                pe.wait_ge(ht_d, n * 2 + 2)
                pe.wait_ge(src_ready, n + 1)
                for b in range(4):
                    for k in range(2):
                        for t in range(T):
                            last = nc.tensor.transpose(PS[:, b, k * S + t * P:k * S + (t + 1) * P],
                                                       src[:, t, (2 * b + k) * P:(2 * b + k + 1) * P], IDENT)
                    last.then_inc(tr_ready, 1)

            def ht_wait(n):
                wait_apart(pe, ht_a, n * 2 + 4, consts_loaded, 16 * NLOAD)
                pe.wait_ge(ht_d, n * 2 + 4)

            def swiglu(l, f):
                n = tr1(l, 4 * f)
                transpose_rows(TMP, n)
                ht_wait(n)

                def pair(j, par):
                    for u in range(2):
                        w = take().rearrange("p (k n) -> p k n", n=256)
                        if u == 0:
                            pe.wait_ge(hidden_ready, l * 22 + f * 11 + j + 1)
                        for c in range(2):
                            for k in range(K):
                                last = mm(PS[:, 2 * par + u, c * S:(c + 1) * S], w[:, k, c * P:(c + 1) * P], HT[:, k, :],
                                          start=(k == 0), stop=(k == K - 1))
                        last.then_inc(chunks_done, 1)

                with loop(pe, 5, (ring, 4)) as i:
                    for j in range(2):
                        pair(i * 2 + j, j)
                pair(10, 0)
                for j in range(FR):
                    w = take().rearrange("p (k n) -> p k n", n=D)
                    pe.wait_ge(hidden_ready, l * 22 + f * 11 + j + 3)
                    for k in range(2):
                        for t in range(T):
                            for h in range(2):
                                last = mm(PS[:, 4 + 2 * t + h, :], GT[:, 2 * j + k, t * P:(t + 1) * P], w[:, k, h * 512:(h + 1) * 512],
                                          start=(j + k == 0), stop=(j == FR - 1 and k == 1))
                    last.then_inc(chunks_done, 1)

            def rows_product(lhs, nchunk, bank, k0=0):
                for j in range(nchunk):
                    w = take().rearrange("p (k n) -> p k n", n=D)
                    for k in range(2):
                        for t in range(T):
                            for h in range(2):
                                last = mm(PS[:, bank + 2 * t + h, :], lhs[:, k0 + 2 * j + k, t * P:(t + 1) * P],
                                          w[:, k, h * 512:(h + 1) * 512],
                                          start=(j + k == 0), stop=(j == nchunk - 1 and k == 1))
                    last.then_inc(chunks_done, 1)

            def project(base, width, j, par):
                w = take()[:, 0:K * width].rearrange("p (k n) -> p k n", n=width)
                pe.wait_ge(proj_a, base + j + 1)
                pe.wait_ge(proj_d, base + j + 1)
                for t in range(T):
                    for k in range(K):
                        last = mm(PS[:, 2 * par + t, 0:width], HT[:, k, t * P:(t + 1) * P], w[:, k, :],
                                  start=(k == 0), stop=(k == K - 1))
                last.then_inc(chunks_done, 1)

            pe.sem_inc(chunks_done, SLOTS)
            pe.wait_ge(consts_loaded, 16 * NLOAD)
            nc.tensor.transpose(PS[:, 4, 0:L * VL], VEC, IDENT[0:L * VL, 0:L * VL]).then_inc(vec_ready, 1)
            pe.wait_ge(rb_ready, 1)
            mm(PS[0:12, 5, :], RBP.rearrange("p g b a -> p (g b a)"), HOTR, start=True, stop=True).then_inc(hot_ready, 1)
            for t in range(T):
                for n in range(NCMP):
                    u = t * P - 16 * n - 31 + 256
                    last = mm(PS[:, 6, (t * NCMP + n) * 8:(t * NCMP + n + 1) * 8], HOT[:, u:u + P], RB[:, 0:8], start=True, stop=True)
            last.then_inc(hot_ready, 1)
            pe.wait_ge(bias_loaded, 16)
            pe.wait_ge(vec_taken, 5)
            for b in range(6):
                last = mm(PS[:, b, :], CON[:, O_FLIP:O_FLIP + P], BFLIP[:, 2 * b:2 * b + 2, :].rearrange("p h n -> p (h n)"), start=True, stop=True)
            last.then_inc(hot_ready, 1)
            pe.wait_ge(vec_taken, 7)

            with loop(pe, L, (ring, C1)) as l:
                swiglu(l, 0)
                n = tr1(l, 1)
                transpose_rows(TMP, n)
                ht_wait(n)
                with loop(pe, N1 // 4, (ring, 4)) as i:
                    for j in range(4):
                        project(l * N1, W1, i * 4 + j, j % 2)
                pe.wait_ge(proj_a, l * N1 + N1 + 2)
                pe.wait_ge(proj_d, l * N1 + N1 + 2)
                pe.wait_ge(heads_ready, l + 1)
                pe.wait_ge(keys_copied, l + 1)
                for b in range(10):
                    if b >= 4:
                        pe.wait_ge(tt_a if b % 2 == 0 else tt_d, l * 5 + (b - 4) // 2 + 1)
                    for i in range(2):
                        for t in range(T):
                            if b < 3:
                                src = QKN[:, t, 4 * b + 2 * i:4 * b + 2 * i + 2, :].rearrange("p h d -> p (h d)")
                            elif b < 8:
                                src = KD[:, t, b - 3, i, :, :].rearrange("p u d -> p (u d)")
                            else:
                                c = (SQ_ if b == 8 else SK_) + i * P
                                src = PROJ[:, t, c:c + P]
                            last = nc.tensor.transpose(PS[:, b % 4, i * S + t * P:i * S + (t + 1) * P], src, IDENT)
                    last.then_inc(htr_ready, 1)
                pe.wait_ge(blocks_ready, l + 1)
                for kv in range(2):
                    for i in range(2):
                        w = take().rearrange("p (k n) -> p k n", n=256)
                        for r in range(8):
                            last = mm(PS[0:64, 4 + kv, 0:256], BT[:, kv, i * 8 + r, :], w[:, r, :],
                                      start=(i + r == 0), stop=(i == 1 and r == 7))
                        last.then_inc(chunks_done, 1)
                wait_apart(pe, cmp_hidden, 2 * l + 2, consts_loaded, 16 * NLOAD)
                for kv in range(2):
                    for i in range(2):
                        last = nc.tensor.transpose(PS[:, 6, (kv * 2 + i) * 64:(kv * 2 + i + 1) * 64],
                                                   HS[:, kv, i * P:(i + 1) * P], IDENT[0:64, 0:64])
                last.then_inc(cmp_tr, 1)
                pe.wait_ge(cmp_trs, l + 1)
                w = take()[:, 0:2 * HD].rearrange("p (k n) -> p k n", n=HD)
                for i in range(2):
                    last = mm(PS[0:64, 7, 0:HD], HST[:, i, :], w[:, i, :], start=(i == 0), stop=(i == 1))
                last.then_inc(chunks_done, 1)
                w = take()[:, 0:2 * HD].rearrange("p (k n) -> p k n", n=HD)
                for i in range(2):
                    last = mm(PS[:, 5, 0:HD], HSTV[:, i, :, :].rearrange("p a n -> p (a n)"), w[:, i, :],
                              start=(i == 0), stop=(i == 1))
                last.then_inc(chunks_done, 1)
                wait_apart(pe, cmp_keys, l + 1, consts_loaded, 16 * NLOAD)
                nc.tensor.transpose(PS[:, 6, 256:320], KCN.rearrange("p u d -> p (u d)"), IDENT[0:64, 0:64]).then_inc(cmp_kt, 1)
                pe.wait_ge(cmp_kts, l + 1)
                for t in range(T):
                    for h in range(8):
                        hp, g, at = 64 * (h % 2), h // 4, (t * 4 + h // 2) * 32
                        last = mm(PS[:, 4 + 3 * (h % 2), at:at + NCMP], TT[hp:hp + 64, h // 2, t * P:(t + 1) * P],
                                  KCT[hp:hp + 64, g * 32:g * 32 + NCMP], start=True, stop=True)
                last.then_inc(scc_ready, 1)

                def scores(u):
                    kind, g, t = UNITS[u]
                    nk = (t + 1) * P
                    n = l * NU + u
                    if u >= 2:
                        pe.wait_ge(sc_taken, n - 1)
                    for h in range(4):
                        if kind < 2:
                            q, kk, hp = (4 * g + h) // 2, 6 + 2 * kind + g, 64 * (h % 2)
                        else:
                            q, kk, hp = 4 + h // 2, 10 + h // 2, 64 * (h % 2)
                        last = mm(PS[:, 2 * (u % 2) + h % 2, (h // 2) * S:(h // 2) * S + nk], TT[hp:hp + 64, q, t * P:(t + 1) * P],
                                  TT[hp:hp + 64, kk, 0:nk], start=True, stop=True)
                    last.then_inc(sc_ready, 1)

                def values(u):
                    kind, g, t = UNITS[u]
                    n = l * NU + u
                    pe.wait_ge(exp_ready, n + 1)
                    if u >= 1:
                        pe.wait_ge(pt_a, n)
                        if both(u):
                            pe.wait_ge(pt_d, l * both(NU) + both(u))
                    for b in range(t + 1):
                        for h in range(4):
                            last = nc.tensor.transpose(PS[:, 4 + b, h * P:(h + 1) * P], PR[:, u % 2, h, b * P:(b + 1) * P], IDENT)
                    last.then_inc(pt_ready, 1)
                    pe.wait_ge(pt_a, n + 1)
                    if t:
                        pe.wait_ge(pt_d, l * both(NU) + both(u + 1))
                    pe.wait_ge(o_taken, l * (NU + 1) + max(u, 1))
                    for h in range(4):
                        vc = (VS if kind == 0 else VW) + g * HD if kind < 2 else WV + (h // 2) * HD
                        for b in range(t + 1):
                            s_ = 2 * (h % 2) + h // 2
                            last = mm(PS[:, 6 + u % 2, h * HD:(h + 1) * HD], PT[:, u % 2, b, s_ * P:(s_ + 1) * P], PROJ[:, b, vc:vc + HD],
                                      start=(b == 0), stop=(b == t))
                    last.then_inc(o_ready, 1)

                pe.wait_ge(tt_a, l * 5 + 5)
                pe.wait_ge(tt_d, l * 5 + 5)
                scores(0)
                pe.wait_ge(pc_ready, l + 1)
                for r in range(2):
                    for t in range(T):
                        last = nc.tensor.transpose(PS[:, 5, (r * 2 + t) * P:(r * 2 + t + 1) * P],
                                                   PC[:, r * 8 + t * 4:r * 8 + t * 4 + 4, :].rearrange("p h n -> p (h n)"), IDENT)
                last.then_inc(pct_ready, 1)
                pe.wait_ge(pct_taken, l + 1)
                for t in range(T):
                    for r in range(2):
                        last = mm(PS[:, 6 + t, r * 256:(r + 1) * 256], PT[:, 1, 0, (r * 2 + t) * P:(r * 2 + t + 1) * P],
                                  VCB.rearrange("p h d -> p (h d)"), start=True, stop=True)
                last.then_inc(oc_ready, 1)
                for u in range(NU):
                    if u + 1 < NU:
                        scores(u + 1)
                    values(u)
                pe.wait_ge(sc_taken, l * NU + NU)
                for h in range(4):
                    hp = 64 * (h % 2)
                    mm(PS[:, h, 0:S], TT[hp:hp + 64, 18 + h // 2, 0:P], TT[hp:hp + 64, 16 + h // 2, :], start=True, stop=True)
                    last = mm(PS[:, h, S:S + P], TT[hp:hp + 64, 18 + h // 2, P:S], TT[hp:hp + 64, 16 + h // 2, P:S], start=True, stop=True)
                last.then_inc(z_ready, 1)
                pe.wait_ge(sp_ready, l + 1)
                pe.wait_ge(o_taken, l * (NU + 1) + NU + 1)
                for h in range(4):
                    mm(PS[:, 4 + h, 0:P], CON[:, O_U:O_U + P], EX[:, h, 0:P], start=True, stop=True)
                    mm(PS[:, 4 + h, P:S], CON[:, O_U:O_U + P], EX[:, h, P:S], start=True, stop=False)
                    mm(PS[:, 4 + h, P:S], CON[:, O_ONE:O_ONE + P], EX[:, h, S:S + P], start=False, stop=True)
                    last = mm(PS[:, 4 + h, S:S + P], CON[:, O_U:O_U + P], EX[:, h, S:S + P], start=True, stop=True)
                last.then_inc(after_ready, 1)
                pe.wait_ge(w_ready, l + 1)
                for h in range(4):
                    vc = SV_ + h * HD
                    mm(PS[:, 0, h * HD:(h + 1) * HD], EX[:, h, 0:P], PROJ[:, 0, vc:vc + HD], start=True, stop=True)
                for h in range(4):
                    vc = SV_ + h * HD
                    mm(PS[:, 0, S + h * HD:S + (h + 1) * HD], EX[:, h, P:S], PROJ[:, 0, vc:vc + HD], start=True, stop=False)
                    last = mm(PS[:, 0, S + h * HD:S + (h + 1) * HD], EX[:, h, S:S + P], PROJ[:, 1, vc:vc + HD], start=False, stop=True)
                last.then_inc(osb_ready, 1)
                n = tr1(l, 2)
                transpose_rows(Y, n)
                ht_wait(n)
                rows_product(HT, 2, 0)
                rows_product(HT, 1, 4, k0=4)
                pe.wait_ge(rows_taken, l + 1)
                rows_product(HT, 1, 0, k0=6)
                n = tr1(l, 3)
                transpose_rows(Y, n)
                ht_wait(n)
                rows_product(HT, 4, 4)
                swiglu(l, 1)

            pe.wait_ge(mem_loaded, 16)
            transpose_rows(TMP, 5 * L)
            ht_wait(5 * L)

            with loop(pe, L, (ring, C2)) as l:
                n = tr2(l, 0)
                transpose_rows(X, n)
                ht_wait(n)
                with loop(pe, N2 // 4, (ring, 4)) as i:
                    for j in range(4):
                        project(L * N1 + l * N2, W2, i * 4 + j, j % 2)
                for j in range(N2 // 4 * 4, N2):
                    project(L * N1 + l * N2, W2, j, j % 2)
                w = take()[:, 0:512]
                for g in range(4):
                    last = nc.tensor.transpose(PS[:, 7, g * P:(g + 1) * P], w[:, g * P:(g + 1) * P], IDENT)
                last.then_inc(chunks_done, 1)
                pe.wait_ge(proj_a, L * N1 + l * N2 + N2 + 2)
                pe.wait_ge(proj_d, L * N1 + l * N2 + N2 + 2)
                for t in range(T):
                    nc.tensor.transpose(PS[0:16, 4, t * P:(t + 1) * P], PROJ[:, t, GA:GA + 16], IDENT)
                for hp in range(2):
                    for t in range(T):
                        last = nc.tensor.transpose(PS[:, 5, hp * S + t * P:hp * S + (t + 1) * P], PROJ[:, t, GQ + hp * P:GQ + (hp + 1) * P], IDENT)
                last.then_inc(ga_ready, 1)
                pe.wait_ge(ga_copied, 2 * l + 2)
                pe.wait_ge(layer_in, l * 64 + 64)
                for t in range(T):
                    last = mm(PS[:, 4, t * S:(t + 1) * S], AT[0:17, t * P:(t + 1) * P], WAB, start=True, stop=True)
                last.then_inc(gl_ready, 1)
                pe.wait_ge(gl_sp, l + 1)
                for t in range(T):
                    last = mm(PS[:, 6, t * S:(t + 1) * S], CON[:, O_REV:O_REV + P], GX[:, t, 0:S], start=True, stop=True)
                for t in range(T):
                    for hp in range(2):
                        last = mm(PS[:, 5, hp * 4 + 2 * t:hp * 4 + 2 * t + 2], GX[:, t, hp * P:(hp + 1) * P], CON[:, O_CHO:O_CHO + 2], start=True, stop=True)
                last.then_inc(gl_cum, 1)
                wait_apart(pe, kdec_ready, l + 1, consts_loaded, 16 * NLOAD)

                def kv(c):
                    t, half = c // 2, 64 * (c % 2)
                    if c >= 2:
                        wait_apart(pe, state_ready, l * 4 + c - 1, consts_loaded, 16 * NLOAD)
                    for h in range(4):
                        o = 64 * (h % 2)
                        last = mm(PS[o:o + 64, c % 2, (h // 2) * P:(h // 2 + 1) * P], KDEC[half:half + 64, t, h * HD:(h + 1) * HD],
                                  PROJ[half:half + 64, t, GV + h * P:GV + (h + 1) * P], start=True, stop=True)
                    last.then_inc(kv_ready, 1)

                kv(0)
                for c in range(4):
                    if c + 1 < 4:
                        kv(c + 1)
                    t, half = c // 2, 64 * (c % 2)
                    wait_apart(pe, state_ready, l * 4 + c + 1, consts_loaded, 16 * NLOAD)
                    for h in range(4):
                        o = 64 * (h % 2)
                        last = mm(PS[half:half + 64, 2 + 2 * (h % 2) + t, (h // 2) * P:(h // 2 + 1) * P], TT[o:o + 64, h // 2, c * 64:(c + 1) * 64],
                                  STATE[o:o + 64, c + 1, h // 2, :], start=True, stop=True)
                last.then_inc(go_ready, 1)
                pe.wait_ge(vn_ready, l + 1)
                pe.wait_ge(ws_copied, l + 1)
                for t in range(T):
                    for g in range(4):
                        last = mm(PS[:, 4 + t, g * P:(g + 1) * P], WST[:, g, :], PROJ[:, t, SV2 + g * P:SV2 + (g + 1) * P], start=True, stop=True)
                last.then_inc(mix_ready, 1)
                n = tr2(l, 1)
                transpose_rows(Y, n)
                ht_wait(n)
                rows_product(HT, 4, 4)
                n = tr2(l, 2)
                transpose_rows(X, n)
                ht_wait(n)
                for j in range(8):
                    w = take().rearrange("p (k n) -> p k n", n=256)
                    rhs = HT if j < 4 else MEMT
                    if j >= 2:
                        pe.wait_ge(qk_a if j % 2 == 0 else qk_d, l * 4 + j // 2)
                    for c in range(2):
                        for k in range(K):
                            last = mm(PS[:, j % 2, c * S:(c + 1) * S], w[:, k, c * P:(c + 1) * P], rhs[:, k, :], start=(k == 0), stop=(k == K - 1))
                    last.then_inc(chunks_done, 1)
                for j in range(4):
                    w = take().rearrange("p (k n) -> p k n", n=256)
                    if j >= 2:
                        pe.wait_ge(vx_a, l * 4 + j - 1)
                        pe.wait_ge(vx_d, l * 4 + j - 1)
                    for t in range(T):
                        for k in range(K):
                            last = mm(PS[:, 2 + 2 * (j % 2) + t, 0:256], MEMT[:, k, t * P:(t + 1) * P], w[:, k, :], start=(k == 0), stop=(k == K - 1))
                    last.then_inc(chunks_done, 1)
                for done in (qk_a, qk_d, vx_a, vx_d):
                    pe.wait_ge(done, l * 4 + 4)
                for t in range(T):
                    for h in range(4):
                        for k in range(2):
                            last = mm(PS[:, 2 * t + h // 2, (h % 2) * S:(h % 2 + 1) * S], TT[:, 2 * h + k, t * P:(t + 1) * P],
                                      TT[:, 8 + 2 * h + k, :], start=(k == 0), stop=(k == 1))
                    last.then_inc(xs_ready, 1)
                for t in range(T):
                    pe.wait_ge(xp_ready, l * 2 + t + 1)
                    for b in range(2):
                        for h in range(4):
                            last = nc.tensor.transpose(PS[:, 4 + 2 * t + b, h * P:(h + 1) * P], PR[:, t, h, b * P:(b + 1) * P], IDENT)
                    last.then_inc(xt_ready, 1)
                pe.wait_ge(xt_a, l * 2 + 2)
                pe.wait_ge(xt_d, l * 2 + 2)
                for h in range(4):
                    for c in range(2):
                        for b in range(2):
                            last = mm(PS[:, h, c * S:(c + 1) * S], VX[:, b, h * 256 + c * P:h * 256 + (c + 1) * P], PXT[:, b, h, :], start=(b == 0), stop=(b == 1))
                    last.then_inc(xo_ready, 1)
                pe.wait_ge(xo_a, l * 2 + 2)
                pe.wait_ge(xo_d, l * 2 + 2)
                rows_product(HT, 4, 4)
                n = tr2(l, 3)
                transpose_rows(X, n)
                ht_wait(n)
                w = take()[:, 0:K * NE].rearrange("p (k n) -> p k n", n=NE)
                for t in range(T):
                    for k in range(K):
                        last = mm(PS[:, 4, t * NE:(t + 1) * NE], HT[:, k, t * P:(t + 1) * P], w[:, k, :], start=(k == 0), stop=(k == K - 1))
                last.then_inc(chunks_done, 1)

                def expert(e, par):
                    for p in range(2):
                        for u in range(2):
                            w = take().rearrange("p (k n) -> p k n", n=256)
                            if u == 0:
                                pe.wait_ge(hidden_ready, 22 * L + l * 2 * NE + e * 2 + p + 1)
                            for c in range(2):
                                for k in range(K):
                                    last = mm(PS[:, 2 * p + u, c * S:(c + 1) * S], w[:, k, c * P:(c + 1) * P], HT[:, k, :],
                                              start=(k == 0), stop=(k == K - 1))
                            last.then_inc(chunks_done, 1)
                    for j in range(2):
                        w = take().rearrange("p (k n) -> p k n", n=D)
                        if j == 0:
                            pe.wait_ge(moe_taken, l * (NE + 1) + e + 1)
                        pe.wait_ge(hidden_ready, 22 * L + l * 2 * NE + e * 2 + j + 3)
                        for k in range(2):
                            for t in range(T):
                                for h in range(2):
                                    last = mm(PS[:, 4 + 2 * t + h, :], EH[:, 2 * j + k, t * P:(t + 1) * P], w[:, k, h * 512:(h + 1) * 512],
                                              start=(j + k == 0), stop=(j + k == 2))
                        last.then_inc(chunks_done, 1)

                with loop(pe, NE // 2, (ring, 12)) as i:
                    for j in range(2):
                        expert(i * 2 + j, j)



        @block.scalar
        def _(act):
            ring = Ring()
            steps = Steps(act, act_step)
            A = nc.scalar.activation

            def chunk():
                ring.next()
                act.wait_ge(chunks_done, ring.done())

            def squares(n, extra=0):
                act.wait_ge(x_ready, n + 1 + extra)
                A(TMP[:, 0, :], X[:, 0, :], ACT.Square, accum_out=SMALL[:, 0:1])
                A(TMP[:, 1, :], X[:, 1, :], ACT.Square, accum_out=SMALL[:, 1:2]).then_inc(squares_ready, 1)

            def ht_copy(n, dst, gains=None, tiles=K):
                for b in (0, 2):
                    act.wait_ge(tr_ready, n * 4 + b + 1)
                    if gains is None or 2 * b >= tiles:
                        A(dst[:, 2 * b:2 * b + 2, :], PS[:, b, :].rearrange("p (k n) -> p k n", k=2), ACT.Copy).then_inc(ht_a, 1)
                    else:
                        A(dst[:, 2 * b, :], PS[:, b, 0:S], ACT.Copy, scale=LV[:, gains + 2 * b:gains + 2 * b + 1])
                        A(dst[:, 2 * b + 1, :], PS[:, b, S:2 * S], ACT.Copy, scale=LV[:, gains + 2 * b + 1:gains + 2 * b + 2]).then_inc(ht_a, 1)

            def silu(index, par):
                chunk()
                act.wait_ge(hidden_ready, index + 1)
                A(SIL[:, par, :], PS[:, 2 * par, :], ACT.Silu).then_inc(silu_ready, 1)
                ring.next()

            def swiglu(l, f, gains):
                squares(st1(l, 2 * f))
                ht_copy(tr1(l, 4 * f), HT, gains)
                with loop(act, 5, (ring, 4)) as i:
                    for j in range(2):
                        silu(l * 22 + f * 11 + i * 2 + j, j)
                silu(l * 22 + f * 11 + 10, 0)
                ring.n += FR

            def project(width, j, par):
                chunk()
                A(PROJ[:, 0, bass.ds(j * width, width)], PS[:, 2 * par, 0:width], ACT.Copy).then_inc(proj_a, 1)

            act.dma_start(X, x_view).then_inc(x_loaded, 16)
            act.sem_inc(proj_a, 2)
            act.sem_inc(ht_a, 2)

            with loop(act, L, (ring, C1), (steps, 1)) as l:
                act.wait_ge(lv_ready, l + 1)
                swiglu(l, 0, V_F1)
                squares(st1(l, 1))
                ht_copy(tr1(l, 1), HT, V_MIX)
                with loop(act, N1 // 4, (ring, 4)) as i:
                    for j in range(4):
                        project(W1, i * 4 + j, j % 2)
                act.wait_ge(proj_a, l * N1 + N1 + 2)
                act.wait_ge(proj_d, l * N1 + N1 + 2)
                for at, c, n in ((0, NQ, 8), (8, WQ, 6), (14, KS, 2), (16, KW, 2)):
                    last = A(QKN[:, :, at:at + n, :].rearrange("p t h d -> p t (h d)"), PROJ[:, :, c:c + n * HD], ACT.Square)
                last.then_inc(head_sq, 1)
                for kv in range(2):
                    for t in range(T):
                        for u in range(2):
                            last = A(KD[:, t, 3 + kv, :, u, :], PROJ[:, t, KC + kv * P:KC + (kv + 1) * P].rearrange("p (g d) -> p g d", g=2), ACT.Copy)
                last.then_inc(keys_copied, 1)
                A(PROJ[:, :, NG:NG + 24], PROJ[:, :, NG:NG + 24], ACT.Sigmoid)
                A(PROJ[:, :, BG:D_IN], PROJ[:, :, BG:D_IN], ACT.Sigmoid).then_inc(gates_ready, 1)
                for b in (0, 2, 4, 6, 8):
                    act.wait_ge(htr_ready, l * 10 + b + 1)
                    scale = {0: LV[:, VL:VL + 1], 2: LV[:, VL + 1:VL + 2], 4: LV[:, V_KN:V_KN + 1], 6: 1.0, 8: HD ** -0.5}[b]
                    A(TT[:, 2 * b:2 * b + 2, :], PS[:, b % 4, :].rearrange("p (k n) -> p k n", k=2), ACT.Copy, scale=scale).then_inc(tt_a, 1)
                for kv in range(2):
                    ring.next()
                    chunk()
                    A(HS[:, kv, :], PS[0:64, 4 + kv, 0:256], ACT.Silu).then_inc(cmp_hidden, 1)
                act.wait_ge(cmp_tr, l + 1)
                A(HST, PS[:, 6, 0:2 * 64].rearrange("p (i n) -> p i n", i=2), ACT.Copy)
                for u in range(2):
                    last = A(HSTV.rearrange("p i (g u) n -> p i g u n", u=2)[:, :, :, u, :],
                             PS[:, 6, 2 * 64:4 * 64].rearrange("p (i g n) -> p i g n", i=2, g=2), ACT.Copy)
                last.then_inc(cmp_trs, 1)
                ring.n += 2
                act.wait_ge(cmp_kt, l + 1)
                A(KCT, PS[:, 6, 256:320], ACT.Copy, scale=LV[:, V_KN:V_KN + 1]).then_inc(cmp_kts, 1)
                act.wait_ge(pc_in, l + 1)
                A(PC[:, :, 0:NCMP], PC[:, :, 0:NCMP], ACT.Exp).then_inc(pc_exp, 1)
                act.wait_ge(pct_ready, l + 1)
                A(PT[:, 1, 0, :], PS[:, 5, :], ACT.Copy).then_inc(pct_taken, 1)

                def exps(u):
                    kind, g, t = UNITS[u]
                    nk = (t + 1) * P
                    c = 16 * (u % 2)
                    act.wait_ge(sc_max, l * NU + u + 1)
                    for s_ in range(4):
                        last = A(PR[:, u % 2, s_, 0:nk], PR[:, u % 2, s_, 0:nk], ACT.Exp, bias=SMALL[:, 208 + c + s_:209 + c + s_],
                                 accum_out=SMALL[:, 212 + c + s_:213 + c + s_])
                    if kind == 2:
                        last = A(SMALL[:, 216 + c:220 + c], SMALL[:, 216 + c:220 + c], ACT.Exp)
                    last.then_inc(exp_ready, 1)

                def copies(u):
                    act.wait_ge(pt_ready, l * NU + u + 1)
                    A(PT[:, u % 2, 0, :], PS[:, 4, :], ACT.Copy).then_inc(pt_a, 1)

                exps(0)
                for u in range(NU):
                    if u + 1 < NU:
                        exps(u + 1)
                    copies(u)
                act.wait_ge(z_ready, l + 1)
                A(ZS, PS[:, 0:4, 0:384], ACT.Copy).then_inc(z_copied, 1)
                act.wait_ge(z_abs, l + 1)
                steps.link(A(EX, EX, ACT.Exp))
                A(EX, EX, ACT.Ln, bias=1.0).then_inc(z_ln, 1)
                act.wait_ge(w_arg, l + 1)
                A(EX, ZS, ACT.Exp).then_inc(w_ready, 1)
                ht_copy(tr1(l, 2), HT)
                ht_copy(tr1(l, 3), HT)
                ring.n += 8
                swiglu(l, 1, V_F2)

            act.wait_ge(x_ready, 3 * L + 1)
            act.dma_start(TMP, a["mem_2"][0].rearrange("(t p) n -> p t n", p=P)).then_inc(mem_loaded, 16)
            ht_copy(5 * L, MEMT)

            with loop(act, L, (ring, C2), (steps, 1)) as l:
                ht_copy(tr2(l, 0), HT)
                with loop(act, N2 // 4, (ring, 4)) as i:
                    for j in range(4):
                        project(W2, i * 4 + j, j % 2)
                for j in range(N2 // 4 * 4, N2):
                    project(W2, j, j % 2)
                chunk()
                act.wait_ge(lv_ready, L + l + 1)
                A(WST[0:64, :, :], PS[0:64, 7, :].rearrange("p (g t) -> p g t", g=4), ACT.Copy)
                A(WST[64:P, :, 64:P], PS[64:P, 7, :].rearrange("p (g t) -> p g t", g=4)[:, :, 64:P], ACT.Copy).then_inc(ws_copied, 1)
                act.wait_ge(ga_ready, l + 1)
                A(AT[0:16, :], PS[0:16, 4, 0:S], ACT.Copy).then_inc(ga_copied, 1)
                A(TT[:, 0:2, :], PS[:, 5, :].rearrange("p (k n) -> p k n", k=2), ACT.Copy, scale=HD ** -0.5).then_inc(ga_copied, 1)
                act.wait_ge(proj_a, L * N1 + l * N2 + N2 + 2)
                act.wait_ge(proj_d, L * N1 + l * N2 + N2 + 2)
                A(PROJ[:, :, SU:D_IN2], PROJ[:, :, SU:D_IN2], ACT.Gelu_apprx_tanh).then_inc(gelu_ready, 1)
                A(PROJ[:, :, GR:GR + 512], PROJ[:, :, GR:GR + 512], ACT.Silu).then_inc(gelu_ready, 1)
                act.wait_ge(sv_centred, l + 1)
                A(TMP[:, :, 512:1024], PROJ[:, :, SV2:SV2 + 512], ACT.Square).then_inc(sv_sq, 1)
                act.wait_ge(gl_abs, l + 1)
                steps.link(A(GX[:, 0:2, 0:S], GX[:, 0:2, 0:S], ACT.Exp))
                A(GX[:, 0:2, 0:S], GX[:, 0:2, 0:S], ACT.Ln, bias=1.0).then_inc(gl_ln, 1)
                act.wait_ge(gl_cum, l + 1)
                A(KEXP, PS[:, 6, :].rearrange("p (t n) -> p t n", t=2), ACT.Exp, scale=-1.0 / 16)
                A(SMALL[:, 200:208], PS[:, 5, 0:8], ACT.Exp, scale=-1.0 / 16).then_inc(gl_exp, 1)
                act.wait_ge(go_ready, l + 1)
                A(TMP[:, :, 0:512].rearrange("p t (r n) -> p r t n", r=2), PS[:, 2:6, 0:256].rearrange("p (r t) n -> p r t n", r=2),
                  ACT.Square).then_inc(go_sq, 1)
                ht_copy(tr2(l, 1), HT, V_GN, 4)
                ring.n += 4
                squares(st2(l, 0), 1)
                ht_copy(tr2(l, 2), HT)
                for j in range(8):
                    if j % 2:
                        ring.next()
                        continue
                    chunk()
                    A(TT[:, 2 * j:2 * j + 2, :], PS[:, 0, :].rearrange("p (k n) -> p k n", k=2), ACT.Copy).then_inc(qk_a, 1)
                for j in range(4):
                    chunk()
                    A(VX[:, 0, j * 256:(j + 1) * 256], PS[:, 2 + 2 * (j % 2), 0:256], ACT.Copy).then_inc(vx_a, 1)
                for t in range(T):
                    act.wait_ge(xm_ready, l * 2 + t + 1)
                    for h in range(4):
                        last = A(PR[:, t, h, :], PS[:, 2 * t + h // 2, (h % 2) * S:(h % 2 + 1) * S], ACT.Exp, scale=1.0 / 16,
                                 bias=SMALL[:, 208 + 16 * t + h:209 + 16 * t + h], accum_out=SMALL[:, 212 + 16 * t + h:213 + 16 * t + h])
                    last.then_inc(xe_ready, 1)
                for t in range(T):
                    act.wait_ge(xt_ready, l * 2 + t + 1)
                    A(PXT[:, 0, :, t * P:(t + 1) * P], PS[:, 4 + 2 * t, :].rearrange("p (h n) -> p h n", h=4), ACT.Copy).then_inc(xt_a, 1)
                for h in (0, 2):
                    act.wait_ge(xo_ready, l * 4 + h + 1)
                    A(HT[:, 2 * h:2 * h + 2, :], PS[:, h, :].rearrange("p (k n) -> p k n", k=2), ACT.Copy).then_inc(xo_a, 1)
                ring.n += 4
                squares(st2(l, 1), 1)
                ht_copy(tr2(l, 3), HT)
                ring.next()
                act.wait_ge(rt_in, l + 1)
                A(SMALL[:, 256:288], SMALL[:, 256:288], ACT.Exp).then_inc(rt_exp, 1)

                def expert(e):
                    for p in range(2):
                        silu(22 * L + l * 2 * NE + e * 2 + p, p)
                    ring.n += 2
                with loop(act, NE // 2, (ring, 12)) as i:
                    for j in range(2):
                        expert(i * 2 + j)
                squares(st2(l, 2), 1)
            act.wait_ge(src_ready, tr2(L, 0) + 1)
            act.dma_start(out_view, X).then_inc(out_stored, 16)
            act.wait_ge(out_stored, 16)

        @block.vector
        def _(dve):
            ring = Ring()
            steps = Steps(dve, dve_step)
            link = steps.link
            V = nc.vector
            TTn, TSc = V.tensor_tensor, V.tensor_scalar
            XF, TMPF, YF = flat(X), flat(TMP), flat(Y)
            LOW = PS[:, 0:4, :].rearrange("p b n -> p (b n)")
            HIGH = PS[:, 4:8, :].rearrange("p b n -> p (b n)")

            def chunk():
                ring.next()
                dve.wait_ge(chunks_done, ring.done())

            def ht_copy(n, dst, gains=None, tiles=K):
                for b in (1, 3):
                    dve.wait_ge(tr_ready, n * 4 + b + 1)
                    if gains is None or 2 * b >= tiles:
                        V.tensor_copy(dst[:, 2 * b:2 * b + 2, :], PS[:, b, :].rearrange("p (k n) -> p k n", k=2)).then_inc(ht_d, 1)
                    else:
                        TSc(dst[:, 2 * b, :], PS[:, b, 0:S], LV[:, gains + 2 * b:gains + 2 * b + 1], None, ALU.mult)
                        TSc(dst[:, 2 * b + 1, :], PS[:, b, S:2 * S], LV[:, gains + 2 * b + 1:gains + 2 * b + 2], None, ALU.mult).then_inc(ht_d, 1)

            def rms_rows(n):
                dve.wait_ge(rstd_ready, n + 1)
                TSc(TMP[:, 0, :], X[:, 0, :], SMALL[:, 4:5], None, ALU.mult)
                TSc(TMP[:, 1, :], X[:, 1, :], SMALL[:, 5:6], None, ALU.mult).then_inc(src_ready, 1)

            def hidden(index, par, dst):
                ring.next()
                dve.wait_ge(silu_ready, index + 1)
                chunk()
                TTn(dst, SIL[:, par, :].rearrange("p (k n) -> p k n", k=2), PS[:, 2 * par + 1, :].rearrange("p (k n) -> p k n", k=2),
                    ALU.mult).then_inc(hidden_ready, 1)

            def swiglu(l, f, gains):
                rms_rows(st1(l, 2 * f))
                ht_copy(tr1(l, 4 * f), HT, gains)
                with loop(dve, 5, (ring, 4)) as i:
                    for j in range(2):
                        hidden(l * 22 + f * 11 + i * 2 + j, j, GT[:, bass.ds(i * 4 + 2 * j, 2), :])
                hidden(l * 22 + f * 11 + 10, 0, GT[:, 20:22, :])
                ring.n += FR - 1
                chunk()
                V.scalar_tensor_tensor(XF, HIGH, 0.5, XF, ALU.mult, ALU.add).then_inc(x_ready, 1)

            def project(width, j, par):
                chunk()
                V.tensor_copy(PROJ[:, 1, bass.ds(j * width, width)], PS[:, 2 * par + 1, 0:width]).then_inc(proj_d, 1)

            def four(x):
                return x.rearrange("p (a b) -> p b a", b=2)

            dve.sem_inc(hidden_ready, 2)
            dve.sem_inc(proj_d, 2)
            dve.sem_inc(ht_d, 2)
            dve.wait_ge(consts_loaded, 16 * NLOAD)
            V.tensor_copy(RBP, RB.rearrange("p (g a b) -> p g b a", g=3, a=2)).then_inc(rb_ready, 1)
            dve.wait_ge(vec_ready, 1)
            V.tensor_copy(VECT, PS[:, 4, 0:L * VL]).then_inc(vec_taken, 1)
            dve.wait_ge(hot_ready, 1)
            V.tensor_copy(VBIAS, PS[0:12, 5, :]).then_inc(bias_row, 1)
            dve.wait_ge(hot_ready, 2)
            for t in range(T):
                for r in range(2):
                    TTn(BIASC[:, r * 8 + t * 4:r * 8 + t * 4 + 4, :],
                        PS[:, 6, t * NCMP * 8:(t + 1) * NCMP * 8].rearrange("p (n h r) -> p r h n", h=4, r=2)[:, r],
                        spread(CON[:, O_MCN + t * NCMP:O_MCN + (t + 1) * NCMP], 1, 4), ALU.add).then_inc(vec_taken, 1)
            dve.wait_ge(hot_ready, 3)
            TTn(BIAS[:, 0:8, :], LOW.rearrange("p (h n) -> p h n", h=8), spread(CON[:, O_MB:O_MB + S], 1, 8), ALU.add).then_inc(vec_taken, 1)
            TTn(BIAS[:, 8:12, :], HIGH[:, 0:4 * S].rearrange("p (h n) -> p h n", h=4), spread(CON[:, O_MS:O_MS + S], 1, 4), ALU.add).then_inc(vec_taken, 1)
            dve.wait_ge(x_loaded, 16)
            dve.sem_inc(x_ready, 1)
            dve.wait_ge(zeroed, 5)
            dve.wait_ge(vec_taken, 5)

            with loop(dve, L, (ring, C1), (steps, DVE1)) as l:
                link(V.tensor_copy(LV[:, 0:VL], VECT[:, bass.ds(l * VL, VL)]))
                V.tensor_copy(SINKL, SINK[:, bass.ds(l, 1), :].rearrange("p o h -> p (o h)"))
                TSc(LV[:, VL:VL + 1], LV[:, V_QN:V_QN + 1], HD ** -0.5, None, ALU.mult)
                link(TSc(LV[:, VL + 1:VL + 2], LV[:, V_WQN:V_WQN + 1], HD ** -0.5, None, ALU.mult))
                dve.sem_inc(lv_ready, 1)
                swiglu(l, 0, V_F1)
                rms_rows(st1(l, 1))
                ht_copy(tr1(l, 1), HT, V_MIX)
                with loop(dve, N1 // 4, (ring, 4)) as i:
                    for j in range(4):
                        project(W1, i * 4 + j, j % 2)
                dve.wait_ge(head_sq, l + 1)
                link(V.tensor_reduce(SMALL[:, 8:44], QKN.rearrange("p t h d -> p (t h) d"), AX.X, ALU.add))
                TSc(SMALL[:, 48:84], SMALL[:, 8:44], 1.0 / HD, 1e-6, ALU.mult, ALU.add).then_inc(head_ms, 1)
                dve.wait_ge(head_rstd, l + 1)
                for t in range(T):
                    r = 96 + 18 * t
                    TTn(QKN[:, t, 0:8, :], PROJ[:, t, NQ:NQ + 512].rearrange("p (h d) -> p h d", d=HD), spread(SMALL[:, r:r + 8], 2, HD), ALU.mult)
                    TTn(QKN[:, t, 8:12, :], PROJ[:, t, WQ:WQ + 256].rearrange("p (h d) -> p h d", d=HD), spread(SMALL[:, r + 8:r + 12], 2, HD), ALU.mult)
                    for kind, c, at in ((0, KS, 14), (1, KW, 16), (2, WK, 12)):
                        for u in range(2):
                            last = TTn(KD[:, t, kind, :, u, :], PROJ[:, t, c:c + P].rearrange("p (h d) -> p h d", d=HD),
                                       spread(SMALL[:, r + at:r + at + 2], 2, HD), ALU.mult)
                last.then_inc(heads_ready, 1)
                for b in (1, 3, 5, 7, 9):
                    dve.wait_ge(htr_ready, l * 10 + b + 1)
                    src = PS[:, b % 4, :].rearrange("p (k n) -> p k n", k=2)
                    scale = {1: LV[:, VL:VL + 1], 3: LV[:, V_KN:V_KN + 1], 5: LV[:, V_WKN:V_WKN + 1]}.get(b)
                    if scale is None:
                        V.tensor_copy(TT[:, 2 * b:2 * b + 2, :], src).then_inc(tt_d, 1)
                    else:
                        TSc(TT[:, 2 * b:2 * b + 2, :], src, scale, None, ALU.mult).then_inc(tt_d, 1)
                dve.wait_ge(tt_a, l * 5 + 5)
                dve.wait_ge(tt_d, l * 5 + 5)
                for kv in range(2):
                    for g in range(2):
                        for par in range(2):
                            q = slice(64 * par, 64 * par + 64)
                            tok = TT[q, 12 + 2 * kv + g, :].rearrange("p (m s) -> p s m", s=16)[:, par::2, :]
                            for half in range(2):
                                last = TTn(BT[q, kv, 8 * half:8 * half + 8, 32 * g:32 * g + NCMP], tok[:, :, half:half + NCMP],
                                           spread(LV[q, V_POS + 8 * half:V_POS + 8 * half + 8], 2, NCMP), ALU.add)
                last.then_inc(blocks_ready, 1)
                ring.n += 4
                chunk()
                link(V.tensor_copy(KCN[:, 0, :], PS[0:64, 7, 0:HD]))
                link(TTn(KCN[:, 1, :], KCN[:, 0, :], KCN[:, 0, :], ALU.mult))
                link(V.tensor_reduce(SMALL[0:64, 139:140], KCN[:, 1, :], AX.X, ALU.add))
                TSc(SMALL[0:64, 140:141], SMALL[0:64, 139:140], 1.0 / HD, 1e-6, ALU.mult, ALU.add).then_inc(cmp_ms, 1)
                chunk()
                for i in range(4):
                    V.tensor_copy(VCB[32 * i:32 * i + 32, i, :], PS[32 * i:32 * i + 32, 5, 0:HD])
                dve.wait_ge(cmp_rstd, l + 1)
                link(TSc(KCN[:, 1, :], KCN[:, 0, :], SMALL[0:64, 141:142], None, ALU.mult))
                V.tensor_copy(KCN[:, 0, :], KCN[:, 1, :]).then_inc(cmp_keys, 1)
                dve.wait_ge(scc_ready, l + 1)
                for r in range(2):
                    last = TTn(PC[:, 8 * r:8 * r + 8, 0:NCMP], PS[:, 4 + 3 * r, 0:256].rearrange("p (h n) -> p h n", n=32)[:, :, 0:NCMP],
                               BIASC[:, 8 * r:8 * r + 8, :], ALU.add)
                link(last)
                link(V.tensor_reduce(SMALL[:, 288:304], PC[:, :, 0:NCMP], AX.X, ALU.max))
                TTn(PC[:, :, 0:NCMP], PC[:, :, 0:NCMP], spread(SMALL[:, 288:304], 2, NCMP), ALU.subtract).then_inc(pc_in, 1)
                dve.wait_ge(pc_exp, l + 1)
                link(V.tensor_reduce(SMALL[:, 304:320], PC[:, :, 0:NCMP], AX.X, ALU.add))
                for r in range(2):
                    for t in range(T):
                        s8 = PC[:, 8 * r + 4 * t:8 * r + 4 * t + 4, 0:NCMP]
                        last = TTn(s8, s8, spread(CON[:, O_MC + t * NCMP:O_MC + (t + 1) * NCMP], 1, 4), ALU.mult)
                last.then_inc(pc_ready, 1)
                link(V.reciprocal(SMALL[:, 320:336], SMALL[:, 304:320]))
                dve.wait_ge(gates_ready, l + 1)
                for t in range(T):
                    last = TTn(SMALL[:, 336:352].rearrange("p (r t h) -> p t r h", r=2, t=2)[:, t],
                               SMALL[:, 320:336].rearrange("p (r t h) -> p t r h", r=2, t=2)[:, t],
                               PROJ[:, t, NG:NG + 8].rearrange("p (h r) -> p r h", r=2), ALU.mult)
                link(last)

                def softmax(u):
                    kind, g, t = UNITS[u]
                    nk = (t + 1) * P
                    c = 16 * (u % 2)
                    n = l * NU + u
                    dve.wait_ge(sc_ready, n + 1)
                    if u >= 2:
                        dve.wait_ge(pt_ready, n - 1)
                    h0 = 4 * g if kind < 2 else 8
                    for r in range(2):
                        last = TTn(PR[:, u % 2, 2 * r:2 * r + 2, 0:nk], PS[:, 2 * (u % 2) + r, :].rearrange("p (h n) -> p h n", h=2)[:, :, 0:nk],
                                   BIAS[:, h0 + 2 * r:h0 + 2 * r + 2, S - nk:S], ALU.add)
                    last.then_inc(sc_taken, 1)
                    dve.wait_ge(sc_taken, n + 1)
                    link(V.tensor_reduce(SMALL[:, 220 + c:224 + c], PR[:, u % 2, :, 0:nk], AX.X, ALU.max))
                    if kind == 2:
                        sink = four(SINKL)
                        mx = SMALL[:, 220 + c:224 + c].rearrange("p (b a) -> p b a", b=2)
                        link(TTn(mx, mx, sink, ALU.max))
                        link(TTn(SMALL[:, 216 + c:220 + c].rearrange("p (b a) -> p b a", b=2), sink, mx, ALU.subtract))
                    TSc(SMALL[:, 208 + c:212 + c], SMALL[:, 220 + c:224 + c], -1.0, None, ALU.mult).then_inc(sc_max, 1)

                def outputs(u):
                    kind, g, t = UNITS[u]
                    c = 16 * (u % 2)
                    dve.wait_ge(exp_ready, l * NU + u + 1)
                    den = SMALL[:, 212 + c:216 + c]
                    if kind == 2:
                        link(TTn(den, den, SMALL[:, 216 + c:220 + c], ALU.add))
                    link(V.reciprocal(COEF[:, u % 2, :], den))
                    if kind < 2:
                        gate = four(PROJ[:, t, NG + 8 * (kind + 1) + 4 * g:NG + 8 * (kind + 1) + 4 * g + 4])
                        co = COEF[:, u % 2, :].rearrange("p (b a) -> p b a", b=2)
                        link(TTn(co, co, gate, ALU.mult))
                    if t:
                        dve.wait_ge(pt_ready, l * NU + u + 1)
                        V.tensor_copy(PT[:, u % 2, 1, :], PS[:, 5, :]).then_inc(pt_d, 1)
                    dve.wait_ge(o_ready, l * NU + u + 1)
                    src = PS[:, 6 + u % 2, 0:256].rearrange("p (a b d) -> p b a d", a=2, b=2)
                    co = spread(COEF[:, u % 2, :].rearrange("p (b a) -> p b a", b=2), 3, HD)
                    if kind == 2:
                        TTn(Y[:, t, 768:1024].rearrange("p (a b d) -> p b a d", a=2, b=2), src, co, ALU.mult).then_inc(o_taken, 1)
                    else:
                        link(TTn(YD.rearrange("p (a b d) -> p b a d", a=2, b=2), src, co, ALU.mult))
                        y = Y[:, t, g * 256:(g + 1) * 256]
                        TTn(y, y, YD, ALU.add).then_inc(o_taken, 1)

                softmax(0)
                dve.wait_ge(oc_ready, l + 1)
                for t in range(T):
                    last = TTn(Y[:, t, 0:512].rearrange("p (h r d) -> p r h d", h=4, r=2), PS[:, 6 + t, :].rearrange("p (r h d) -> p r h d", r=2, h=4),
                               spread(SMALL[:, 336:352].rearrange("p (r t h) -> p t r h", r=2, t=2)[:, t], 3, HD), ALU.mult)
                last.then_inc(o_taken, 1)
                for u in range(NU):
                    if u + 1 < NU:
                        softmax(u + 1)
                    outputs(u)
                dve.wait_ge(z_copied, l + 1)
                V.scalar_tensor_tensor(flat(EX), flat(ZS), -1.0, flat(ZS), ALU.mult, ALU.min).then_inc(z_abs, 1)
                dve.wait_ge(z_ln, l + 1)
                link(V.scalar_tensor_tensor(flat(EX), flat(ZS), 0.0, flat(EX), ALU.max, ALU.add))
                TTn(EX, EX, spread(CON[:, O_SB:O_SB + 384], 1, 4), ALU.mult).then_inc(sp_ready, 1)
                dve.wait_ge(after_ready, l + 1)
                link(TTn(ZS, ZS, PS[:, 4:8, 0:384], ALU.subtract))
                TTn(ZS, ZS, spread(CON[:, O_SBN:O_SBN + 384], 1, 4), ALU.add).then_inc(w_arg, 1)
                dve.wait_ge(osb_ready, l + 1)
                V.tensor_copy(Y[:, :, 512:768], PS[:, 0, :].rearrange("p (t n) -> p t n", t=2)).then_inc(src_ready, 1)
                ht_copy(tr1(l, 2), HT)
                ring.n += 1
                chunk()
                bg = [PROJ[:, :, BG + i * D:BG + (i + 1) * D] for i in range(3)]
                low, high = (x.rearrange("p (t n) -> p t n", t=2) for x in (LOW, HIGH))
                TTn(TMP, low, bg[0], ALU.mult).then_inc(rows_taken, 1)
                chunk()
                link(TTn(Y, high, bg[1], ALU.mult))
                link(TTn(TMPF, TMPF, YF, ALU.add))
                chunk()
                link(TTn(Y, low, bg[2], ALU.mult))
                TTn(YF, TMPF, YF, ALU.add).then_inc(src_ready, 1)
                ht_copy(tr1(l, 3), HT)
                ring.n += 3
                chunk()
                TTn(XF, HIGH, XF, ALU.add).then_inc(x_ready, 1)
                swiglu(l, 1, V_F2)

            dve.wait_ge(x_ready, 3 * L + 1)
            dve.sem_inc(src_ready, 2)
            ht_copy(5 * L, MEMT)

            def layer_norm(l, k):
                link(V.tensor_reduce(SMALL[:, 352:354], X, AX.X, ALU.add))
                link(TSc(SMALL[:, 354:356], SMALL[:, 352:354], -1.0 / D, None, ALU.mult))
                TSc(X[:, 0, :], X[:, 0, :], SMALL[:, 354:355], None, ALU.add)
                TSc(X[:, 1, :], X[:, 1, :], SMALL[:, 355:356], None, ALU.add).then_inc(x_ready, 1)
                dve.wait_ge(lngb_in, (l * 3 + k) * 32 + 32)
                dve.wait_ge(rstd_ready, st2(l, k) + 1)
                for t in range(T):
                    last = V.scalar_tensor_tensor(X[:, t, :], X[:, t, :], SMALL[:, 4 + t:5 + t], LNGB[:, 0, :], ALU.mult, ALU.mult)
                link(last)
                TTn(X, X, spread(LNGB[:, 1, :], 1, T), ALU.add).then_inc(src_ready, 1)

            with loop(dve, L, (ring, C2), (steps, DVE2)) as l:
                link(V.tensor_copy(LV[:, 0:VL], VECT[:, bass.ds(l * VL, VL)]))
                V.memset(WST, 0.0)
                link(V.memset(STATE[:, 0, :, :], 0.0))
                dve.sem_inc(lv_ready, 1)
                ht_copy(tr2(l, 0), HT)
                with loop(dve, N2 // 4, (ring, 4)) as i:
                    for j in range(4):
                        project(W2, i * 4 + j, j % 2)
                for j in range(N2 // 4 * 4, N2):
                    project(W2, j, j % 2)
                ring.next()
                v = PROJ[:, :, SV2:SV2 + 512].rearrange("p t (g c) -> p t g c", g=4)
                dve.wait_ge(gelu_ready, 2 * l + 1)
                link(V.tensor_reduce(SMALL[:, 356:364].rearrange("p (t g) -> p t g", t=2), v, AX.X, ALU.add))
                link(TSc(SMALL[:, 364:372], SMALL[:, 356:364], -1.0 / P, None, ALU.mult))
                for t in range(T):
                    last = TTn(v[:, t], v[:, t], spread(SMALL[:, 364 + 4 * t:368 + 4 * t], 2, P), ALU.add)
                last.then_inc(sv_centred, 1)
                dve.wait_ge(gl_ready, l + 1)
                x = PS[:, 4, :].rearrange("p (t n) -> p t n", t=2)
                link(TSc(GX[:, 2:4, 0:S], x, -1.0, 0.0, ALU.mult, ALU.max))
                V.scalar_tensor_tensor(GX[:, 0:2, 0:S], GX[:, 2:4, 0:S], -2.0, x, ALU.mult, ALU.subtract).then_inc(gl_abs, 1)
                dve.wait_ge(gl_ln, l + 1)
                TTn(GX[:, 0:2, 0:S], GX[:, 0:2, 0:S], GX[:, 2:4, 0:S], ALU.add).then_inc(gl_sp, 1)
                dve.wait_ge(gl_exp, l + 1)
                TTn(KDEC, PROJ[:, :, GK:GK + 256], KEXP, ALU.mult).then_inc(kdec_ready, 1)
                for c in range(4):
                    dve.wait_ge(kv_ready, l * 4 + c + 1)
                    if c:
                        dve.wait_ge(state_ready, l * 4 + c)
                    for hp in range(2):
                        last = V.scalar_tensor_tensor(STATE[:, c + 1, hp, :], STATE[:, c, hp, :], SMALL[:, 200 + hp * 4 + c:201 + hp * 4 + c],
                                                      PS[:, c % 2, hp * P:(hp + 1) * P], ALU.mult, ALU.add)
                    last.then_inc(state_ready, 1)
                dve.wait_ge(sv_sq, l + 1)
                V.tensor_reduce(SMALL[:, 152:160].rearrange("p (t g) -> p t g", t=2), TMP[:, :, 512:1024].rearrange("p t (g c) -> p t g c", g=4), AX.X, ALU.add)
                dve.wait_ge(go_sq, l + 1)
                link(V.tensor_reduce(SMALL[:, 144:152].rearrange("p (t g) -> p t g", t=2), TMP[:, :, 0:512].rearrange("p t (g c) -> p t g c", g=4), AX.X, ALU.add))
                TSc(SMALL[:, 160:168], SMALL[:, 144:152], 1.0 / P, 1e-6, ALU.mult, ALU.add)
                TSc(SMALL[:, 168:176], SMALL[:, 152:160], 1.0 / P, 1e-5, ALU.mult, ALU.add).then_inc(gs_ms, 1)
                dve.wait_ge(gs_rstd, l + 1)
                for t in range(T):
                    last = TTn(Y[:, t, 0:512].rearrange("p (h r c) -> p r h c", h=2, r=2),
                               PS[:, 2:6, 0:256].rearrange("p (r t) (h c) -> p t r h c", r=2, h=2)[:, t],
                               spread(SMALL[:, 176 + 4 * t:180 + 4 * t].rearrange("p (r h) -> p r h", r=2), 3, P), ALU.mult)
                link(last)
                dve.wait_ge(gelu_ready, 2 * l + 2)
                TTn(Y[:, :, 0:512], Y[:, :, 0:512], PROJ[:, :, GR:GR + 512], ALU.mult)
                for t in range(T):
                    last = TTn(v[:, t], v[:, t], spread(SMALL[:, 184 + 4 * t:188 + 4 * t], 2, P), ALU.mult)
                link(last)
                dve.wait_ge(layer_in, l * 64 + 64)
                vv = PROJ[:, :, SV2:SV2 + 512]
                link(TTn(vv, vv, spread(SGB[:, 0, :], 1, T), ALU.mult))
                TTn(vv, vv, spread(SGB[:, 1, :], 1, T), ALU.add).then_inc(vn_ready, 1)
                dve.wait_ge(mix_ready, l + 1)
                for t in range(T):
                    for g in range(4):
                        last = V.scalar_tensor_tensor(Y[:, t, 512 + g * P:512 + (g + 1) * P], PS[:, 4 + t, g * P:(g + 1) * P], LV[:, V_BS + g:V_BS + g + 1],
                                                      PROJ[:, t, SU + g * P:SU + (g + 1) * P], ALU.add, ALU.mult)
                last.then_inc(src_ready, 1)
                ht_copy(tr2(l, 1), HT, V_GN, 4)
                ring.n += 3
                chunk()
                link(V.scalar_tensor_tensor(XF, XF, ALPHA, HIGH, ALU.mult, ALU.add))
                layer_norm(l, 0)
                ht_copy(tr2(l, 2), HT)
                for j in range(8):
                    if j % 2 == 0:
                        ring.next()
                        continue
                    chunk()
                    V.tensor_copy(TT[:, 2 * j:2 * j + 2, :], PS[:, 1, :].rearrange("p (k n) -> p k n", k=2)).then_inc(qk_d, 1)
                for j in range(4):
                    chunk()
                    V.tensor_copy(VX[:, 1, j * 256:(j + 1) * 256], PS[:, 3 + 2 * (j % 2), 0:256]).then_inc(vx_d, 1)
                for t in range(T):
                    c = 16 * t
                    dve.wait_ge(xs_ready, l * 2 + t + 1)
                    link(V.tensor_reduce(SMALL[:, 220 + c:224 + c], PS[:, 2 * t:2 * t + 2, :].rearrange("p b n -> p (b n)").rearrange("p (h n) -> p h n", h=4), AX.X, ALU.max))
                    TSc(SMALL[:, 208 + c:212 + c], SMALL[:, 220 + c:224 + c], -1.0 / 16, None, ALU.mult).then_inc(xm_ready, 1)
                for t in range(T):
                    c = 16 * t
                    dve.wait_ge(xe_ready, l * 2 + t + 1)
                    link(V.reciprocal(COEF[:, t, :], SMALL[:, 212 + c:216 + c]))
                    for h in range(4):
                        last = TSc(PR[:, t, h, :], PR[:, t, h, :], COEF[:, t, h:h + 1], None, ALU.mult)
                    last.then_inc(xp_ready, 1)
                for t in range(T):
                    dve.wait_ge(xt_ready, l * 2 + t + 1)
                    V.tensor_copy(PXT[:, 1, :, t * P:(t + 1) * P], PS[:, 5 + 2 * t, :].rearrange("p (h n) -> p h n", h=4)).then_inc(xt_d, 1)
                for h in (1, 3):
                    dve.wait_ge(xo_ready, l * 4 + h + 1)
                    V.tensor_copy(HT[:, 2 * h:2 * h + 2, :], PS[:, h, :].rearrange("p (k n) -> p k n", k=2)).then_inc(xo_d, 1)
                ring.n += 3
                chunk()
                link(V.scalar_tensor_tensor(XF, XF, ALPHA, HIGH, ALU.mult, ALU.add))
                layer_norm(l, 1)
                ht_copy(tr2(l, 3), HT)
                chunk()
                R = SMALL[:, 256:288]
                r3 = R.rearrange("p (t n) -> p t n", t=2)
                TTn(r3, PS[:, 4, 0:32].rearrange("p (t n) -> p t n", t=2), spread(BR, 1, T), ALU.add).then_inc(moe_taken, 1)
                dve.wait_ge(moe_taken, l * (NE + 1) + 1)
                link(V.tensor_reduce(SMALL[:, 372:374], r3, AX.X, ALU.max))
                TTn(r3, r3, spread(SMALL[:, 372:374], 2, NE), ALU.subtract).then_inc(rt_in, 1)
                V.memset(RTN, 0.0)
                dve.wait_ge(rt_exp, l + 1)
                link(V.tensor_reduce(SMALL[:, 374:376], r3, AX.X, ALU.add))
                link(V.reciprocal(SMALL[:, 376:378], SMALL[:, 374:376]))
                link(TTn(r3, r3, spread(SMALL[:, 376:378], 2, NE), ALU.mult))
                r4 = R.rearrange("p (g i) -> p g i", i=4)
                cmp = RTC.rearrange("p (g i j) -> p g i j", i=4, j=4)
                for j in range(4):
                    other = bass.AP(tensor=r4.tensor, offset=r4[:, :, j:j + 1].offset, ap=[*r4[:, :, j:j + 1].ap[:2], [0, j + 1]])
                    last = TTn(cmp[:, :, 0:j + 1, j], other, r4[:, :, 0:j + 1], ALU.is_gt)
                    if j < 3:
                        other = bass.AP(tensor=r4.tensor, offset=other.offset, ap=[*r4[:, :, j:j + 1].ap[:2], [0, 3 - j]])
                        last = TTn(cmp[:, :, j + 1:4, j], other, r4[:, :, j + 1:4], ALU.is_ge)
                link(last)
                link(V.tensor_reduce(SMALL[:, 384:416], RTC.rearrange("p (n j) -> p n j", j=4), AX.X, ALU.add))
                link(V.scalar_tensor_tensor(SMALL[:, 416:448], SMALL[:, 384:416], 1.5, R, ALU.is_lt, ALU.mult))
                link(V.tensor_reduce(SMALL[:, 448:456], SMALL[:, 416:448].rearrange("p (g i) -> p g i", i=4), AX.X, ALU.add))
                gs = SMALL[:, 448:456].rearrange("p (t g) -> p t g", t=2)
                link(V.tensor_reduce(SMALL[:, 456:458], gs, AX.X, ALU.max))
                eq = SMALL[:, 460:468].rearrange("p (t g) -> p t g", t=2)
                link(TTn(eq, gs, spread(SMALL[:, 456:458], 2, 4), ALU.is_equal))
                before = RTN.rearrange("p (t g) -> p t g", t=2)
                for g in range(1, 4):
                    link(TTn(before[:, :, g], before[:, :, g - 1], eq[:, :, g - 1], ALU.add))
                link(V.scalar_tensor_tensor(SMALL[:, 468:476], RTN, 0.5, SMALL[:, 460:468], ALU.is_lt, ALU.mult))
                link(V.reciprocal(SMALL[:, 458:460], SMALL[:, 456:458]))
                link(TTn(SMALL[:, 468:476].rearrange("p (t g) -> p t g", t=2), SMALL[:, 468:476].rearrange("p (t g) -> p t g", t=2),
                         spread(SMALL[:, 458:460], 2, 4), ALU.mult))
                for t in range(T):
                    TTn(GATE[:, :, t].rearrange("p (g i) -> p g i", i=4), SMALL[:, 416 + 16 * t:432 + 16 * t].rearrange("p (g i) -> p g i", i=4),
                        spread(SMALL[:, 468 + 4 * t:472 + 4 * t], 2, 4), ALU.mult)
                V.memset(TMP, 0.0).then_inc(dve_step, 1)
                steps.n += 1
                wait_apart(dve, dve_step, steps.v + steps.n, consts_loaded, 16 * NLOAD)

                def expert(e, j):
                    for p in range(2):
                        hidden(22 * L + l * 2 * NE + e * 2 + p, p, EH[:, 2 * p:2 * p + 2, :])
                    ring.next()
                    chunk()
                    for t in range(T):
                        last = V.scalar_tensor_tensor(TMP[:, t, :], PS[:, 4 + 2 * t:6 + 2 * t, :].rearrange("p b n -> p (b n)"), GCUR[:, 2 * j + t:2 * j + t + 1],
                                                      TMP[:, t, :], ALU.mult, ALU.add)
                    last.then_inc(moe_taken, 1)
                    dve.wait_ge(moe_taken, l * (NE + 1) + e + 2)

                with loop(dve, NE // 2, (ring, 12), (steps, 1)) as i:
                    link(V.tensor_copy(GCUR, GATE[:, bass.ds(i * 2, 2), :].rearrange("p e t -> p (e t)")))
                    for j in range(2):
                        expert(i * 2 + j, j)
                link(V.scalar_tensor_tensor(XF, XF, ALPHA, TMPF, ALU.mult, ALU.add))
                layer_norm(l, 2)


def t5_bucket(dist):
    d = np.maximum(dist, 0)
    df = np.maximum(d, 1).astype(np.float32)
    large = 16 + (np.log(df / np.float32(16)) / np.float32(math.log(8)) * np.float32(16)).astype(np.int32)
    return np.where(d < 16, d, np.minimum(large, 31))


def constants():
    con = np.zeros((P, CONW), np.float32)
    i = np.arange(P)[:, None]
    neg = np.float32(-1e30)
    con[:, O_ID:O_ID + P] = np.eye(P)
    j = np.arange(S)[None, :]
    dist = P + i - j
    con[:, O_MB:O_MB + S] = np.where(dist >= 0, 0, neg)
    con[:, O_MS:O_MS + S] = np.where((dist >= 0) & (dist < P), 0, neg)
    for t in range(T):
        ok = t * P + i - (16 * np.arange(NCMP)[None, :] + 31) >= 0
        con[:, O_MC + t * NCMP:O_MC + (t + 1) * NCMP] = ok
        con[:, O_MCN + t * NCMP:O_MCN + (t + 1) * NCMP] = np.where(ok, 0, neg)
    q = np.concatenate([np.arange(S), np.arange(P)])[None, :]
    con[:, O_SB:O_SB + 384] = i < q
    con[:, O_SBN:O_SBN + 384] = np.where(i < q, 0, neg)
    c = np.arange(P)[None, :]
    con[:, O_U:O_U + P] = i >= c
    con[:, O_ONE:O_ONE + P] = 1
    con[:, O_REV:O_REV + P] = (i > c) & (i // 64 == c // 64)
    con[:, O_CHO:O_CHO + 2] = i // 64 == np.arange(2)[None, :]
    con[:, O_FLIP:O_FLIP + P] = np.eye(P)[::-1]
    b = np.arange(32)[:, None]
    w = np.arange(512)[None, :]
    hot_rev = (t5_bucket(383 - w) == b).astype(np.float32)
    hot = (t5_bucket(w - 256) == b).astype(np.float32)
    return con, hot_rev, hot


def kernel(**inputs):
    import concourse.bacc as bacc
    from concourse.bass_utils import run_bass_kernel_spmd as run

    nc = bacc.Bacc("TRN2", target_bir_lowering=False, num_devices=1)
    arrays = {n: np.ascontiguousarray(x) for n, x in inputs.items()}
    for n, x in zip(("con", "hot_rev", "hot"), constants()):
        arrays[n] = x
    aps = {n: nc.dram_tensor(n, x.shape, F32, kind="ExternalInput").ap() for n, x in arrays.items()}
    out = nc.dram_tensor("out", (1, S, D), F32, kind="ExternalOutput").ap()
    scratch = nc.dram_tensor("bias_scratch", (12, 512), F32, kind="Internal").ap()
    build(nc, aps, out, aps["con"], aps["hot_rev"], aps["hot"], scratch)
    r = run(nc, [arrays], core_ids=[0])
    return r.results[0]["out"]
```

```python
import math
from contextlib import ExitStack, contextmanager

import numpy as np

import concourse.bass as bass
from concourse import mybir

F32 = mybir.dt.float32
F32R = mybir.dt.float32r
ALU = mybir.AluOpType
ACT = mybir.ActivationFunctionType
AX = mybir.AxisListType

P = 128
S = 256
T = S // P
D = 1024
K = D // P
L = 2
F = 2816
FP = F // 256
FR = F // 256
HD = 64
D_IN = 5656
W1 = 202
N1 = D_IN // W1
D_IN2 = 2576
W2 = 184
N2 = D_IN2 // W2
SLOTS = 4
SLOT = 2048
NE = 16
DE = 512
NG_ = 4
EG = NE // NG_
NCMP = 15
(NQ, KC, VC, KS, VS, KW, VW, NG, SQ_, SK_, SV_, WQ, WK, WV, BG) = (
    0, 512, 640, 768, 896, 1024, 1152, 1280, 1304, 1560, 1816, 2072, 2328, 2456, 2584)
GQ, GK, GV, GR, GA, SU, SV2 = 0, 256, 512, 1024, 1536, 1552, 2064
ALPHA = (2.0 * L) ** 0.25
C1 = (FP * 2 + FR) * 2 + N1 + 4 + 2 + 4 + 4
C2 = N2 + 4 + 16 + 6 * NE + 2
S1 = C1 - 6
S2 = C2 - 1
V_F1, V_MIX, V_F2, V_POS, V_QN, V_KN, V_WQN, V_WKN, V_GN, V_BS = 0, 8, 16, 24, 40, 41, 42, 43, 44, 48
VL = 52
(O_ID, O_MB, O_MS, O_MC, O_MCN, O_SB, O_SBN, O_U, O_ONE, O_REV, O_CHO, O_FLIP, O_NTH) = (
    0, 128, 384, 640, 670, 700, 1084, 1468, 1596, 1724, 1852, 1854, 1982)
CONW = 2110
DVE1, DVE2 = 103, 115
NVEC = 3 + 1 + 8 + 2
NLOAD = 1 + NVEC + 5
UNITS = [(2, 0, 0), (2, 0, 1)] + [(k, g, t) for k in range(2) for g in range(2) for t in range(T)]
NU = len(UNITS)


def both(u):
    return sum(t for _, _, t in UNITS[:u])



class Ring:

    def __init__(self):
        self.v, self.n = 0, 0

    def next(self):
        self.n += 1
        return (self.n - 1) % SLOTS

    def full(self):
        return self.v * (16 // SLOTS) + 16 * ((self.n - 1) // SLOTS + 1)

    def done(self):
        return self.v + SLOTS + self.n


class Count:

    def __init__(self):
        self.v, self.n = 0, 0


class Steps:

    def __init__(self, eng, sem):
        self.eng, self.sem, self.v, self.n = eng, sem, 0, 0

    def link(self, ins):
        ins.then_inc(self.sem, 1)
        self.n += 1
        self.eng.wait_ge(self.sem, self.v + self.n)


def wait_apart(eng, sem, value, held, least):
    value = eng.compute_val(value)
    eng.wait_ge(held, least)
    eng.wait_ge(sem, value)


@contextmanager
def loop(eng, count, *counters):
    before = [(c.v, c.n) for c, _ in counters]
    with eng.Fori(0, count) as i:
        for (c, per), (v, n) in zip(counters, before):
            c.v = v + i * per
        yield i
        for (c, per), (v, n) in zip(counters, before):
            assert c.n - n == per, f"a turn has {c.n - n} steps, not {per}"
    for (c, per), (v, n) in zip(counters, before):
        c.v, c.n = v, n + count * per


def build(nc, a, out, con, hot_rev, hot, scratch):
    ctx = ExitStack()
    with ctx:
        def sb(name, shape, dtype=F32):
            return ctx.enter_context(nc.sbuf_tensor(name, shape, dtype))[:]

        def over(name, shape, at):
            return nc.alloc_sbuf_tensor_at(name, shape, F32R, offset=at).ap()

        def sem(name):
            return ctx.enter_context(nc.semaphore(name))

        CON = sb("CON", [P, CONW])
        IDENT = CON[:, O_ID:O_ID + P]
        X = sb("X", [P, T, D])
        TMP = sb("TMP", [P, T, D])
        HTH = sb("HTH", [P, K, S], F32R)
        HTL = sb("HTL", [P, K, S], F32R)
        at_ring = nc.sbuf_base
        RINGS = sb("RINGS", [P, SLOTS, SLOT])
        at_proj = nc.sbuf_base
        PROJ = sb("PROJ", [P, T, D_IN])
        TT = sb("TT", [P, 20, S])
        QKN = sb("QKN", [P, T, 18, HD])
        KD = sb("KD", [P, T, 5, 2, 2, HD])
        BIAS = sb("BIAS", [P, 12, S])
        BIASC = sb("BIASC", [P, 16, NCMP])
        at_pr = nc.sbuf_base
        PR = sb("PR", [P, 2, 4, S])
        PT = sb("PT", [P, 2, 2, 512])
        Y = sb("Y", [P, T, D])
        LV = sb("LV", [P, VL + 2])
        VECT = sb("VECT", [P, L * VL])
        VEC = sb("VEC", [L * VL, P])
        HS = sb("HS", [64, 2, 256])
        HST = sb("HST", [P, 2, 64])
        HSTV = sb("HSTV", [P, 2, 4, 32])
        KCN = sb("KCN", [64, 2, HD])
        KCT = sb("KCT", [P, 64])
        VCB = sb("VCB", [P, 4, HD])
        PC = sb("PC", [P, 16, 32])
        SMALL = sb("SMALL", [P, 512])
        SINK = sb("SINK", [P, L, 4])
        NEGH = sb("NEGH", [P, 64])
        WAB = sb("WAB", [17, S])
        AT = sb("AT", [32, S])
        BR = sb("BR", [P, NE])
        GATE = sb("GATE", [P, NE, T])
        GCUR = sb("GCUR", [P, 4])
        GSEAT = sb("GSEAT", [P, NE])
        CROWDED = ctx.enter_context(nc.sbuf_tensor("CROWDED", [P, 1], mybir.dt.int32))[:]
        COEF = sb("COEF", [P, 2, 4])
        SINKL = sb("SINKL", [P, 4])
        YD = sb("YD", [P, 256])
        RTN = sb("RTN", [P, 8])
        RTC = sb("RTC", [P, 128])
        RB = sb("RB", [32, 12])
        RBP = sb("RBP", [32, 3, 2, 2])

        def flat(x):
            return x.rearrange("p t n -> p (t n)")

        SEAT = flat(PROJ)[:, 0:1024].rearrange("p (g t n) -> p g t n", g=NG_, t=T)
        SEATT = flat(TMP)[:, 0:1024].rearrange("p (g t n) -> p g t n", g=NG_, t=T)
        XSEAT = flat(TMP)[:, 1024:2048].rearrange("p (k n) -> p k n", n=P)
        YSEAT = flat(PROJ)[:, 1024:1024 + NG_ * D]
        PROJ2 = flat(PROJ)[:, 0:T * D_IN2].rearrange("p (t n) -> p t n", t=T)
        RH = over("RH", [P, 2, SLOT], at_pr)
        RL = over("RL", [P, SLOTS, SLOT], at_ring)
        GH, GL = (over(n, [P, 22, S], at_proj + 4 * i * 22 * S) for i, n in enumerate(("GH", "GL")))
        MEMH, MEML = (over(n, [P, K, S], at_proj + 4 * (T * D_IN2 + i * K * S)) for i, n in enumerate(("MEMH", "MEML")))
        EHH, EHL = (over(n, [P, 4, S], at_proj + 4 * (T * D_IN2 + 2 * K * S + i * 4 * S)) for i, n in enumerate(("EHH", "EHL")))
        HT, GT, MEMT, EH = (HTH, HTL), (GH, GL), (MEMH, MEML), (EHH, EHL)
        BTF = flat(KD.rearrange("p t a b c d -> p t (a b c d)"))[:, 0:2048]
        BT = BTF.rearrange("p (a r n) -> p a r n", a=2, r=16)
        HOTR = flat(PROJ)[0:32, 0:512]
        HOT = flat(PROJ)[0:32, 512:1024]
        VBIAS = flat(PROJ)[0:12, 1024:1536]
        BFLIP = flat(PROJ)[:, 2048:2048 + 12 * S].rearrange("p (h n) -> p h n", h=12)
        SIL = flat(Y)[:, 0:1024].rearrange("p (a n) -> p a n", a=2)
        HIDDEN = flat(Y)[:, 1024:2048].rearrange("p (a k n) -> p a k n", a=2, k=2)
        EX = flat(TMP)[:, 0:1536].rearrange("p (h n) -> p h n", h=4)
        GX = PR.rearrange("p u h n -> p (u h n)")[:, 0:1024].rearrange("p (h n) -> p h n", h=4)
        ZS = PR.rearrange("p u h n -> p (u h n)")[:, 0:1536].rearrange("p (h n) -> p h n", h=4)
        LNGB = flat(BIAS)[:, 0:2 * D].rearrange("p (g n) -> p g n", g=2)
        SGB = flat(BIAS)[:, 2 * D:2 * D + 1024].rearrange("p (g n) -> p g n", g=2)
        STATE = BTF[:, 0:1280].rearrange("p (c h v) -> p c h v", c=5, h=2)
        WST = BTF[:, 1280:1792].rearrange("p (g t) -> p g t", g=4)
        VX = flat(PROJ)[:, 0:2048].rearrange("p (t n) -> p t n", t=2)
        PXT = flat(PROJ)[:, 2048:4096].rearrange("p (b h n) -> p b h n", b=2, h=4)
        KDEC = QKN[:, :, 0:4, :].rearrange("p t h d -> p t (h d)")
        KEXP = QKN[:, :, 4:8, :].rearrange("p t h d -> p t (h d)")

        OH = SMALL[:, 476:484].rearrange("p (t g) -> p t g", t=T)

        def spread(ap, at, n):
            return bass.AP(tensor=ap.tensor, offset=ap.offset, ap=[*ap.ap[:at], [0, n], *ap.ap[at:]])

        PS = ctx.enter_context(nc.psum_tensor("PS", [P, 8, 512], F32))[:]

        ring_full = [sem(f"ring_full{i}") for i in range(SLOTS)]
        chunks_done = sem("chunks_done")
        consts_loaded = sem("consts_loaded")
        vectors_loaded = sem("vectors_loaded")
        x_loaded = sem("x_loaded")
        mem_loaded = sem("mem_loaded")
        bias_row = sem("bias_row")
        rb_ready = sem("rb_ready")
        bias_stored = sem("bias_stored")
        bias_loaded = sem("bias_loaded")
        hot_ready = sem("hot_ready")
        vec_ready = sem("vec_ready")
        vec_taken = sem("vec_taken")
        lv_ready = sem("lv_ready")
        zeroed = sem("zeroed")
        x_ready = sem("x_ready")
        squares_ready = sem("squares_ready")
        rstd_ready = sem("rstd_ready")
        src_ready = sem("src_ready")
        tr_ready = sem("tr_ready")
        wh_ready = sem("wh_ready")
        wl_ready = sem("wl_ready")
        ht_h = sem("ht_h")
        ht_l = sem("ht_l")
        silu_ready = sem("silu_ready")
        hidden_ready = sem("hidden_ready")
        proj_a = sem("proj_a")
        proj_d = sem("proj_d")
        head_sq = sem("head_sq")
        head_ms = sem("head_ms")
        head_rstd = sem("head_rstd")
        gates_ready = sem("gates_ready")
        heads_ready = sem("heads_ready")
        keys_copied = sem("keys_copied")
        htr_ready = sem("htr_ready")
        tt_a = sem("tt_a")
        tt_d = sem("tt_d")
        blocks_ready = sem("blocks_ready")
        cmp_hidden = sem("cmp_hidden")
        cmp_tr = sem("cmp_tr")
        cmp_trs = sem("cmp_trs")
        cmp_ms = sem("cmp_ms")
        cmp_rstd = sem("cmp_rstd")
        cmp_keys = sem("cmp_keys")
        cmp_kt = sem("cmp_kt")
        cmp_kts = sem("cmp_kts")
        scc_ready = sem("scc_ready")
        pc_in = sem("pc_in")
        pc_exp = sem("pc_exp")
        pc_ready = sem("pc_ready")
        pct_ready = sem("pct_ready")
        pct_taken = sem("pct_taken")
        oc_ready = sem("oc_ready")
        sc_ready = sem("sc_ready")
        sc_taken = sem("sc_taken")
        sc_max = sem("sc_max")
        exp_ready = sem("exp_ready")
        pt_ready = sem("pt_ready")
        pt_a = sem("pt_a")
        pt_d = sem("pt_d")
        o_ready = sem("o_ready")
        o_taken = sem("o_taken")
        z_ready = sem("z_ready")
        z_copied = sem("z_copied")
        z_abs = sem("z_abs")
        z_ln = sem("z_ln")
        sp_ready = sem("sp_ready")
        after_ready = sem("after_ready")
        w_arg = sem("w_arg")
        w_ready = sem("w_ready")
        osb_ready = sem("osb_ready")
        rows_taken = sem("rows_taken")
        ga_ready = sem("ga_ready")
        ga_copied = sem("ga_copied")
        gl_ready = sem("gl_ready")
        gl_abs = sem("gl_abs")
        gl_ln = sem("gl_ln")
        gl_sp = sem("gl_sp")
        gl_cum = sem("gl_cum")
        gl_exp = sem("gl_exp")
        kdec_ready = sem("kdec_ready")
        kv_ready = sem("kv_ready")
        state_ready = sem("state_ready")
        go_ready = sem("go_ready")
        go_sq = sem("go_sq")
        gs_ms = sem("gs_ms")
        gs_rstd = sem("gs_rstd")
        gelu_ready = sem("gelu_ready")
        sv_centred = sem("sv_centred")
        sv_sq = sem("sv_sq")
        vn_ready = sem("vn_ready")
        mix_ready = sem("mix_ready")
        layer_in = sem("layer_in")
        ws_copied = sem("ws_copied")
        lngb_in = sem("lngb_in")
        qk_a = sem("qk_a")
        qk_d = sem("qk_d")
        vx_a = sem("vx_a")
        vx_d = sem("vx_d")
        xs_ready = sem("xs_ready")
        xm_ready = sem("xm_ready")
        xe_ready = sem("xe_ready")
        xp_ready = sem("xp_ready")
        xt_ready = sem("xt_ready")
        xt_a = sem("xt_a")
        xt_d = sem("xt_d")
        xo_ready = sem("xo_ready")
        xo_h = sem("xo_h")
        xo_l = sem("xo_l")
        rt_in = sem("rt_in")
        rt_exp = sem("rt_exp")
        moe_taken = sem("moe_taken")
        oh_ready = sem("oh_ready")
        pos_ready = sem("pos_ready")
        crowd_known = sem("crowd_known")
        seat_ready = sem("seat_ready")
        seat_tr = sem("seat_tr")
        seat_taken = sem("seat_taken")
        gather_ready = sem("gather_ready")
        seat_a = sem("seat_a")
        seat_d = sem("seat_d")
        scatter_ready = sem("scatter_ready")
        moe_summed = sem("moe_summed")
        out_stored = sem("out_stored")
        act_step = sem("act_step")
        dve_step = sem("dve_step")
        pool_step = sem("pool_step")

        def tr1(l, k):
            return l * 5 + k

        def tr2(l, k):
            return 1 + 5 * L + l * 4 + k

        def st1(l, k):
            return l * 3 + k

        def st2(l, k):
            return 3 * L + l * 3 + k

        x_view = a["x"][0].rearrange("(t p) n -> p t n", p=P)
        out_view = out[0].rearrange("(t p) n -> p t n", p=P)

        def load_vectors(eng, l, loaded):
            nload, b = 0, l * VL
            for name, at, n in (("ffn1_norm", V_F1, 8), ("mix_norm", V_MIX, 8), ("ffn2_norm", V_F2, 8)):
                eng.dma_start(VEC[b + at:b + at + n, :], a[name][l].rearrange("(k p) -> k p", p=P)).then_inc(loaded, 16)
                nload += 1
            eng.dma_start(VEC[b + V_POS:b + V_POS + 16, :],
                          a["nsa_cmp_pos"][l].rearrange("(r q) d -> r (q d)", q=2)).then_inc(loaded, 16)
            nload += 1
            for name, at in (("nsa_q_norm", V_QN), ("nsa_k_norm", V_KN), ("swa_q_norm", V_WQN), ("swa_k_norm", V_WKN)):
                for h in range(2):
                    eng.dma_start(VEC[b + at:b + at + 1, h * HD:(h + 1) * HD], a[name][l:l + 1, :]).then_inc(loaded, 16)
                    nload += 1
            eng.dma_start(VEC[b + V_GN:b + V_GN + 4, :], a["gla_norm_g_2"][l].rearrange("(k p) -> k p", p=P)).then_inc(loaded, 16)
            eng.dma_start(VEC[b + V_BS:b + V_BS + 4, :], a["b_s_2"][l]).then_inc(loaded, 16)
            nload += 2
            return nload

        block = ctx.enter_context(nc.Block())

        @block.sync
        def _(sp):
            ring = Ring()

            def load(src, shape_fn):
                slot = ring.next()
                sp.wait_ge(chunks_done, ring.v + ring.n)
                sp.dma_start(shape_fn(RINGS[:, slot, :]), src).then_inc(ring_full[slot], 16)

            def cols(w, l, c0, n):
                src = w[l].rearrange("(k p) n -> p k n", p=P)[:, :, bass.ds(c0, n)]
                load(src, lambda r: r[:, 0:src.shape[1] * n].rearrange("p (k n) -> p k n", n=n))

            def rows(w, l, r0, n=D):
                src = w[l, bass.ds(r0, 2 * P), :].rearrange("(k p) n -> p k n", p=P)
                load(src, lambda r: r[:, 0:2 * n].rearrange("p (k n) -> p k n", n=n))

            def many(count, fn, per=1):
                unit = SLOTS // math.gcd(SLOTS, per)
                whole = count // unit
                if whole > 1:
                    with loop(sp, whole, (ring, unit * per)) as i:
                        for j in range(unit):
                            fn(i * unit + j)
                    left = whole * unit
                else:
                    left = 0
                for j in range(left, count):
                    fn(j)

            def swiglu(l, n):
                def pair(j):
                    cols(a[n + "_w_gate"], l, j * 256, 256)
                    cols(a[n + "_w_up"], l, j * 256, 256)
                many(FP, pair, 2)
                many(FR, lambda j: rows(a[n + "_w_down"], l, j * 256))

            with loop(sp, L, (ring, C1)) as l:
                swiglu(l, "ffn1")
                many(N1, lambda j: cols(a["w_in"], l, j * W1, W1))
                for kv in ("k", "v"):
                    for i in range(2):
                        src = a[f"nsa_cmp_{kv}_w1"][l, i * 1024:(i + 1) * 1024, :].rearrange("(k p) n -> p k n", p=P)
                        load(src, lambda r: r.rearrange("p (k n) -> p k n", n=256))
                for kv in ("k", "v"):
                    src = a[f"nsa_cmp_{kv}_w2"][l].rearrange("(k p) n -> p k n", p=P)
                    load(src, lambda r: r[:, 0:2 * HD].rearrange("p (k n) -> p k n", n=HD))
                rows(a["w_up_nsa"], l, 0)
                rows(a["w_up_nsa"], l, 256)
                rows(a["w_up_sb"], l, 0)
                rows(a["w_up_swa"], l, 0)
                many(4, lambda j: rows(a["w_out"], l, j * 256))
                swiglu(l, "ffn2")

            with loop(sp, L, (ring, C2)) as l:
                many(N2, lambda j: cols(a["w_in_2"], l, j * W2, W2))
                load(a["w_s_2"][l].rearrange("g t s -> t g s"),
                     lambda r: r[:, 0:512].rearrange("p (g s) -> p g s", s=P))
                many(4, lambda j: rows(a["w_out_2"], l, j * 256))
                for n in ("wq_x_2", "wk_x_2", "wv_x_2"):
                    many(4, lambda j: cols(a[n], l, j * 256, 256))
                many(4, lambda j: rows(a["wo_x_2"], l, j * 256))
                src_r = a["w_router_2"].rearrange("(k p) n -> p k n", p=P)
                load(src_r, lambda r: r[:, 0:K * NE].rearrange("p (k n) -> p k n", n=NE))

                def expert(e):
                    for i in range(2):
                        for w in (a["w_gate_2"], a["w_up_2"]):
                            src = w[l].rearrange("e (k p) n -> p e k n", p=P)[:, bass.ds(e, 1), :, i * 256:(i + 1) * 256]
                            load(src.rearrange("p e k n -> p (e k) n"), lambda r: r.rearrange("p (k n) -> p k n", n=256))
                    for i in range(2):
                        src = a["w_down_2"][l].rearrange("e (k p) n -> p e k n", p=P)[:, bass.ds(e, 1), 2 * i:2 * i + 2, :]
                        load(src.rearrange("p e k n -> p (e k) n"), lambda r: r.rearrange("p (k n) -> p k n", n=D))
                many(NE, expert, 6)

        @block.gpsimd
        def _(pool):
            steps = Steps(pool, pool_step)
            nload = 0
            nc.gpsimd.dma_start(CON, con).then_inc(consts_loaded, 16)
            nload += 1
            nload += load_vectors(pool, 0, consts_loaded)
            nc.gpsimd.dma_start(RB, a["rel_bias"]).then_inc(consts_loaded, 16)
            nc.gpsimd.dma_start(HOTR, hot_rev).then_inc(consts_loaded, 16)
            nc.gpsimd.dma_start(HOT, hot).then_inc(consts_loaded, 16)
            nc.gpsimd.dma_start(SINK.rearrange("p l h -> p (l h)"),
                                a["swa_sinks"].rearrange("l h -> (l h)").rearrange("(o n) -> o n", o=1).to_broadcast([P, L * 4])).then_inc(consts_loaded, 16)
            nc.gpsimd.dma_start(BR, a["b_router_2"].rearrange("(o n) -> o n", o=1).to_broadcast([P, NE])).then_inc(consts_loaded, 16)
            nload += 5
            assert nload == NLOAD
            nc.gpsimd.memset(NEGH, -0.5).then_inc(zeroed, 1)
            nc.gpsimd.memset(PC, 0.0).then_inc(zeroed, 1)
            nc.gpsimd.memset(AT, 1.0).then_inc(zeroed, 1)
            nc.gpsimd.memset(VCB, 0.0).then_inc(zeroed, 1)
            pool.wait_ge(bias_row, 1)
            nc.gpsimd.dma_start(scratch, VBIAS).then_inc(bias_stored, 16)
            pool.wait_ge(bias_stored, 16)
            nc.gpsimd.dma_start(BFLIP, bass.AP(tensor=scratch.tensor, offset=P, ap=[[1, P], [512, 12], [1, S]])).then_inc(bias_loaded, 16)
            pool.wait_ge(zeroed, 1)

            def row_rstd(n, eps):
                wait_apart(pool, squares_ready, n + 1, zeroed, 1)
                steps.link(nc.gpsimd.tensor_scalar(SMALL[:, 2:4], SMALL[:, 0:2], 1.0 / D, eps, ALU.mult, ALU.add))
                nc.gpsimd.tensor_tensor(SMALL[:, 4:6], SMALL[:, 2:4], NEGH[:, 0:2], ALU.pow).then_inc(rstd_ready, 1)

            with loop(pool, L, (steps, 3)) as l:
                row_rstd(st1(l, 0), 1e-6)
                row_rstd(st1(l, 1), 1e-6)
                pool.wait_ge(head_ms, l + 1)
                nc.gpsimd.tensor_tensor(SMALL[:, 96:132], SMALL[:, 48:84], NEGH[:, 0:36], ALU.pow).then_inc(head_rstd, 1)
                pool.wait_ge(cmp_ms, l + 1)
                nc.gpsimd.tensor_tensor(SMALL[0:64, 141:142], SMALL[0:64, 140:141], NEGH[0:64, 0:1], ALU.pow).then_inc(cmp_rstd, 1)
                row_rstd(st1(l, 2), 1e-6)

            with loop(pool, L, (steps, 3)) as l:
                for k in range(3):
                    pool.wait_ge(src_ready, tr2(l, 0 if k == 0 else k + 1) + 1)
                    for i, n in enumerate(("ln_g_2", "ln_b_2")):
                        nc.gpsimd.dma_start(LNGB[:, i, :], a[n][bass.ds(l, 1), k, :].to_broadcast([P, D])).then_inc(lngb_in, 16)
                    if k == 0:
                        nc.gpsimd.dma_start(SGB[:, 0, :], a["sgu_ln_g_2"][bass.ds(l, 1), :].to_broadcast([P, 512])).then_inc(layer_in, 16)
                        nc.gpsimd.dma_start(SGB[:, 1, :], a["sgu_ln_b_2"][bass.ds(l, 1), :].to_broadcast([P, 512])).then_inc(layer_in, 16)
                        nc.gpsimd.dma_start(WAB[0:16, :], a["w_a2_2"][l]).then_inc(layer_in, 16)
                        nc.gpsimd.dma_start(WAB[16:17, :], a["b_a_2"][bass.ds(l, 1), :]).then_inc(layer_in, 16)
                        pool.wait_ge(gs_ms, l + 1)
                        nc.gpsimd.tensor_tensor(SMALL[:, 176:192], SMALL[:, 160:176], NEGH[:, 0:16], ALU.pow).then_inc(gs_rstd, 1)
                    row_rstd(st2(l, k), 1e-5)

        @block.tensor
        def _(pe):
            ring = Ring()
            mm = nc.tensor.matmul

            splits = Count()

            def take():
                slot = ring.next()
                pe.wait_ge(ring_full[slot], ring.full())
                return RINGS[:, slot, :]

            def split_products(width, early, items, ht=None):
                slot = ring.next()
                par = (ring.n - 1) % 2
                splits.n += 1
                pe.wait_ge(wh_ready, splits.v + splits.n)
                listed = items(RH[:, par, 0:width], RL[:, slot, 0:width])

                def rounded(dst, a_, b_, start, stop, left):
                    mm(dst, a_[0], b_[0], start=start, stop=False)
                    mm(dst, a_[0], b_[1], start=False, stop=False) if left else mm(dst, a_[1], b_[0], start=False, stop=False)

                def rest(dst, a_, b_, start, stop, left):
                    return mm(dst, a_[1], b_[0], start=False, stop=stop) if left else mm(dst, a_[0], b_[1], start=False, stop=stop)

                for i, item in enumerate(listed[:early]):
                    if ht is not None and i < K and i % 2 == 0:
                        ht_wait(ht, i // 2)
                    rounded(*item)
                pe.wait_ge(wl_ready, splits.v + splits.n)
                for item in listed[:early]:
                    last = rest(*item)
                for item in listed[early:]:
                    rounded(*item)
                    last = rest(*item)
                last.then_inc(chunks_done, 1)

            def to_columns(bank, rhs, ht=None):
                def items(wh, wl):
                    wh, wl = (w.rearrange("p (k n) -> p k n", n=256) for w in (wh, wl))
                    return [(PS[:, bank, c * S:(c + 1) * S], (wh[:, k, c * P:(c + 1) * P], wl[:, k, c * P:(c + 1) * P]),
                             (rhs[0][:, k, :], rhs[1][:, k, :]), k == 0, k == K - 1, True) for c in range(2) for k in range(K)]
                split_products(SLOT, K, items, ht)

            def to_rows(width, bank_of, lhs, at=0, ht=None):
                def items(wh, wl):
                    wh, wl = (w.rearrange("p (k n) -> p k n", n=width) for w in (wh, wl))
                    return [(PS[:, bank_of(t), at * t:at * t + width], (lhs[0][:, k, t * P:(t + 1) * P], lhs[1][:, k, t * P:(t + 1) * P]),
                             (wh[:, k, :], wl[:, k, :]), k == 0, k == K - 1, False) for t in range(T) for k in range(K)]
                split_products(K * width, K if at else 2 * K, items, ht)

            def add_rows(bank, lhs, k0, first, end, tiles=T):
                def items(wh, wl):
                    wh, wl = (w.rearrange("p (k n) -> p k n", n=D) for w in (wh, wl))
                    return [(PS[:, bank + 2 * t + h, :], (lhs[0][:, k0 + k, t * P:(t + 1) * P], lhs[1][:, k0 + k, t * P:(t + 1) * P]),
                             (wh[:, k, h * 512:(h + 1) * 512], wl[:, k, h * 512:(h + 1) * 512]), first and k == 0, end and k == 1, False)
                            for k in range(2) for t in range(tiles) for h in range(2)]
                split_products(SLOT, 4 * tiles, items)

            def transpose_rows(src, n):
                pe.wait_ge(ht_l, n * 4 + 4)
                pe.wait_ge(src_ready, n + 1)
                for b in range(4):
                    for k in range(2):
                        for t in range(T):
                            last = nc.tensor.transpose(PS[:, b, k * S + t * P:k * S + (t + 1) * P],
                                                       src[:, t, (2 * b + k) * P:(2 * b + k + 1) * P], IDENT)
                    last.then_inc(tr_ready, 1)

            def ht_wait(n, bank=3):
                wait_apart(pe, ht_l, n * 4 + bank + 5, consts_loaded, 16 * NLOAD)

            def swiglu(l, f):
                n = tr1(l, 4 * f)
                transpose_rows(TMP, n)

                def pair(j, par, ht=None):
                    for u in range(2):
                        if u == 0:
                            pe.wait_ge(hidden_ready, l * 22 + f * 11 + j + 1)
                        to_columns(2 * par + u, HT, ht if u == 0 else None)

                pair(0, 0, n)
                with loop(pe, 5, (ring, 4), (splits, 4)) as i:
                    for j in range(2):
                        pair(i * 2 + 1 + j, 1 - j)
                for j in range(FR):
                    pe.wait_ge(hidden_ready, l * 22 + f * 11 + j + 3)
                    add_rows(4, GT, 2 * j, j == 0, j == FR - 1)

            def rows_product(lhs, nchunk, bank, k0=0, ht=None):
                for j in range(nchunk):
                    if ht is not None:
                        ht_wait(ht, k0 // 2 + j)
                    add_rows(bank, lhs, k0 + 2 * j, j == 0, j == nchunk - 1)

            def project(base, width, j, par, ht=None):
                pe.wait_ge(proj_a, base + j + 1)
                pe.wait_ge(proj_d, base + j + 1)
                to_rows(width, lambda t: 2 * par + t, HT, ht=ht)

            pe.sem_inc(chunks_done, SLOTS)
            pe.wait_ge(consts_loaded, 16 * NLOAD)
            pe.wait_ge(vectors_loaded, 16 * NVEC * (L - 1))
            nc.tensor.transpose(PS[:, 4, 0:L * VL], VEC, IDENT[0:L * VL, 0:L * VL]).then_inc(vec_ready, 1)
            pe.wait_ge(rb_ready, 1)
            mm(PS[0:12, 5, :], RBP.rearrange("p g b a -> p (g b a)"), HOTR, start=True, stop=True).then_inc(hot_ready, 1)
            for t in range(T):
                for n in range(NCMP):
                    u = t * P - 16 * n - 31 + 256
                    last = mm(PS[:, 6, (t * NCMP + n) * 8:(t * NCMP + n + 1) * 8], HOT[:, u:u + P], RB[:, 0:8], start=True, stop=True)
            last.then_inc(hot_ready, 1)
            pe.wait_ge(bias_loaded, 16)
            pe.wait_ge(vec_taken, 5)
            for b in range(6):
                last = mm(PS[:, b, :], CON[:, O_FLIP:O_FLIP + P], BFLIP[:, 2 * b:2 * b + 2, :].rearrange("p h n -> p (h n)"), start=True, stop=True)
            last.then_inc(hot_ready, 1)
            pe.wait_ge(vec_taken, 7)

            with loop(pe, L, (ring, C1), (splits, S1)) as l:
                swiglu(l, 0)
                n = tr1(l, 1)
                transpose_rows(TMP, n)
                for j in range(4):
                    project(l * N1, W1, j, j % 2, n if j == 0 else None)
                with loop(pe, N1 // 4 - 1, (ring, 4), (splits, 4)) as i:
                    for j in range(4):
                        project(l * N1, W1, i * 4 + 4 + j, j % 2)
                pe.wait_ge(proj_a, l * N1 + N1 + 2)
                pe.wait_ge(proj_d, l * N1 + N1 + 2)
                pe.wait_ge(heads_ready, l + 1)
                pe.wait_ge(keys_copied, l + 1)
                for b in range(10):
                    if b >= 4:
                        pe.wait_ge(tt_a if b % 2 == 0 else tt_d, l * 5 + (b - 4) // 2 + 1)
                    for i in range(2):
                        for t in range(T):
                            if b < 3:
                                src = QKN[:, t, 4 * b + 2 * i:4 * b + 2 * i + 2, :].rearrange("p h d -> p (h d)")
                            elif b < 8:
                                src = KD[:, t, b - 3, i, :, :].rearrange("p u d -> p (u d)")
                            else:
                                c = (SQ_ if b == 8 else SK_) + i * P
                                src = PROJ[:, t, c:c + P]
                            last = nc.tensor.transpose(PS[:, b % 4, i * S + t * P:i * S + (t + 1) * P], src, IDENT)
                    last.then_inc(htr_ready, 1)
                pe.wait_ge(blocks_ready, l + 1)
                for kv in range(2):
                    for i in range(2):
                        w = take().rearrange("p (k n) -> p k n", n=256)
                        for r in range(8):
                            last = mm(PS[0:64, 4 + kv, 0:256], BT[:, kv, i * 8 + r, :], w[:, r, :],
                                      start=(i + r == 0), stop=(i == 1 and r == 7))
                        last.then_inc(chunks_done, 1)
                wait_apart(pe, cmp_hidden, 2 * l + 2, consts_loaded, 16 * NLOAD)
                for kv in range(2):
                    for i in range(2):
                        last = nc.tensor.transpose(PS[:, 6, (kv * 2 + i) * 64:(kv * 2 + i + 1) * 64],
                                                   HS[:, kv, i * P:(i + 1) * P], IDENT[0:64, 0:64])
                last.then_inc(cmp_tr, 1)
                pe.wait_ge(cmp_trs, l + 1)
                w = take()[:, 0:2 * HD].rearrange("p (k n) -> p k n", n=HD)
                for i in range(2):
                    last = mm(PS[0:64, 7, 0:HD], HST[:, i, :], w[:, i, :], start=(i == 0), stop=(i == 1))
                last.then_inc(chunks_done, 1)
                w = take()[:, 0:2 * HD].rearrange("p (k n) -> p k n", n=HD)
                for i in range(2):
                    last = mm(PS[:, 5, 0:HD], HSTV[:, i, :, :].rearrange("p a n -> p (a n)"), w[:, i, :],
                              start=(i == 0), stop=(i == 1))
                last.then_inc(chunks_done, 1)
                wait_apart(pe, cmp_keys, l + 1, consts_loaded, 16 * NLOAD)
                nc.tensor.transpose(PS[:, 6, 256:320], KCN.rearrange("p u d -> p (u d)"), IDENT[0:64, 0:64]).then_inc(cmp_kt, 1)
                pe.wait_ge(cmp_kts, l + 1)
                for t in range(T):
                    for h in range(8):
                        hp, g, at = 64 * (h % 2), h // 4, (t * 4 + h // 2) * 32
                        last = mm(PS[:, 4 + 3 * (h % 2), at:at + NCMP], TT[hp:hp + 64, h // 2, t * P:(t + 1) * P],
                                  KCT[hp:hp + 64, g * 32:g * 32 + NCMP], start=True, stop=True)
                last.then_inc(scc_ready, 1)

                def scores(u):
                    kind, g, t = UNITS[u]
                    nk = (t + 1) * P
                    n = l * NU + u
                    if u >= 2:
                        pe.wait_ge(sc_taken, n - 1)
                    for h in range(4):
                        if kind < 2:
                            q, kk, hp = (4 * g + h) // 2, 6 + 2 * kind + g, 64 * (h % 2)
                        else:
                            q, kk, hp = 4 + h // 2, 10 + h // 2, 64 * (h % 2)
                        last = mm(PS[:, 2 * (u % 2) + h % 2, (h // 2) * S:(h // 2) * S + nk], TT[hp:hp + 64, q, t * P:(t + 1) * P],
                                  TT[hp:hp + 64, kk, 0:nk], start=True, stop=True)
                    last.then_inc(sc_ready, 1)

                def transposed(u):
                    kind, g, t = UNITS[u]
                    n = l * NU + u
                    pe.wait_ge(exp_ready, n + 1)
                    if u >= 1:
                        pe.wait_ge(pt_a, n)
                        if both(u):
                            pe.wait_ge(pt_d, l * both(NU) + both(u))
                    for b in range(t + 1):
                        for h in range(4):
                            last = nc.tensor.transpose(PS[:, 4 + b, h * P:(h + 1) * P], PR[:, u % 2, h, b * P:(b + 1) * P], IDENT)
                    last.then_inc(pt_ready, 1)

                def values(u):
                    kind, g, t = UNITS[u]
                    n = l * NU + u
                    pe.wait_ge(pt_a, n + 1)
                    if t:
                        pe.wait_ge(pt_d, l * both(NU) + both(u + 1))
                    pe.wait_ge(o_taken, l * (NU + 1) + max(u, 1))
                    for h in range(4):
                        vc = (VS if kind == 0 else VW) + g * HD if kind < 2 else WV + (h // 2) * HD
                        for b in range(t + 1):
                            s_ = 2 * (h % 2) + h // 2
                            last = mm(PS[:, 6 + u % 2, h * HD:(h + 1) * HD], PT[:, u % 2, b, s_ * P:(s_ + 1) * P], PROJ[:, b, vc:vc + HD],
                                      start=(b == 0), stop=(b == t))
                    last.then_inc(o_ready, 1)

                pe.wait_ge(tt_a, l * 5 + 5)
                pe.wait_ge(tt_d, l * 5 + 5)
                scores(0)
                pe.wait_ge(pc_ready, l + 1)
                for r in range(2):
                    for t in range(T):
                        last = nc.tensor.transpose(PS[:, 5, (r * 2 + t) * P:(r * 2 + t + 1) * P],
                                                   PC[:, r * 8 + t * 4:r * 8 + t * 4 + 4, :].rearrange("p h n -> p (h n)"), IDENT)
                last.then_inc(pct_ready, 1)
                pe.wait_ge(pct_taken, l + 1)
                for t in range(T):
                    for r in range(2):
                        last = mm(PS[:, 6 + t, r * 256:(r + 1) * 256], PT[:, 1, 0, (r * 2 + t) * P:(r * 2 + t + 1) * P],
                                  VCB.rearrange("p h d -> p (h d)"), start=True, stop=True)
                last.then_inc(oc_ready, 1)
                for u in range(NU):
                    if u + 1 < NU:
                        scores(u + 1)
                    transposed(u)
                    if u:
                        values(u - 1)
                values(NU - 1)
                pe.wait_ge(sc_taken, l * NU + NU)
                for h in range(4):
                    hp = 64 * (h % 2)
                    mm(PS[:, h, 0:S], TT[hp:hp + 64, 18 + h // 2, 0:P], TT[hp:hp + 64, 16 + h // 2, :], start=True, stop=True)
                    last = mm(PS[:, h, S:S + P], TT[hp:hp + 64, 18 + h // 2, P:S], TT[hp:hp + 64, 16 + h // 2, P:S], start=True, stop=True)
                last.then_inc(z_ready, 1)
                pe.wait_ge(sp_ready, l + 1)
                pe.wait_ge(o_taken, l * (NU + 1) + NU + 1)
                for h in range(4):
                    mm(PS[:, 4 + h, 0:P], CON[:, O_U:O_U + P], EX[:, h, 0:P], start=True, stop=True)
                    mm(PS[:, 4 + h, P:S], CON[:, O_U:O_U + P], EX[:, h, P:S], start=True, stop=False)
                    mm(PS[:, 4 + h, P:S], CON[:, O_ONE:O_ONE + P], EX[:, h, S:S + P], start=False, stop=True)
                    last = mm(PS[:, 4 + h, S:S + P], CON[:, O_U:O_U + P], EX[:, h, S:S + P], start=True, stop=True)
                last.then_inc(after_ready, 1)
                pe.wait_ge(w_ready, l + 1)
                for h in range(4):
                    vc = SV_ + h * HD
                    mm(PS[:, 0, h * HD:(h + 1) * HD], EX[:, h, 0:P], PROJ[:, 0, vc:vc + HD], start=True, stop=True)
                for h in range(4):
                    vc = SV_ + h * HD
                    mm(PS[:, 0, S + h * HD:S + (h + 1) * HD], EX[:, h, P:S], PROJ[:, 0, vc:vc + HD], start=True, stop=False)
                    last = mm(PS[:, 0, S + h * HD:S + (h + 1) * HD], EX[:, h, S:S + P], PROJ[:, 1, vc:vc + HD], start=False, stop=True)
                last.then_inc(osb_ready, 1)
                n = tr1(l, 2)
                transpose_rows(Y, n)
                ht_wait(n)
                rows_product(HT, 2, 0)
                rows_product(HT, 1, 4, k0=4)
                pe.wait_ge(rows_taken, l + 1)
                rows_product(HT, 1, 0, k0=6)
                n = tr1(l, 3)
                transpose_rows(Y, n)
                rows_product(HT, 4, 4, ht=n)
                swiglu(l, 1)

            pe.wait_ge(mem_loaded, 16)
            transpose_rows(TMP, 5 * L)
            ht_wait(5 * L)

            with loop(pe, L, (ring, C2), (splits, S2)) as l:
                n = tr2(l, 0)
                transpose_rows(X, n)
                for j in range(N2 % 4):
                    project(L * N1 + l * N2, W2, j, j % 2, n if j == 0 else None)
                with loop(pe, N2 // 4, (ring, 4), (splits, 4)) as i:
                    for j in range(4):
                        project(L * N1 + l * N2, W2, i * 4 + 2 + j, j % 2)
                w = take()[:, 0:512]
                for g in range(4):
                    last = nc.tensor.transpose(PS[:, 7, g * P:(g + 1) * P], w[:, g * P:(g + 1) * P], IDENT)
                last.then_inc(chunks_done, 1)
                pe.wait_ge(proj_a, L * N1 + l * N2 + N2 + 2)
                pe.wait_ge(proj_d, L * N1 + l * N2 + N2 + 2)
                for t in range(T):
                    nc.tensor.transpose(PS[0:16, 4, t * P:(t + 1) * P], PROJ2[:, t, GA:GA + 16], IDENT)
                for hp in range(2):
                    for t in range(T):
                        last = nc.tensor.transpose(PS[:, 5, hp * S + t * P:hp * S + (t + 1) * P], PROJ2[:, t, GQ + hp * P:GQ + (hp + 1) * P], IDENT)
                last.then_inc(ga_ready, 1)
                pe.wait_ge(ga_copied, 2 * l + 2)
                pe.wait_ge(layer_in, l * 64 + 64)
                for t in range(T):
                    last = mm(PS[:, 4, t * S:(t + 1) * S], AT[0:17, t * P:(t + 1) * P], WAB, start=True, stop=True)
                last.then_inc(gl_ready, 1)
                pe.wait_ge(gl_sp, l + 1)
                for t in range(T):
                    last = mm(PS[:, 6, t * S:(t + 1) * S], CON[:, O_REV:O_REV + P], GX[:, t, 0:S], start=True, stop=True)
                for t in range(T):
                    for hp in range(2):
                        last = mm(PS[:, 5, hp * 4 + 2 * t:hp * 4 + 2 * t + 2], GX[:, t, hp * P:(hp + 1) * P], CON[:, O_CHO:O_CHO + 2], start=True, stop=True)
                last.then_inc(gl_cum, 1)
                wait_apart(pe, kdec_ready, l + 1, consts_loaded, 16 * NLOAD)

                def kv(c):
                    t, half = c // 2, 64 * (c % 2)
                    if c >= 2:
                        wait_apart(pe, state_ready, l * 4 + c - 1, consts_loaded, 16 * NLOAD)
                    for h in range(4):
                        o = 64 * (h % 2)
                        last = mm(PS[o:o + 64, c % 2, (h // 2) * P:(h // 2 + 1) * P], KDEC[half:half + 64, t, h * HD:(h + 1) * HD],
                                  PROJ2[half:half + 64, t, GV + h * P:GV + (h + 1) * P], start=True, stop=True)
                    last.then_inc(kv_ready, 1)

                kv(0)
                for c in range(4):
                    if c + 1 < 4:
                        kv(c + 1)
                    t, half = c // 2, 64 * (c % 2)
                    wait_apart(pe, state_ready, l * 4 + c + 1, consts_loaded, 16 * NLOAD)
                    for h in range(4):
                        o = 64 * (h % 2)
                        last = mm(PS[half:half + 64, 2 + 2 * (h % 2) + t, (h // 2) * P:(h // 2 + 1) * P], TT[o:o + 64, h // 2, c * 64:(c + 1) * 64],
                                  STATE[o:o + 64, c + 1, h // 2, :], start=True, stop=True)
                last.then_inc(go_ready, 1)
                pe.wait_ge(vn_ready, l + 1)
                pe.wait_ge(ws_copied, l + 1)
                for t in range(T):
                    for g in range(4):
                        last = mm(PS[:, 4 + t, g * P:(g + 1) * P], WST[:, g, :], PROJ2[:, t, SV2 + g * P:SV2 + (g + 1) * P], start=True, stop=True)
                last.then_inc(mix_ready, 1)
                n = tr2(l, 1)
                transpose_rows(Y, n)
                rows_product(HT, 4, 4, ht=n)
                n = tr2(l, 2)
                transpose_rows(X, n)
                for j in range(8):
                    if j >= 2:
                        pe.wait_ge(qk_a if j % 2 == 0 else qk_d, l * 4 + j // 2)
                    to_columns(j % 2, HT if j < 4 else MEMT, n if j == 0 else None)
                for j in range(4):
                    if j >= 2:
                        pe.wait_ge(vx_a, l * 4 + j - 1)
                        pe.wait_ge(vx_d, l * 4 + j - 1)
                    to_rows(256, lambda t: 2 + 2 * (j % 2) + t, MEMT)
                for done in (qk_a, qk_d, vx_a, vx_d):
                    pe.wait_ge(done, l * 4 + 4)
                for t in range(T):
                    for h in range(4):
                        for k in range(2):
                            last = mm(PS[:, 2 * t + h // 2, (h % 2) * S:(h % 2 + 1) * S], TT[:, 2 * h + k, t * P:(t + 1) * P],
                                      TT[:, 8 + 2 * h + k, :], start=(k == 0), stop=(k == 1))
                    last.then_inc(xs_ready, 1)
                for t in range(T):
                    pe.wait_ge(xp_ready, l * 2 + t + 1)
                    for b in range(2):
                        for h in range(4):
                            last = nc.tensor.transpose(PS[:, 4 + 2 * t + b, h * P:(h + 1) * P], PR[:, t, h, b * P:(b + 1) * P], IDENT)
                    last.then_inc(xt_ready, 1)
                pe.wait_ge(xt_a, l * 2 + 2)
                pe.wait_ge(xt_d, l * 2 + 2)
                for h in range(4):
                    for c in range(2):
                        for b in range(2):
                            last = mm(PS[:, h, c * S:(c + 1) * S], VX[:, b, h * 256 + c * P:h * 256 + (c + 1) * P], PXT[:, b, h, :], start=(b == 0), stop=(b == 1))
                    last.then_inc(xo_ready, 1)
                pe.wait_ge(xo_l, l * 4 + 4)
                rows_product(HT, 4, 4)
                n = tr2(l, 3)
                transpose_rows(X, n)
                ht_wait(n)
                to_rows(NE, lambda t: 4, HT, NE)

                def expert(e, n, tiles):
                    for p in range(2):
                        for u in range(2):
                            if u == 0:
                                pe.wait_ge(hidden_ready, 22 * L + l * 2 * NE + e * 2 + p + 1)
                            if n == S:
                                to_columns(2 * p + u, HT)
                            else:
                                w = take().rearrange("p (k n) -> p k n", n=256)
                                for c in range(2):
                                    for k in range(K):
                                        last = mm(PS[:, 2 * p + u, c * S:c * S + n], w[:, k, c * P:(c + 1) * P], XSEAT[:, k, :],
                                                  start=(k == 0), stop=(k == K - 1))
                                last.then_inc(chunks_done, 1)
                    for j in range(2):
                        if j == 0:
                            pe.wait_ge(moe_taken, l * (NE + 1) + e + 1)
                        pe.wait_ge(hidden_ready, 22 * L + l * 2 * NE + e * 2 + j + 3)
                        add_rows(4, EH, 2 * j, j == 0, j == 1, tiles)

                pe.wait_ge(oh_ready, l + 1)
                mm(PS[:, 4, 32:36], CON[:, O_U:O_U + P], OH[:, 0, :], start=True, stop=False)
                mm(PS[:, 4, 32:36], CON[:, O_ONE:O_ONE + P], OH[:, 1, :], start=False, stop=True)
                mm(PS[:, 4, 36:40], CON[:, O_U:O_U + P], OH[:, 1, :], start=True, stop=True)
                mm(PS[:, 4, 40:44], CON[:, O_ONE:O_ONE + P], OH[:, 0, :], start=True, stop=False)
                mm(PS[:, 4, 40:44], CON[:, O_ONE:O_ONE + P], OH[:, 1, :], start=False, stop=True).then_inc(pos_ready, 1)
                wait_apart(pe, crowd_known, l + 1, consts_loaded, 16 * NLOAD)
                crowded = pe.value_load(CROWDED[0:1, 0:1], min_val=0, max_val=1)
                with pe.If(crowded > 0):
                    with loop(pe, NE // 2, (ring, 12), (splits, 12)) as i:
                        for j in range(2):
                            expert(i * 2 + j, S, T)
                    pe.sem_inc(seat_tr, 1)
                    pe.sem_inc(gather_ready, NG_)
                    pe.sem_inc(scatter_ready, 1)
                with pe.Else():
                    ring.n -= 6 * NE
                    splits.n -= 6 * NE
                    pe.wait_ge(seat_ready, l + 1)
                    for g in range(NG_):
                        for t in range(T):
                            nc.tensor.transpose(PS[:, 6 + g // 2, ((g % 2) * T + t) * P:((g % 2) * T + t + 1) * P], SEAT[:, g, t, :], IDENT)
                    for g in range(NG_):
                        for t in range(T):
                            last = mm(PS[:, 5, g * EG:(g + 1) * EG], SEAT[:, g, t, :], GATE[:, g * EG:(g + 1) * EG, t], start=(t == 0), stop=(t == T - 1))
                    last.then_inc(seat_tr, 1)
                    with loop(pe, NG_, (ring, 6 * EG), (splits, 2 * EG)) as g:
                        pe.wait_ge(seat_taken, l + 1)
                        pe.wait_ge(seat_a, l * NG_ + g + 1)
                        pe.wait_ge(seat_d, l * NG_ + g + 1)
                        for k in range(K):
                            for t in range(T):
                                last = mm(PS[:, 6 + k // 4, (k % 4) * P:(k % 4 + 1) * P], X[:, t, k * P:(k + 1) * P],
                                          SEAT[:, bass.ds(g, 1), t, :].rearrange("p o n -> p (o n)"), start=(t == 0), stop=(t == T - 1))
                        last.then_inc(gather_ready, 1)
                        pe.wait_ge(seat_a, l * NG_ + g + 2)
                        pe.wait_ge(seat_d, l * NG_ + g + 2)
                        for j in range(EG):
                            expert(g * EG + j, P, 1)
                    pe.wait_ge(moe_taken, l * (NE + 1) + NE + 1)
                    for t in range(T):
                        for h in range(2):
                            for g in range(NG_):
                                last = mm(PS[:, 4 + 2 * t + h, :], SEATT[:, g, t, :], YSEAT[:, g * D + h * 512:g * D + (h + 1) * 512],
                                          start=(g == 0), stop=(g == NG_ - 1))
                    last.then_inc(scatter_ready, 1)
                    splits.n += 4 * NE

        @block.scalar
        def _(act):
            ring = Ring()
            steps = Steps(act, act_step)
            A = nc.scalar.activation

            def chunk():
                ring.next()
                act.wait_ge(chunks_done, ring.done())

            def squares(n, extra=0):
                act.wait_ge(x_ready, n + 1 + extra)
                A(TMP[:, 0, :], X[:, 0, :], ACT.Square, accum_out=SMALL[:, 0:1])
                A(TMP[:, 1, :], X[:, 1, :], ACT.Square, accum_out=SMALL[:, 1:2]).then_inc(squares_ready, 1)

            def ht_copy(n, dst, gains=None, tiles=K):
                for b in range(4):
                    act.wait_ge(tr_ready, n * 4 + b + 1)
                    if gains is None or 2 * b >= tiles:
                        A(dst[0][:, 2 * b:2 * b + 2, :], PS[:, b, :].rearrange("p (k n) -> p k n", k=2), ACT.Copy).then_inc(ht_h, 1)
                    else:
                        A(dst[0][:, 2 * b, :], PS[:, b, 0:S], ACT.Copy, scale=LV[:, gains + 2 * b:gains + 2 * b + 1])
                        A(dst[0][:, 2 * b + 1, :], PS[:, b, S:2 * S], ACT.Copy, scale=LV[:, gains + 2 * b + 1:gains + 2 * b + 2]).then_inc(ht_h, 1)

            ahead, splits = Ring(), Count()

            def split(width=SLOT, back=2):
                slot = ahead.next()
                par = (ahead.n - 1) % 2
                splits.n += 1
                act.wait_ge(ring_full[slot], ahead.full())
                act.wait_ge(chunks_done, ahead.v + SLOTS + ahead.n - back)
                A(RH[:, par, 0:width], RINGS[:, slot, 0:width], ACT.Copy).then_inc(wh_ready, 1)

            def silu(index, par):
                chunk()
                act.wait_ge(hidden_ready, index + 1)
                A(SIL[:, par, :], PS[:, 2 * par, :], ACT.Silu).then_inc(silu_ready, 1)
                split()
                chunk()
                split()

            def swiglu(l, f, gains):
                squares(st1(l, 2 * f))
                split()
                split()
                ht_copy(tr1(l, 4 * f), HT, gains)
                with loop(act, 5, (ring, 4), (ahead, 4), (splits, 4)) as i:
                    for j in range(2):
                        silu(l * 22 + f * 11 + i * 2 + j, j)
                silu(l * 22 + f * 11 + 10, 0)
                for j in range(FR - 2):
                    chunk()
                    split()
                ring.n += 2

            def project(width, j, par, more=True, to=PROJ):
                chunk()
                if more:
                    split(K * width)
                A(to[:, 0, bass.ds(j * width, width)], PS[:, 2 * par, 0:width], ACT.Copy).then_inc(proj_a, 1)

            act.dma_start(X, x_view).then_inc(x_loaded, 16)
            for l in range(1, L):
                load_vectors(act, l, vectors_loaded)
            act.sem_inc(proj_a, 2)
            act.sem_inc(seat_a, 1)

            with loop(act, L, (ring, C1), (ahead, C1), (splits, S1), (steps, 1)) as l:
                act.wait_ge(lv_ready, l + 1)
                swiglu(l, 0, V_F1)
                squares(st1(l, 1))
                split(K * W1)
                split(K * W1)
                ht_copy(tr1(l, 1), HT, V_MIX)
                with loop(act, N1 // 4 - 1, (ring, 4), (ahead, 4), (splits, 4)) as i:
                    for j in range(4):
                        project(W1, i * 4 + j, j % 2)
                for j in range(N1 - 4, N1):
                    project(W1, j, j % 2, j < N1 - 2)
                act.wait_ge(proj_a, l * N1 + N1 + 2)
                act.wait_ge(proj_d, l * N1 + N1 + 2)
                for at, c, n in ((0, NQ, 8), (8, WQ, 6), (14, KS, 2), (16, KW, 2)):
                    last = A(QKN[:, :, at:at + n, :].rearrange("p t h d -> p t (h d)"), PROJ[:, :, c:c + n * HD], ACT.Square)
                last.then_inc(head_sq, 1)
                for kv in range(2):
                    for t in range(T):
                        for u in range(2):
                            last = A(KD[:, t, 3 + kv, :, u, :], PROJ[:, t, KC + kv * P:KC + (kv + 1) * P].rearrange("p (g d) -> p g d", g=2), ACT.Copy)
                last.then_inc(keys_copied, 1)
                A(PROJ[:, :, NG:NG + 24], PROJ[:, :, NG:NG + 24], ACT.Sigmoid)
                A(PROJ[:, :, BG:D_IN], PROJ[:, :, BG:D_IN], ACT.Sigmoid).then_inc(gates_ready, 1)
                for b in (0, 2, 4, 6, 8):
                    act.wait_ge(htr_ready, l * 10 + b + 1)
                    scale = {0: LV[:, VL:VL + 1], 2: LV[:, VL + 1:VL + 2], 4: LV[:, V_KN:V_KN + 1], 6: 1.0, 8: HD ** -0.5}[b]
                    A(TT[:, 2 * b:2 * b + 2, :], PS[:, b % 4, :].rearrange("p (k n) -> p k n", k=2), ACT.Copy, scale=scale).then_inc(tt_a, 1)
                ahead.n += 6
                for kv in range(2):
                    ring.next()
                    chunk()
                    A(HS[:, kv, :], PS[0:64, 4 + kv, 0:256], ACT.Silu).then_inc(cmp_hidden, 1)
                act.wait_ge(cmp_tr, l + 1)
                A(HST, PS[:, 6, 0:2 * 64].rearrange("p (i n) -> p i n", i=2), ACT.Copy)
                for u in range(2):
                    last = A(HSTV.rearrange("p i (g u) n -> p i g u n", u=2)[:, :, :, u, :],
                             PS[:, 6, 2 * 64:4 * 64].rearrange("p (i g n) -> p i g n", i=2, g=2), ACT.Copy)
                last.then_inc(cmp_trs, 1)
                ring.n += 2
                act.wait_ge(cmp_kt, l + 1)
                A(KCT, PS[:, 6, 256:320], ACT.Copy, scale=LV[:, V_KN:V_KN + 1]).then_inc(cmp_kts, 1)
                act.wait_ge(pc_in, l + 1)
                A(PC[:, :, 0:NCMP], PC[:, :, 0:NCMP], ACT.Exp).then_inc(pc_exp, 1)
                act.wait_ge(pct_ready, l + 1)
                A(PT[:, 1, 0, :], PS[:, 5, :], ACT.Copy).then_inc(pct_taken, 1)

                def exps(u):
                    kind, g, t = UNITS[u]
                    nk = (t + 1) * P
                    c = 16 * (u % 2)
                    act.wait_ge(sc_max, l * NU + u + 1)
                    for s_ in range(4):
                        last = A(PR[:, u % 2, s_, 0:nk], PR[:, u % 2, s_, 0:nk], ACT.Exp, bias=SMALL[:, 208 + c + s_:209 + c + s_],
                                 accum_out=SMALL[:, 212 + c + s_:213 + c + s_])
                    if kind == 2:
                        last = A(SMALL[:, 216 + c:220 + c], SMALL[:, 216 + c:220 + c], ACT.Exp)
                    last.then_inc(exp_ready, 1)

                def copies(u):
                    act.wait_ge(pt_ready, l * NU + u + 1)
                    A(PT[:, u % 2, 0, :], PS[:, 4, :], ACT.Copy).then_inc(pt_a, 1)

                exps(0)
                for u in range(NU):
                    if u + 1 < NU:
                        exps(u + 1)
                    copies(u)
                act.wait_ge(z_ready, l + 1)
                A(ZS, PS[:, 0:4, 0:384], ACT.Copy).then_inc(z_copied, 1)
                act.wait_ge(z_abs, l + 1)
                steps.link(A(EX, EX, ACT.Exp))
                A(EX, EX, ACT.Ln, bias=1.0).then_inc(z_ln, 1)
                act.wait_ge(w_arg, l + 1)
                A(EX, ZS, ACT.Exp).then_inc(w_ready, 1)
                act.wait_ge(w_ready, l + 1)
                split()
                split()
                ht_copy(tr1(l, 2), HT)
                for j in range(4):
                    split()
                ht_copy(tr1(l, 3), HT)
                for j in range(2):
                    split()
                ring.n += 8
                swiglu(l, 1, V_F2)

            act.wait_ge(x_ready, 3 * L + 1)
            act.dma_start(TMP, a["mem_2"][0].rearrange("(t p) n -> p t n", p=P)).then_inc(mem_loaded, 16)
            ht_copy(5 * L, MEMT)

            with loop(act, L, (ring, C2), (ahead, C2), (splits, S2), (steps, 1)) as l:
                split(K * W2)
                split(K * W2)
                ht_copy(tr2(l, 0), HT)
                with loop(act, N2 // 4, (ring, 4), (ahead, 4), (splits, 4)) as i:
                    for j in range(4):
                        project(W2, i * 4 + j, j % 2, True, PROJ2)
                for j in range(N2 // 4 * 4, N2):
                    project(W2, j, j % 2, False, PROJ2)
                ahead.n += 1
                chunk()
                act.wait_ge(lv_ready, L + l + 1)
                A(WST[0:64, :, :], PS[0:64, 7, :].rearrange("p (g t) -> p g t", g=4), ACT.Copy)
                A(WST[64:P, :, 64:P], PS[64:P, 7, :].rearrange("p (g t) -> p g t", g=4)[:, :, 64:P], ACT.Copy).then_inc(ws_copied, 1)
                act.wait_ge(ga_ready, l + 1)
                A(AT[0:16, :], PS[0:16, 4, 0:S], ACT.Copy).then_inc(ga_copied, 1)
                A(TT[:, 0:2, :], PS[:, 5, :].rearrange("p (k n) -> p k n", k=2), ACT.Copy, scale=HD ** -0.5).then_inc(ga_copied, 1)
                act.wait_ge(proj_a, L * N1 + l * N2 + N2 + 2)
                act.wait_ge(proj_d, L * N1 + l * N2 + N2 + 2)
                A(PROJ2[:, :, SU:D_IN2], PROJ2[:, :, SU:D_IN2], ACT.Gelu_apprx_tanh).then_inc(gelu_ready, 1)
                A(PROJ2[:, :, GR:GR + 512], PROJ2[:, :, GR:GR + 512], ACT.Silu).then_inc(gelu_ready, 1)
                act.wait_ge(sv_centred, l + 1)
                A(TMP[:, :, 512:1024], PROJ2[:, :, SV2:SV2 + 512], ACT.Square).then_inc(sv_sq, 1)
                act.wait_ge(gl_abs, l + 1)
                steps.link(A(GX[:, 0:2, 0:S], GX[:, 0:2, 0:S], ACT.Exp))
                A(GX[:, 0:2, 0:S], GX[:, 0:2, 0:S], ACT.Ln, bias=1.0).then_inc(gl_ln, 1)
                act.wait_ge(gl_cum, l + 1)
                A(KEXP, PS[:, 6, :].rearrange("p (t n) -> p t n", t=2), ACT.Exp, scale=-1.0 / 16)
                A(SMALL[:, 200:208], PS[:, 5, 0:8], ACT.Exp, scale=-1.0 / 16).then_inc(gl_exp, 1)
                split()
                split()
                act.wait_ge(go_ready, l + 1)
                A(TMP[:, :, 0:512].rearrange("p t (r n) -> p r t n", r=2), PS[:, 2:6, 0:256].rearrange("p (r t) n -> p r t n", r=2),
                  ACT.Square).then_inc(go_sq, 1)
                ht_copy(tr2(l, 1), HT, V_GN, 4)
                for j in range(4):
                    split()
                ring.n += 4
                squares(st2(l, 0), 1)
                ht_copy(tr2(l, 2), HT)
                for j in range(8):
                    chunk()
                    split()
                    if j % 2:
                        continue
                    A(TT[:, 2 * j:2 * j + 2, :], PS[:, 0, :].rearrange("p (k n) -> p k n", k=2), ACT.Copy).then_inc(qk_a, 1)
                for j in range(4):
                    chunk()
                    if j < 2:
                        split()
                    A(VX[:, 0, j * 256:(j + 1) * 256], PS[:, 2 + 2 * (j % 2), 0:256], ACT.Copy).then_inc(vx_a, 1)
                for t in range(T):
                    act.wait_ge(xm_ready, l * 2 + t + 1)
                    for h in range(4):
                        last = A(PR[:, t, h, :], PS[:, 2 * t + h // 2, (h % 2) * S:(h % 2 + 1) * S], ACT.Exp, scale=1.0 / 16,
                                 bias=SMALL[:, 208 + 16 * t + h:209 + 16 * t + h], accum_out=SMALL[:, 212 + 16 * t + h:213 + 16 * t + h])
                    last.then_inc(xe_ready, 1)
                for t in range(T):
                    act.wait_ge(xt_ready, l * 2 + t + 1)
                    A(PXT[:, 0, :, t * P:(t + 1) * P], PS[:, 4 + 2 * t, :].rearrange("p (h n) -> p h n", h=4), ACT.Copy).then_inc(xt_a, 1)
                split()
                split()
                for h in range(4):
                    act.wait_ge(xo_ready, l * 4 + h + 1)
                    A(HTH[:, 2 * h:2 * h + 2, :], PS[:, h, :].rearrange("p (k n) -> p k n", k=2), ACT.Copy).then_inc(xo_h, 1)
                split()
                split()
                ring.n += 4
                squares(st2(l, 1), 1)
                split(K * NE)
                ht_copy(tr2(l, 3), HT)
                chunk()
                act.wait_ge(rt_in, l + 1)
                A(SMALL[:, 256:288], SMALL[:, 256:288], ACT.Exp).then_inc(rt_exp, 1)

                def expert(e, more=True):
                    for p in range(2):
                        silu(22 * L + l * 2 * NE + e * 2 + p, p)
                    for j in range(2):
                        chunk()
                        if more:
                            split()

                def seated_expert(e):
                    for p in range(2):
                        index = 22 * L + l * 2 * NE + e * 2 + p
                        chunk()
                        act.wait_ge(hidden_ready, index + 1)
                        A(SIL[:, p, :].rearrange("p (k n) -> p k n", k=2)[:, :, 0:P], PS[:, 2 * p, :].rearrange("p (k n) -> p k n", k=2)[:, :, 0:P],
                          ACT.Silu).then_inc(silu_ready, 1)
                        ring.next()
                        ahead.n += 4 * (1 - p)
                        split(back=6)
                    ring.n += 2

                wait_apart(act, crowd_known, l + 1, consts_loaded, 16 * NLOAD)
                crowded = act.value_load(CROWDED[0:1, 0:1], min_val=0, max_val=1)
                with act.If(crowded > 0):
                    split()
                    split()
                    with loop(act, NE // 2 - 1, (ring, 12), (ahead, 12), (splits, 12)) as i:
                        for j in range(2):
                            expert(i * 2 + j)
                    expert(NE - 2)
                    expert(NE - 1, False)
                    act.sem_inc(seat_a, NG_)
                with act.Else():
                    for c in (ring, ahead, splits):
                        c.n -= 6 * NE
                    with loop(act, NG_, (ring, 6 * EG), (ahead, 6 * EG), (splits, 2 * EG)) as g:
                        act.wait_ge(gather_ready, l * NG_ + g + 1)
                        A(XSEAT[:, 0:4, :], PS[:, 6, :].rearrange("p (k n) -> p k n", n=P), ACT.Copy).then_inc(seat_a, 1)
                        for j in range(EG):
                            seated_expert(g * EG + j)
                    act.wait_ge(wh_ready, splits.v + splits.n)
                    act.sem_inc(wh_ready, 4 * NE)
                    splits.n += 4 * NE
                squares(st2(l, 2), 1)
            act.wait_ge(src_ready, tr2(L, 0) + 1)
            act.dma_start(out_view, X).then_inc(out_stored, 16)
            act.wait_ge(out_stored, 16)

        @block.vector
        def _(dve):
            ring = Ring()
            steps = Steps(dve, dve_step)
            link = steps.link
            V = nc.vector
            TTn, TSc = V.tensor_tensor, V.tensor_scalar
            XF, TMPF, YF = flat(X), flat(TMP), flat(Y)
            LOW = PS[:, 0:4, :].rearrange("p b n -> p (b n)")
            HIGH = PS[:, 4:8, :].rearrange("p b n -> p (b n)")

            def chunk():
                ring.next()
                dve.wait_ge(chunks_done, ring.done())

            def ht_copy(n, dst, gains=None, tiles=K):
                for b in range(4):
                    dve.wait_ge(ht_h, n * 4 + b + 1)
                    if gains is None or 2 * b >= tiles:
                        TTn(dst[1][:, 2 * b:2 * b + 2, :], PS[:, b, :].rearrange("p (k n) -> p k n", k=2), dst[0][:, 2 * b:2 * b + 2, :].bitcast(F32),
                            ALU.subtract).then_inc(ht_l, 1)
                    else:
                        for k in (2 * b, 2 * b + 1):
                            last = V.scalar_tensor_tensor(dst[1][:, k, :], PS[:, b, (k % 2) * S:(k % 2 + 1) * S], LV[:, gains + k:gains + k + 1],
                                                          dst[0][:, k, :].bitcast(F32), ALU.mult, ALU.subtract)
                        last.then_inc(ht_l, 1)

            ahead, splits = Ring(), Count()

            def split(width=SLOT):
                slot = ahead.next()
                par = (ahead.n - 1) % 2
                splits.n += 1
                dve.wait_ge(wh_ready, splits.v + splits.n)
                TTn(RL[:, slot, 0:width], RINGS[:, slot, 0:width], RH[:, par, 0:width].bitcast(F32), ALU.subtract).then_inc(wl_ready, 1)

            def rms_rows(n):
                dve.wait_ge(rstd_ready, n + 1)
                TSc(TMP[:, 0, :], X[:, 0, :], SMALL[:, 4:5], None, ALU.mult)
                TSc(TMP[:, 1, :], X[:, 1, :], SMALL[:, 5:6], None, ALU.mult).then_inc(src_ready, 1)

            def hidden(index, par, dst, n=S, apart=False):
                ring.next()
                if not apart:
                    split()
                dve.wait_ge(silu_ready, index + 1)
                chunk()
                dve.wait_ge(hidden_ready, index + 1)
                hid = HIDDEN[:, par, :, 0:n]
                link(TTn(hid, SIL[:, par, :].rearrange("p (k n) -> p k n", k=2)[:, :, 0:n],
                         PS[:, 2 * par + 1, :].rearrange("p (k n) -> p k n", k=2)[:, :, 0:n], ALU.mult))
                link(V.tensor_copy(dst[0], hid))
                TTn(dst[1], hid, dst[0].bitcast(F32), ALU.subtract).then_inc(hidden_ready, 1)
                if not apart:
                    split()

            def swiglu(l, f, gains):
                rms_rows(st1(l, 2 * f))
                split()
                split()
                ht_copy(tr1(l, 4 * f), HT, gains)
                with loop(dve, 5, (ring, 4), (ahead, 4), (splits, 4), (steps, 4)) as i:
                    for j in range(2):
                        hidden(l * 22 + f * 11 + i * 2 + j, j, [x[:, bass.ds(i * 4 + 2 * j, 2), :] for x in GT])
                hidden(l * 22 + f * 11 + 10, 0, [x[:, 20:22, :] for x in GT])
                for j in range(FR - 2):
                    split()
                ring.n += FR - 1
                chunk()
                V.scalar_tensor_tensor(XF, HIGH, 0.5, XF, ALU.mult, ALU.add).then_inc(x_ready, 1)

            def project(width, j, par, more=True, to=PROJ):
                if more:
                    split(K * width)
                chunk()
                V.tensor_copy(to[:, 1, bass.ds(j * width, width)], PS[:, 2 * par + 1, 0:width]).then_inc(proj_d, 1)

            def four(x):
                return x.rearrange("p (a b) -> p b a", b=2)

            dve.sem_inc(hidden_ready, 2)
            dve.sem_inc(proj_d, 2)
            dve.sem_inc(ht_l, 4)
            dve.sem_inc(seat_d, 1)
            dve.wait_ge(consts_loaded, 16 * NLOAD)
            V.tensor_copy(RBP, RB.rearrange("p (g a b) -> p g b a", g=3, a=2)).then_inc(rb_ready, 1)
            dve.wait_ge(vec_ready, 1)
            V.tensor_copy(VECT, PS[:, 4, 0:L * VL]).then_inc(vec_taken, 1)
            dve.wait_ge(hot_ready, 1)
            V.tensor_copy(VBIAS, PS[0:12, 5, :]).then_inc(bias_row, 1)
            dve.wait_ge(hot_ready, 2)
            for t in range(T):
                for r in range(2):
                    TTn(BIASC[:, r * 8 + t * 4:r * 8 + t * 4 + 4, :],
                        PS[:, 6, t * NCMP * 8:(t + 1) * NCMP * 8].rearrange("p (n h r) -> p r h n", h=4, r=2)[:, r],
                        spread(CON[:, O_MCN + t * NCMP:O_MCN + (t + 1) * NCMP], 1, 4), ALU.add).then_inc(vec_taken, 1)
            dve.wait_ge(hot_ready, 3)
            TTn(BIAS[:, 0:8, :], LOW.rearrange("p (h n) -> p h n", h=8), spread(CON[:, O_MB:O_MB + S], 1, 8), ALU.add).then_inc(vec_taken, 1)
            TTn(BIAS[:, 8:12, :], HIGH[:, 0:4 * S].rearrange("p (h n) -> p h n", h=4), spread(CON[:, O_MS:O_MS + S], 1, 4), ALU.add).then_inc(vec_taken, 1)
            dve.wait_ge(x_loaded, 16)
            dve.sem_inc(x_ready, 1)
            dve.wait_ge(zeroed, 4)
            dve.wait_ge(vec_taken, 5)

            with loop(dve, L, (ring, C1), (ahead, C1), (splits, S1), (steps, DVE1)) as l:
                link(V.tensor_copy(LV[:, 0:VL], VECT[:, bass.ds(l * VL, VL)]))
                V.tensor_copy(SINKL, SINK[:, bass.ds(l, 1), :].rearrange("p o h -> p (o h)"))
                TSc(LV[:, VL:VL + 1], LV[:, V_QN:V_QN + 1], HD ** -0.5, None, ALU.mult)
                link(TSc(LV[:, VL + 1:VL + 2], LV[:, V_WQN:V_WQN + 1], HD ** -0.5, None, ALU.mult))
                dve.sem_inc(lv_ready, 1)
                swiglu(l, 0, V_F1)
                rms_rows(st1(l, 1))
                split(K * W1)
                split(K * W1)
                ht_copy(tr1(l, 1), HT, V_MIX)
                with loop(dve, N1 // 4 - 1, (ring, 4), (ahead, 4), (splits, 4)) as i:
                    for j in range(4):
                        project(W1, i * 4 + j, j % 2)
                for j in range(N1 - 4, N1):
                    project(W1, j, j % 2, j < N1 - 2)
                dve.wait_ge(head_sq, l + 1)
                link(V.tensor_reduce(SMALL[:, 8:44], QKN.rearrange("p t h d -> p (t h) d"), AX.X, ALU.add))
                TSc(SMALL[:, 48:84], SMALL[:, 8:44], 1.0 / HD, 1e-6, ALU.mult, ALU.add).then_inc(head_ms, 1)
                dve.wait_ge(head_rstd, l + 1)
                for t in range(T):
                    r = 96 + 18 * t
                    TTn(QKN[:, t, 0:8, :], PROJ[:, t, NQ:NQ + 512].rearrange("p (h d) -> p h d", d=HD), spread(SMALL[:, r:r + 8], 2, HD), ALU.mult)
                    TTn(QKN[:, t, 8:12, :], PROJ[:, t, WQ:WQ + 256].rearrange("p (h d) -> p h d", d=HD), spread(SMALL[:, r + 8:r + 12], 2, HD), ALU.mult)
                    for kind, c, at in ((0, KS, 14), (1, KW, 16), (2, WK, 12)):
                        for u in range(2):
                            last = TTn(KD[:, t, kind, :, u, :], PROJ[:, t, c:c + P].rearrange("p (h d) -> p h d", d=HD),
                                       spread(SMALL[:, r + at:r + at + 2], 2, HD), ALU.mult)
                last.then_inc(heads_ready, 1)
                for b in (1, 3, 5, 7, 9):
                    dve.wait_ge(htr_ready, l * 10 + b + 1)
                    src = PS[:, b % 4, :].rearrange("p (k n) -> p k n", k=2)
                    scale = {1: LV[:, VL:VL + 1], 3: LV[:, V_KN:V_KN + 1], 5: LV[:, V_WKN:V_WKN + 1]}.get(b)
                    if scale is None:
                        V.tensor_copy(TT[:, 2 * b:2 * b + 2, :], src).then_inc(tt_d, 1)
                    else:
                        TSc(TT[:, 2 * b:2 * b + 2, :], src, scale, None, ALU.mult).then_inc(tt_d, 1)
                dve.wait_ge(tt_a, l * 5 + 5)
                dve.wait_ge(tt_d, l * 5 + 5)
                V.memset(BTF.rearrange("p (m g n) -> p m g n", g=2, n=32)[:, :, :, NCMP:32], 0.0)
                for kv in range(2):
                    for g in range(2):
                        for par in range(2):
                            q = slice(64 * par, 64 * par + 64)
                            tok = TT[q, 12 + 2 * kv + g, :].rearrange("p (m s) -> p s m", s=16)[:, par::2, :]
                            for half in range(2):
                                last = TTn(BT[q, kv, 8 * half:8 * half + 8, 32 * g:32 * g + NCMP], tok[:, :, half:half + NCMP],
                                           spread(LV[q, V_POS + 8 * half:V_POS + 8 * half + 8], 2, NCMP), ALU.add)
                last.then_inc(blocks_ready, 1)
                ahead.n += 6
                ring.n += 4
                chunk()
                link(V.tensor_copy(KCN[:, 0, :], PS[0:64, 7, 0:HD]))
                link(TTn(KCN[:, 1, :], KCN[:, 0, :], KCN[:, 0, :], ALU.mult))
                link(V.tensor_reduce(SMALL[0:64, 139:140], KCN[:, 1, :], AX.X, ALU.add))
                TSc(SMALL[0:64, 140:141], SMALL[0:64, 139:140], 1.0 / HD, 1e-6, ALU.mult, ALU.add).then_inc(cmp_ms, 1)
                chunk()
                for i in range(4):
                    V.tensor_copy(VCB[32 * i:32 * i + 32, i, :], PS[32 * i:32 * i + 32, 5, 0:HD])
                dve.wait_ge(cmp_rstd, l + 1)
                link(TSc(KCN[:, 1, :], KCN[:, 0, :], SMALL[0:64, 141:142], None, ALU.mult))
                V.tensor_copy(KCN[:, 0, :], KCN[:, 1, :]).then_inc(cmp_keys, 1)
                dve.wait_ge(scc_ready, l + 1)
                for r in range(2):
                    last = TTn(PC[:, 8 * r:8 * r + 8, 0:NCMP], PS[:, 4 + 3 * r, 0:256].rearrange("p (h n) -> p h n", n=32)[:, :, 0:NCMP],
                               BIASC[:, 8 * r:8 * r + 8, :], ALU.add)
                link(last)
                link(V.tensor_reduce(SMALL[:, 288:304], PC[:, :, 0:NCMP], AX.X, ALU.max))
                TTn(PC[:, :, 0:NCMP], PC[:, :, 0:NCMP], spread(SMALL[:, 288:304], 2, NCMP), ALU.subtract).then_inc(pc_in, 1)
                dve.wait_ge(pc_exp, l + 1)
                link(V.tensor_reduce(SMALL[:, 304:320], PC[:, :, 0:NCMP], AX.X, ALU.add))
                for r in range(2):
                    for t in range(T):
                        s8 = PC[:, 8 * r + 4 * t:8 * r + 4 * t + 4, 0:NCMP]
                        last = TTn(s8, s8, spread(CON[:, O_MC + t * NCMP:O_MC + (t + 1) * NCMP], 1, 4), ALU.mult)
                last.then_inc(pc_ready, 1)
                link(V.reciprocal(SMALL[:, 320:336], SMALL[:, 304:320]))
                dve.wait_ge(gates_ready, l + 1)
                for t in range(T):
                    last = TTn(SMALL[:, 336:352].rearrange("p (r t h) -> p t r h", r=2, t=2)[:, t],
                               SMALL[:, 320:336].rearrange("p (r t h) -> p t r h", r=2, t=2)[:, t],
                               PROJ[:, t, NG:NG + 8].rearrange("p (h r) -> p r h", r=2), ALU.mult)
                link(last)

                def softmax(u):
                    kind, g, t = UNITS[u]
                    nk = (t + 1) * P
                    c = 16 * (u % 2)
                    n = l * NU + u
                    dve.wait_ge(sc_ready, n + 1)
                    if u >= 2:
                        dve.wait_ge(pt_ready, n - 1)
                    h0 = 4 * g if kind < 2 else 8
                    for r in range(2):
                        last = TTn(PR[:, u % 2, 2 * r:2 * r + 2, 0:nk], PS[:, 2 * (u % 2) + r, :].rearrange("p (h n) -> p h n", h=2)[:, :, 0:nk],
                                   BIAS[:, h0 + 2 * r:h0 + 2 * r + 2, S - nk:S], ALU.add)
                    last.then_inc(sc_taken, 1)
                    dve.wait_ge(sc_taken, n + 1)
                    link(V.tensor_reduce(SMALL[:, 220 + c:224 + c], PR[:, u % 2, :, 0:nk], AX.X, ALU.max))
                    if kind == 2:
                        sink = four(SINKL)
                        mx = SMALL[:, 220 + c:224 + c].rearrange("p (b a) -> p b a", b=2)
                        link(TTn(mx, mx, sink, ALU.max))
                        link(TTn(SMALL[:, 216 + c:220 + c].rearrange("p (b a) -> p b a", b=2), sink, mx, ALU.subtract))
                    TSc(SMALL[:, 208 + c:212 + c], SMALL[:, 220 + c:224 + c], -1.0, None, ALU.mult).then_inc(sc_max, 1)

                def weights(u):
                    kind, g, t = UNITS[u]
                    c = 16 * (u % 2)
                    dve.wait_ge(exp_ready, l * NU + u + 1)
                    den = SMALL[:, 212 + c:216 + c]
                    if kind == 2:
                        link(TTn(den, den, SMALL[:, 216 + c:220 + c], ALU.add))
                    link(V.reciprocal(COEF[:, u % 2, :], den))
                    if kind < 2:
                        gate = four(PROJ[:, t, NG + 8 * (kind + 1) + 4 * g:NG + 8 * (kind + 1) + 4 * g + 4])
                        co = COEF[:, u % 2, :].rearrange("p (b a) -> p b a", b=2)
                        link(TTn(co, co, gate, ALU.mult))
                    if t:
                        dve.wait_ge(pt_ready, l * NU + u + 1)
                        V.tensor_copy(PT[:, u % 2, 1, :], PS[:, 5, :]).then_inc(pt_d, 1)

                def outputs(u):
                    kind, g, t = UNITS[u]
                    dve.wait_ge(o_ready, l * NU + u + 1)
                    src = PS[:, 6 + u % 2, 0:256].rearrange("p (a b d) -> p b a d", a=2, b=2)
                    co = spread(COEF[:, u % 2, :].rearrange("p (b a) -> p b a", b=2), 3, HD)
                    if kind == 2:
                        TTn(Y[:, t, 768:1024].rearrange("p (a b d) -> p b a d", a=2, b=2), src, co, ALU.mult).then_inc(o_taken, 1)
                    else:
                        dve.wait_ge(o_taken, l * (NU + 1) + u + 1)
                        link(TTn(YD.rearrange("p (a b d) -> p b a d", a=2, b=2), src, co, ALU.mult))
                        y = Y[:, t, g * 256:(g + 1) * 256]
                        TTn(y, y, YD, ALU.add).then_inc(o_taken, 1)

                softmax(0)
                dve.wait_ge(oc_ready, l + 1)
                for t in range(T):
                    last = TTn(Y[:, t, 0:512].rearrange("p (h r d) -> p r h d", h=4, r=2), PS[:, 6 + t, :].rearrange("p (r h d) -> p r h d", r=2, h=4),
                               spread(SMALL[:, 336:352].rearrange("p (r t h) -> p t r h", r=2, t=2)[:, t], 3, HD), ALU.mult)
                last.then_inc(o_taken, 1)
                for u in range(NU):
                    if u + 1 < NU:
                        softmax(u + 1)
                    weights(u)
                    if u:
                        outputs(u - 1)
                outputs(NU - 1)
                dve.wait_ge(z_copied, l + 1)
                V.scalar_tensor_tensor(flat(EX), flat(ZS), -1.0, flat(ZS), ALU.mult, ALU.min).then_inc(z_abs, 1)
                dve.wait_ge(z_ln, l + 1)
                link(V.scalar_tensor_tensor(flat(EX), flat(ZS), 0.0, flat(EX), ALU.max, ALU.add))
                TTn(EX, EX, spread(CON[:, O_SB:O_SB + 384], 1, 4), ALU.mult).then_inc(sp_ready, 1)
                dve.wait_ge(after_ready, l + 1)
                link(TTn(ZS, ZS, PS[:, 4:8, 0:384], ALU.subtract))
                TTn(ZS, ZS, spread(CON[:, O_SBN:O_SBN + 384], 1, 4), ALU.add).then_inc(w_arg, 1)
                dve.wait_ge(osb_ready, l + 1)
                V.tensor_copy(Y[:, :, 512:768], PS[:, 0, :].rearrange("p (t n) -> p t n", t=2)).then_inc(src_ready, 1)
                split()
                split()
                ht_copy(tr1(l, 2), HT)
                split()
                ring.n += 1
                chunk()
                bg = [PROJ[:, :, BG + i * D:BG + (i + 1) * D] for i in range(3)]
                low, high = (x.rearrange("p (t n) -> p t n", t=2) for x in (LOW, HIGH))
                TTn(TMP, low, bg[0], ALU.mult).then_inc(rows_taken, 1)
                split()
                chunk()
                split()
                link(TTn(Y, high, bg[1], ALU.mult))
                link(TTn(TMPF, TMPF, YF, ALU.add))
                chunk()
                link(TTn(Y, low, bg[2], ALU.mult))
                TTn(YF, TMPF, YF, ALU.add).then_inc(src_ready, 1)
                split()
                ht_copy(tr1(l, 3), HT)
                for j in range(2):
                    split()
                ring.n += 3
                chunk()
                TTn(XF, HIGH, XF, ALU.add).then_inc(x_ready, 1)
                swiglu(l, 1, V_F2)

            dve.wait_ge(x_ready, 3 * L + 1)
            dve.sem_inc(src_ready, 2)
            ht_copy(5 * L, MEMT)

            def layer_norm(l, k):
                link(V.tensor_reduce(SMALL[:, 352:354], X, AX.X, ALU.add))
                link(TSc(SMALL[:, 354:356], SMALL[:, 352:354], -1.0 / D, None, ALU.mult))
                TSc(X[:, 0, :], X[:, 0, :], SMALL[:, 354:355], None, ALU.add)
                TSc(X[:, 1, :], X[:, 1, :], SMALL[:, 355:356], None, ALU.add).then_inc(x_ready, 1)
                dve.wait_ge(lngb_in, (l * 3 + k) * 32 + 32)
                dve.wait_ge(rstd_ready, st2(l, k) + 1)
                for t in range(T):
                    last = V.scalar_tensor_tensor(X[:, t, :], X[:, t, :], SMALL[:, 4 + t:5 + t], LNGB[:, 0, :], ALU.mult, ALU.mult)
                link(last)
                TTn(X, X, spread(LNGB[:, 1, :], 1, T), ALU.add).then_inc(src_ready, 1)

            with loop(dve, L, (ring, C2), (ahead, C2), (splits, S2), (steps, DVE2)) as l:
                link(V.tensor_copy(LV[:, 0:VL], VECT[:, bass.ds(l * VL, VL)]))
                V.memset(WST, 0.0)
                link(V.memset(STATE[:, 0, :, :], 0.0))
                dve.sem_inc(lv_ready, 1)
                split(K * W2)
                split(K * W2)
                ht_copy(tr2(l, 0), HT)
                with loop(dve, N2 // 4, (ring, 4), (ahead, 4), (splits, 4)) as i:
                    for j in range(4):
                        project(W2, i * 4 + j, j % 2, True, PROJ2)
                for j in range(N2 // 4 * 4, N2):
                    project(W2, j, j % 2, False, PROJ2)
                ring.next()
                ahead.next()
                v = PROJ2[:, :, SV2:SV2 + 512].rearrange("p t (g c) -> p t g c", g=4)
                dve.wait_ge(gelu_ready, 2 * l + 1)
                link(V.tensor_reduce(SMALL[:, 356:364].rearrange("p (t g) -> p t g", t=2), v, AX.X, ALU.add))
                link(TSc(SMALL[:, 364:372], SMALL[:, 356:364], -1.0 / P, None, ALU.mult))
                for t in range(T):
                    last = TTn(v[:, t], v[:, t], spread(SMALL[:, 364 + 4 * t:368 + 4 * t], 2, P), ALU.add)
                last.then_inc(sv_centred, 1)
                dve.wait_ge(gl_ready, l + 1)
                x = PS[:, 4, :].rearrange("p (t n) -> p t n", t=2)
                link(TSc(GX[:, 2:4, 0:S], x, -1.0, 0.0, ALU.mult, ALU.max))
                V.scalar_tensor_tensor(GX[:, 0:2, 0:S], GX[:, 2:4, 0:S], -2.0, x, ALU.mult, ALU.subtract).then_inc(gl_abs, 1)
                dve.wait_ge(gl_ln, l + 1)
                TTn(GX[:, 0:2, 0:S], GX[:, 0:2, 0:S], GX[:, 2:4, 0:S], ALU.add).then_inc(gl_sp, 1)
                dve.wait_ge(gl_exp, l + 1)
                TTn(KDEC, PROJ2[:, :, GK:GK + 256], KEXP, ALU.mult).then_inc(kdec_ready, 1)
                for c in range(4):
                    dve.wait_ge(kv_ready, l * 4 + c + 1)
                    if c:
                        dve.wait_ge(state_ready, l * 4 + c)
                    for hp in range(2):
                        last = V.scalar_tensor_tensor(STATE[:, c + 1, hp, :], STATE[:, c, hp, :], SMALL[:, 200 + hp * 4 + c:201 + hp * 4 + c],
                                                      PS[:, c % 2, hp * P:(hp + 1) * P], ALU.mult, ALU.add)
                    last.then_inc(state_ready, 1)
                dve.wait_ge(sv_sq, l + 1)
                V.tensor_reduce(SMALL[:, 152:160].rearrange("p (t g) -> p t g", t=2), TMP[:, :, 512:1024].rearrange("p t (g c) -> p t g c", g=4), AX.X, ALU.add)
                dve.wait_ge(go_sq, l + 1)
                link(V.tensor_reduce(SMALL[:, 144:152].rearrange("p (t g) -> p t g", t=2), TMP[:, :, 0:512].rearrange("p t (g c) -> p t g c", g=4), AX.X, ALU.add))
                TSc(SMALL[:, 160:168], SMALL[:, 144:152], 1.0 / P, 1e-6, ALU.mult, ALU.add)
                TSc(SMALL[:, 168:176], SMALL[:, 152:160], 1.0 / P, 1e-5, ALU.mult, ALU.add).then_inc(gs_ms, 1)
                dve.wait_ge(gs_rstd, l + 1)
                for t in range(T):
                    last = TTn(Y[:, t, 0:512].rearrange("p (h r c) -> p r h c", h=2, r=2),
                               PS[:, 2:6, 0:256].rearrange("p (r t) (h c) -> p t r h c", r=2, h=2)[:, t],
                               spread(SMALL[:, 176 + 4 * t:180 + 4 * t].rearrange("p (r h) -> p r h", r=2), 3, P), ALU.mult)
                link(last)
                dve.wait_ge(gelu_ready, 2 * l + 2)
                TTn(Y[:, :, 0:512], Y[:, :, 0:512], PROJ2[:, :, GR:GR + 512], ALU.mult)
                for t in range(T):
                    last = TTn(v[:, t], v[:, t], spread(SMALL[:, 184 + 4 * t:188 + 4 * t], 2, P), ALU.mult)
                link(last)
                dve.wait_ge(layer_in, l * 64 + 64)
                vv = PROJ2[:, :, SV2:SV2 + 512]
                link(TTn(vv, vv, spread(SGB[:, 0, :], 1, T), ALU.mult))
                TTn(vv, vv, spread(SGB[:, 1, :], 1, T), ALU.add).then_inc(vn_ready, 1)
                dve.wait_ge(mix_ready, l + 1)
                for t in range(T):
                    for g in range(4):
                        last = V.scalar_tensor_tensor(Y[:, t, 512 + g * P:512 + (g + 1) * P], PS[:, 4 + t, g * P:(g + 1) * P], LV[:, V_BS + g:V_BS + g + 1],
                                                      PROJ2[:, t, SU + g * P:SU + (g + 1) * P], ALU.add, ALU.mult)
                last.then_inc(src_ready, 1)
                split()
                split()
                ht_copy(tr2(l, 1), HT, V_GN, 4)
                split()
                split()
                ring.n += 3
                chunk()
                link(V.scalar_tensor_tensor(XF, XF, ALPHA, HIGH, ALU.mult, ALU.add))
                layer_norm(l, 0)
                split()
                split()
                ht_copy(tr2(l, 2), HT)
                for j in range(8):
                    split()
                    if j % 2 == 0:
                        ring.next()
                        continue
                    chunk()
                    V.tensor_copy(TT[:, 2 * j:2 * j + 2, :], PS[:, 1, :].rearrange("p (k n) -> p k n", k=2)).then_inc(qk_d, 1)
                for j in range(4):
                    if j < 2:
                        split()
                    chunk()
                    V.tensor_copy(VX[:, 1, j * 256:(j + 1) * 256], PS[:, 3 + 2 * (j % 2), 0:256]).then_inc(vx_d, 1)
                for t in range(T):
                    c = 16 * t
                    dve.wait_ge(xs_ready, l * 2 + t + 1)
                    link(V.tensor_reduce(SMALL[:, 220 + c:224 + c], PS[:, 2 * t:2 * t + 2, :].rearrange("p b n -> p (b n)").rearrange("p (h n) -> p h n", h=4), AX.X, ALU.max))
                    TSc(SMALL[:, 208 + c:212 + c], SMALL[:, 220 + c:224 + c], -1.0 / 16, None, ALU.mult).then_inc(xm_ready, 1)
                for t in range(T):
                    c = 16 * t
                    dve.wait_ge(xe_ready, l * 2 + t + 1)
                    link(V.reciprocal(COEF[:, t, :], SMALL[:, 212 + c:216 + c]))
                    for h in range(4):
                        last = TSc(PR[:, t, h, :], PR[:, t, h, :], COEF[:, t, h:h + 1], None, ALU.mult)
                    last.then_inc(xp_ready, 1)
                for t in range(T):
                    dve.wait_ge(xt_ready, l * 2 + t + 1)
                    V.tensor_copy(PXT[:, 1, :, t * P:(t + 1) * P], PS[:, 5 + 2 * t, :].rearrange("p (h n) -> p h n", h=4)).then_inc(xt_d, 1)
                split()
                split()
                for h in range(4):
                    dve.wait_ge(xo_h, l * 4 + h + 1)
                    TTn(HTL[:, 2 * h:2 * h + 2, :], PS[:, h, :].rearrange("p (k n) -> p k n", k=2), HTH[:, 2 * h:2 * h + 2, :].bitcast(F32),
                        ALU.subtract).then_inc(xo_l, 1)
                split()
                split()
                ring.n += 3
                chunk()
                link(V.scalar_tensor_tensor(XF, XF, ALPHA, HIGH, ALU.mult, ALU.add))
                layer_norm(l, 1)
                split(K * NE)
                ht_copy(tr2(l, 3), HT)
                chunk()
                R = SMALL[:, 256:288]
                r3 = R.rearrange("p (t n) -> p t n", t=2)
                TTn(r3, PS[:, 4, 0:32].rearrange("p (t n) -> p t n", t=2), spread(BR, 1, T), ALU.add).then_inc(moe_taken, 1)
                dve.wait_ge(moe_taken, l * (NE + 1) + 1)
                link(V.tensor_reduce(SMALL[:, 372:374], r3, AX.X, ALU.max))
                TTn(r3, r3, spread(SMALL[:, 372:374], 2, NE), ALU.subtract).then_inc(rt_in, 1)
                V.memset(RTN, 0.0)
                dve.wait_ge(rt_exp, l + 1)
                link(V.tensor_reduce(SMALL[:, 374:376], r3, AX.X, ALU.add))
                link(V.reciprocal(SMALL[:, 376:378], SMALL[:, 374:376]))
                link(TTn(r3, r3, spread(SMALL[:, 376:378], 2, NE), ALU.mult))
                r4 = R.rearrange("p (g i) -> p g i", i=4)
                cmp = RTC.rearrange("p (g i j) -> p g i j", i=4, j=4)
                for j in range(4):
                    other = bass.AP(tensor=r4.tensor, offset=r4[:, :, j:j + 1].offset, ap=[*r4[:, :, j:j + 1].ap[:2], [0, j + 1]])
                    last = TTn(cmp[:, :, 0:j + 1, j], other, r4[:, :, 0:j + 1], ALU.is_gt)
                    if j < 3:
                        other = bass.AP(tensor=r4.tensor, offset=other.offset, ap=[*r4[:, :, j:j + 1].ap[:2], [0, 3 - j]])
                        last = TTn(cmp[:, :, j + 1:4, j], other, r4[:, :, j + 1:4], ALU.is_ge)
                link(last)
                link(V.tensor_reduce(SMALL[:, 384:416], RTC.rearrange("p (n j) -> p n j", j=4), AX.X, ALU.add))
                link(V.scalar_tensor_tensor(SMALL[:, 416:448], SMALL[:, 384:416], 1.5, R, ALU.is_lt, ALU.mult))
                link(V.tensor_reduce(SMALL[:, 448:456], SMALL[:, 416:448].rearrange("p (g i) -> p g i", i=4), AX.X, ALU.add))
                gs = SMALL[:, 448:456].rearrange("p (t g) -> p t g", t=2)
                link(V.tensor_reduce(SMALL[:, 456:458], gs, AX.X, ALU.max))
                eq = SMALL[:, 460:468].rearrange("p (t g) -> p t g", t=2)
                link(TTn(eq, gs, spread(SMALL[:, 456:458], 2, 4), ALU.is_equal))
                before = RTN.rearrange("p (t g) -> p t g", t=2)
                for g in range(1, 4):
                    link(TTn(before[:, :, g], before[:, :, g - 1], eq[:, :, g - 1], ALU.add))
                link(V.scalar_tensor_tensor(SMALL[:, 468:476], RTN, 0.5, SMALL[:, 460:468], ALU.is_lt, ALU.mult))
                V.tensor_copy(OH.rearrange("p t g -> p (t g)"), SMALL[:, 468:476]).then_inc(oh_ready, 1)
                link(V.reciprocal(SMALL[:, 458:460], SMALL[:, 456:458]))
                link(TTn(SMALL[:, 468:476].rearrange("p (t g) -> p t g", t=2), SMALL[:, 468:476].rearrange("p (t g) -> p t g", t=2),
                         spread(SMALL[:, 458:460], 2, 4), ALU.mult))
                for t in range(T):
                    TTn(GATE[:, :, t].rearrange("p (g i) -> p g i", i=4), SMALL[:, 416 + 16 * t:432 + 16 * t].rearrange("p (g i) -> p g i", i=4),
                        spread(SMALL[:, 468 + 4 * t:472 + 4 * t], 2, 4), ALU.mult)
                dve.wait_ge(pos_ready, l + 1)
                link(V.tensor_copy(SMALL[:, 484:496], PS[:, 4, 32:44]))
                link(V.tensor_reduce(SMALL[:, 496:497], SMALL[:, 492:496], AX.X, ALU.max))
                TSc(CROWDED, SMALL[:, 496:497], P + 0.5, None, ALU.is_gt).then_inc(crowd_known, 1)
                wait_apart(dve, crowd_known, l + 1, consts_loaded, 16 * NLOAD)
                crowded = dve.value_load(CROWDED[0:1, 0:1], min_val=0, max_val=1)
                apart = steps.n

                def take_rows(e, gate, rows):
                    ring.next()
                    chunk()
                    for t, row in enumerate(rows):
                        last = V.scalar_tensor_tensor(row, PS[:, 4 + 2 * t:6 + 2 * t, :].rearrange("p b n -> p (b n)"), gate[:, t:t + 1],
                                                      row, ALU.mult, ALU.add)
                    last.then_inc(moe_taken, 1)
                    dve.wait_ge(moe_taken, l * (NE + 1) + e + 2)

                def expert(e, gate, more):
                    for p in range(2):
                        hidden(22 * L + l * 2 * NE + e * 2 + p, p, [x[:, 2 * p:2 * p + 2, :] for x in EH])
                    if more:
                        split()
                        split()
                    take_rows(e, gate, (TMP[:, 0, :], TMP[:, 1, :]))

                def seated_expert(e, gate, row):
                    for p in range(2):
                        hidden(22 * L + l * 2 * NE + e * 2 + p, p, [x[:, 2 * p:2 * p + 2, 0:P] for x in EH], P, True)
                        ahead.n += 4 * (1 - p)
                        split()
                    take_rows(e, gate, (row,))

                with dve.If(crowded > 0):
                    V.memset(TMP, 0.0).then_inc(dve_step, 1)
                    steps.n += 1
                    wait_apart(dve, dve_step, steps.v + steps.n, consts_loaded, 16 * NLOAD)

                    split()
                    split()

                    def two(i, more=True):
                        link(V.tensor_copy(GCUR, GATE[:, bass.ds(i * 2, 2), :].rearrange("p e t -> p (e t)")))
                        for j in range(2):
                            expert(i * 2 + j, GCUR[:, 2 * j:2 * j + 2], more or j == 0)

                    with loop(dve, NE // 2 - 1, (ring, 12), (ahead, 12), (splits, 12), (steps, 9)) as i:
                        two(i)
                    two(NE // 2 - 1, False)
                    V.scalar_tensor_tensor(XF, XF, ALPHA, TMPF, ALU.mult, ALU.add).then_inc(moe_summed, 1)
                    dve.sem_inc(seat_ready, 1)
                    dve.sem_inc(seat_taken, 1)
                    dve.sem_inc(seat_d, NG_)
                with dve.Else():
                    dense, steps.n = steps.n - apart, apart
                    for c in (ring, ahead, splits):
                        c.n -= 6 * NE
                    for g in range(NG_):
                        for t in range(T):
                            last = TSc(SEAT[:, g, t, :], CON[:, O_NTH:O_NTH + P], SMALL[:, 484 + t * NG_ + g:485 + t * NG_ + g],
                                       OH[:, t, g:g + 1], ALU.is_equal, ALU.mult)
                    last.then_inc(seat_ready, 1)
                    link(V.memset(YSEAT, 0.0))
                    dve.wait_ge(seat_tr, l + 1)
                    V.tensor_copy(GSEAT, PS[:, 5, 0:NE])
                    V.tensor_copy(flat(TMP)[:, 0:1024], PS[:, 6:8, :].rearrange("p b n -> p (b n)")).then_inc(seat_taken, 1)
                    wait_apart(dve, seat_taken, l + 1, consts_loaded, 16 * NLOAD)

                    with loop(dve, NG_, (ring, 6 * EG), (ahead, 6 * EG), (splits, 2 * EG), (steps, 1 + 4 * EG)) as g:
                        dve.wait_ge(gather_ready, l * NG_ + g + 1)
                        V.tensor_copy(XSEAT[:, 4:8, :], PS[:, 7, :].rearrange("p (k n) -> p k n", n=P)).then_inc(seat_d, 1)
                        link(V.tensor_copy(GCUR, GSEAT[:, bass.ds(g * EG, EG)]))
                        for j in range(EG):
                            seated_expert(g * EG + j, GCUR[:, j:j + 1], YSEAT[:, bass.ds(g * D, D)])
                    dve.wait_ge(scatter_ready, l + 1)
                    V.scalar_tensor_tensor(XF, XF, ALPHA, HIGH, ALU.mult, ALU.add).then_inc(moe_summed, 1)
                    dve.wait_ge(wl_ready, splits.v + splits.n)
                    dve.sem_inc(wl_ready, 4 * NE)
                    splits.n += 4 * NE
                    sparse = steps.n - apart
                    assert dense >= sparse, (dense, sparse)
                    if dense > sparse:
                        dve.sem_inc(dve_step, dense - sparse)
                    steps.n += dense - sparse
                dve.wait_ge(moe_summed, l + 1)
                layer_norm(l, 2)


def t5_bucket(dist):
    d = np.maximum(dist, 0)
    df = np.maximum(d, 1).astype(np.float32)
    large = 16 + (np.log(df / np.float32(16)) / np.float32(math.log(8)) * np.float32(16)).astype(np.int32)
    return np.where(d < 16, d, np.minimum(large, 31))


def constants():
    con = np.zeros((P, CONW), np.float32)
    i = np.arange(P)[:, None]
    neg = np.float32(-1e30)
    con[:, O_ID:O_ID + P] = np.eye(P)
    j = np.arange(S)[None, :]
    dist = P + i - j
    con[:, O_MB:O_MB + S] = np.where(dist >= 0, 0, neg)
    con[:, O_MS:O_MS + S] = np.where((dist >= 0) & (dist < P), 0, neg)
    for t in range(T):
        ok = t * P + i - (16 * np.arange(NCMP)[None, :] + 31) >= 0
        con[:, O_MC + t * NCMP:O_MC + (t + 1) * NCMP] = ok
        con[:, O_MCN + t * NCMP:O_MCN + (t + 1) * NCMP] = np.where(ok, 0, neg)
    q = np.concatenate([np.arange(S), np.arange(P)])[None, :]
    con[:, O_SB:O_SB + 384] = i < q
    con[:, O_SBN:O_SBN + 384] = np.where(i < q, 0, neg)
    c = np.arange(P)[None, :]
    con[:, O_U:O_U + P] = i >= c
    con[:, O_ONE:O_ONE + P] = 1
    con[:, O_REV:O_REV + P] = (i > c) & (i // 64 == c // 64)
    con[:, O_CHO:O_CHO + 2] = i // 64 == np.arange(2)[None, :]
    con[:, O_FLIP:O_FLIP + P] = np.eye(P)[::-1]
    con[:, O_NTH:O_NTH + P] = 1 + np.arange(P)
    b = np.arange(32)[:, None]
    w = np.arange(512)[None, :]
    hot_rev = (t5_bucket(383 - w) == b).astype(np.float32)
    hot = (t5_bucket(w - 256) == b).astype(np.float32)
    return con, hot_rev, hot


def kernel(**inputs):
    import concourse.bacc as bacc
    from concourse.bass_utils import run_bass_kernel_spmd as run

    nc = bacc.Bacc("TRN2", target_bir_lowering=False, num_devices=1)
    arrays = {n: np.ascontiguousarray(x) for n, x in inputs.items()}
    for n, x in zip(("con", "hot_rev", "hot"), constants()):
        arrays[n] = x
    aps = {n: nc.dram_tensor(n, x.shape, F32, kind="ExternalInput").ap() for n, x in arrays.items()}
    out = nc.dram_tensor("out", (1, S, D), F32, kind="ExternalOutput").ap()
    scratch = nc.dram_tensor("bias_scratch", (12, 512), F32, kind="Internal").ap()
    build(nc, aps, out, aps["con"], aps["hot_rev"], aps["hot"], scratch)
    r = run(nc, [arrays], core_ids=[0])
    return r.results[0]["out"]
```
